# Optimizing a Trainium2 kernel written in Bass

```python
import math
import jax, jax.numpy as jnp
from jax import lax
import numpy as np

D_MODEL = 2048
BATCH = 1
SEQ = 512
DEPTH = 1
DEC_BATCH = 8
DEC_SEQ = 1
PAST_LEN = 1024
PAGE_SIZE = 128

MIX_WIDTH = D_MODEL
HEAD_DIM = 128
SB_HEADS = (MIX_WIDTH // 2) // HEAD_DIM
CM_DIM = 128
CM_HEADS = (MIX_WIDTH - SB_HEADS * HEAD_DIM) // CM_DIM
SB_W = SB_HEADS * HEAD_DIM
CM_W = CM_HEADS * CM_DIM
IN_W = 3 * SB_W + 2 * CM_W
CHUNK = 128
Q_BLOCK = 128
D_FF = ((8 * D_MODEL // 3 + 255) // 256) * 256
PLE_DIM = 256
EPS = 1e-6
SB_SCALE = 1.0 / math.sqrt(HEAD_DIM)
SB_BIAS_MIN = 2.0
SB_BIAS_MAX = 8.0

kernel_name = "hymba_stickbreak_chunkmlp_decode_step"

def rmsnorm(x, g):
    xf = x.astype(jnp.float32)
    y = xf * lax.rsqrt(jnp.mean(xf * xf, axis=-1, keepdims=True) + EPS)
    return (y * g.astype(jnp.float32)).astype(x.dtype)

def layernorm(x, g, b):
    xf = x.astype(jnp.float32)
    mu = jnp.mean(xf, axis=-1, keepdims=True)
    xc = xf - mu
    y = xc * lax.rsqrt(jnp.mean(xc * xc, axis=-1, keepdims=True) + EPS)
    return (y * g.astype(jnp.float32) + b.astype(jnp.float32)).astype(x.dtype)

def mixer_inputs(h, g_mix, w_in, g_q, g_k, sgu_ln_g, sgu_ln_b):
    B, L, _ = h.shape
    z = rmsnorm(h, g_mix) @ w_in
    q, k, v, u, vc = jnp.split(z, [SB_W, 2 * SB_W, 3 * SB_W, 3 * SB_W + CM_W], axis=-1)
    q = rmsnorm(q.reshape(B, L, SB_HEADS, HEAD_DIM), g_q)
    k = rmsnorm(k.reshape(B, L, SB_HEADS, HEAD_DIM), g_k)
    v = v.reshape(B, L, SB_HEADS, HEAD_DIM)
    u = jax.nn.gelu(u, approximate=False).reshape(B, L, CM_HEADS, CM_DIM)
    vc = jax.nn.gelu(vc, approximate=False).reshape(B, L, CM_HEADS, CM_DIM)
    vc = layernorm(vc, sgu_ln_g, sgu_ln_b)
    return q, k, v, u, vc

def stick_breaking(q, k, v, sb_bias, q_pos, k_pos):
    z = jnp.einsum('bqhd,bkhd->bhqk', q.astype(jnp.float32), k.astype(jnp.float32)) * SB_SCALE
    z = z + sb_bias.astype(jnp.float32)[None, :, None, None]
    causal = k_pos[None, :] < q_pos[:, None]
    log_keep = jnp.where(causal, jax.nn.log_sigmoid(-z), 0.0)
    after = lax.cumsum(log_keep, axis=3, reverse=True) - log_keep
    a = jnp.where(causal, jnp.exp(jax.nn.log_sigmoid(z) + after), 0.0)
    return jnp.einsum('bhqk,bkhd->bqhd', a, v.astype(jnp.float32)).astype(v.dtype)

def stick_breaking_prompt(q, k, v, sb_bias):
    B, L, H, D = q.shape
    nb = L // Q_BLOCK
    qb = q.reshape(B, nb, Q_BLOCK, H, D).transpose(1, 0, 2, 3, 4)
    pos = jnp.arange(L, dtype=jnp.int32)
    qpos_b = pos.reshape(nb, Q_BLOCK)
    out = lax.map(lambda args: stick_breaking(args[0], k, v, sb_bias, args[1], pos), (qb, qpos_b))
    return out.transpose(1, 0, 2, 3, 4).reshape(B, L, H, D)

def chunk_mlp(u, vn, w_s, b_s):
    B, L, H, D = vn.shape
    pad = (-L) % CHUNK
    vp = jnp.pad(vn, ((0, 0), (0, pad), (0, 0), (0, 0)))
    nc = (L + pad) // CHUNK
    vch = vp.reshape(B, nc, CHUNK, H, D)
    mask = jnp.tril(jnp.ones((CHUNK, CHUNK), dtype=bool))
    wm = jnp.where(mask[None], w_s, 0.0)
    mixed = jnp.einsum('hts,bcshd->bcthd', wm, vch) + b_s.T[:, :, None]
    mixed = mixed.reshape(B, nc * CHUNK, H, D)[:, :L]
    return (u * mixed).astype(u.dtype)

def layer_out(h, o_sb, o_cm, p, g_out_sb, g_out_cm, w_out, g_ffn, w_gate, w_up, w_down,
              g_ple, w_ple_gate, w_ple_proj):
    B, L, _ = h.shape
    o = jnp.concatenate([rmsnorm(o_sb.reshape(B, L, SB_W), g_out_sb),
                         rmsnorm(o_cm.reshape(B, L, CM_W), g_out_cm)], axis=-1)
    h = h + o @ w_out
    f = rmsnorm(h, g_ffn)
    h = h + (jax.nn.silu(f @ w_gate) * (f @ w_up)) @ w_down
    h = h + jax.nn.sigmoid(rmsnorm(h, g_ple) @ w_ple_gate) * (p @ w_ple_proj)
    return h

def setup_inputs(seed: int = 0) -> dict:
    key = jax.random.key(seed)
    ks = jax.random.split(key, 32)
    n_pages = PAST_LEN // PAGE_SIZE
    n_used = DEC_BATCH * n_pages
    n_phys = n_used + max(1, n_used // 4)

    def nrm(k, shape, s):
        return jax.random.normal(k, shape, jnp.float32) * s

    def gain(k, shape):
        return 1.0 + 0.1 * jax.random.normal(k, shape, jnp.float32)

    page_table = jax.random.permutation(ks[4], n_phys)[:n_used].reshape(DEC_BATCH, n_pages).astype(jnp.int32)
    sb_bias = (-jnp.linspace(SB_BIAS_MIN, SB_BIAS_MAX, SB_HEADS, dtype=jnp.float32)[None, :]
               + nrm(ks[25], (DEPTH, SB_HEADS), 0.1))
    return {
        "x_prompt": nrm(ks[0], (BATCH, SEQ, D_MODEL), 1.0),
        "x_sample": nrm(ks[1], (DEC_BATCH, DEC_SEQ, D_MODEL), 1.0),
        "cache_k": nrm(ks[2], (DEPTH, n_phys, PAGE_SIZE, SB_HEADS, HEAD_DIM), 1.0),
        "cache_v": nrm(ks[3], (DEPTH, n_phys, PAGE_SIZE, SB_HEADS, HEAD_DIM), 1.0),
        "page_table": page_table,
        "p_prompt": nrm(ks[5], (DEPTH, BATCH, SEQ, PLE_DIM), 1.0),
        "p_sample": nrm(ks[6], (DEPTH, DEC_BATCH, DEC_SEQ, PLE_DIM), 1.0),
        "g_mix": gain(ks[7], (DEPTH, D_MODEL)),
        "w_in": nrm(ks[8], (DEPTH, D_MODEL, IN_W), D_MODEL ** -0.5),
        "g_q": gain(ks[9], (DEPTH, HEAD_DIM)),
        "g_k": gain(ks[10], (DEPTH, HEAD_DIM)),
        "sb_bias": sb_bias,
        "sgu_ln_g": gain(ks[11], (DEPTH, CM_HEADS, CM_DIM)),
        "sgu_ln_b": nrm(ks[12], (DEPTH, CM_HEADS, CM_DIM), 0.02),
        "w_s": nrm(ks[13], (DEPTH, CM_HEADS, CHUNK, CHUNK), CHUNK ** -0.5),
        "b_s": gain(ks[14], (DEPTH, CM_HEADS, CHUNK)),
        "g_out_sb": gain(ks[15], (DEPTH, SB_W)),
        "g_out_cm": gain(ks[16], (DEPTH, CM_W)),
        "w_out": nrm(ks[17], (DEPTH, MIX_WIDTH, D_MODEL), MIX_WIDTH ** -0.5),
        "g_ffn": gain(ks[18], (DEPTH, D_MODEL)),
        "w_gate": nrm(ks[19], (DEPTH, D_MODEL, D_FF), D_MODEL ** -0.5),
        "w_up": nrm(ks[20], (DEPTH, D_MODEL, D_FF), D_MODEL ** -0.5),
        "w_down": nrm(ks[21], (DEPTH, D_FF, D_MODEL), D_FF ** -0.5),
        "g_ple": gain(ks[22], (DEPTH, D_MODEL)),
        "w_ple_gate": nrm(ks[23], (DEPTH, D_MODEL, D_MODEL), D_MODEL ** -0.5),
        "w_ple_proj": nrm(ks[24], (DEPTH, PLE_DIM, D_MODEL), PLE_DIM ** -0.5),
    }

def reference(x_prompt, x_sample, cache_k, cache_v, page_table, p_prompt, p_sample,
              g_mix, w_in, g_q, g_k, sb_bias, sgu_ln_g, sgu_ln_b, w_s, b_s, g_out_sb, g_out_cm,
              w_out, g_ffn, w_gate, w_up, w_down, g_ple, w_ple_gate, w_ple_proj):
    dec_b, dec_len = x_sample.shape[0], x_sample.shape[1]
    past_len = page_table.shape[1] * cache_k.shape[2]
    q_pos_s = past_len + jnp.arange(dec_len, dtype=jnp.int32)
    k_pos_s = jnp.arange(past_len + dec_len, dtype=jnp.int32)
    hp, hs = x_prompt, x_sample
    kp_l, vp_l, ks_l, vs_l, cs_l = [], [], [], [], []
    for i in range(DEPTH):
        qp, kp, vp, up, cp = mixer_inputs(hp, g_mix[i], w_in[i], g_q[i], g_k[i], sgu_ln_g[i], sgu_ln_b[i])
        o_sb_p = stick_breaking_prompt(qp, kp, vp, sb_bias[i])
        o_cm_p = chunk_mlp(up, cp, w_s[i], b_s[i])
        hp = layer_out(hp, o_sb_p, o_cm_p, p_prompt[i], g_out_sb[i], g_out_cm[i], w_out[i],
                       g_ffn[i], w_gate[i], w_up[i], w_down[i], g_ple[i], w_ple_gate[i], w_ple_proj[i])
        qs, kn, vn, us, cs = mixer_inputs(hs, g_mix[i], w_in[i], g_q[i], g_k[i], sgu_ln_g[i], sgu_ln_b[i])
        k_past = cache_k[i][page_table].reshape(dec_b, past_len, SB_HEADS, HEAD_DIM)
        v_past = cache_v[i][page_table].reshape(dec_b, past_len, SB_HEADS, HEAD_DIM)
        k_all = jnp.concatenate([k_past.astype(kn.dtype), kn], axis=1)
        v_all = jnp.concatenate([v_past.astype(vn.dtype), vn], axis=1)
        o_sb_s = stick_breaking(qs, k_all, v_all, sb_bias[i], q_pos_s, k_pos_s)
        o_cm_s = chunk_mlp(us, cs, w_s[i], b_s[i])
        hs = layer_out(hs, o_sb_s, o_cm_s, p_sample[i], g_out_sb[i], g_out_cm[i], w_out[i],
                       g_ffn[i], w_gate[i], w_up[i], w_down[i], g_ple[i], w_ple_gate[i], w_ple_proj[i])
        kp_l.append(kp)
        vp_l.append(vp)
        ks_l.append(kn)
        vs_l.append(vn)
        cs_l.append(cs)
    k_prompt_new = jnp.stack(kp_l)
    v_prompt_new = jnp.stack(vp_l)
    k_sample_new = jnp.stack(ks_l)
    v_sample_new = jnp.stack(vs_l)
    chunk_v_sample = jnp.stack(cs_l)
    return (hp, hs, k_prompt_new, v_prompt_new, k_sample_new, v_sample_new, chunk_v_sample)


_drawn_inputs = setup_inputs


def setup_inputs(seed=0):
    import zlib

    import numpy as np

    out = dict(_drawn_inputs(seed))
    spreads = {}
    factors = {'sgu_ln_b': 2.908, 'g_ple': 4.359}
    for name, (base, spread) in spreads.items():
        noise = np.random.default_rng([zlib.crc32(name.encode()), seed]).standard_normal(out[name].shape)
        drawn = base * np.exp(spread * noise) if base else spread * noise
        out[name] = __import__('jax').numpy.asarray(drawn.astype(out[name].dtype))
    for name, factor in factors.items():
        out[name] = (out[name] * factor).astype(out[name].dtype)
    return out
```

```python
from contextlib import ExitStack

import concourse.bass as bass
from concourse import mybir

F32 = mybir.dt.float32
F32R = mybir.dt.float32r
I32 = mybir.dt.int32
ALU = mybir.AluOpType
ACT = mybir.ActivationFunctionType

P = 128
D_MODEL = 2048
PROMPT = 512
SAMPLES = 8
TOK = PROMPT + SAMPLES
HALF = TOK // 2
HEADS = 8
PAGES = 8
N_PHYS = 80
D_FF = 5632
EPS = 1e-6
SCALE = float(P) ** -0.5

KT = D_MODEL // P
SLOTS = 16
FFN_GROUP = 4
FFN_CHUNKS = D_FF // P // FFN_GROUP

U_MLP = HEADS
U_KV = U_MLP + 2 * HEADS
U_OUT = U_KV + 2 * HEADS
U_OUT_SB = U_OUT + 8
U_FFN = U_OUT_SB + 8
U_LOOP = U_FFN + 2 * FFN_GROUP
CHUNK_UNITS = 3 * FFN_GROUP
U_LAST_DOWN = U_LOOP + CHUNK_UNITS * (FFN_CHUNKS - 1)
U_PROJ = U_LAST_DOWN + FFN_GROUP
U_GATE = U_PROJ + 2
UNITS = U_GATE + KT

T_OUT = U_OUT
T_OUT_SB = T_OUT + KT
T_FFN = T_OUT_SB + KT
T_LOOP = T_FFN + 2 * FFN_GROUP
CHUNK_TILES = 2 * FFN_GROUP + KT
T_LAST_DOWN = T_LOOP + CHUNK_TILES * (FFN_CHUNKS - 1)
T_PROJ = T_LAST_DOWN + KT
T_GATE = T_PROJ + KT



def tiles_before(u):
    if u <= U_OUT:
        return u
    if u <= U_FFN:
        return T_OUT + 2 * (u - U_OUT)
    if u <= U_LOOP:
        return T_FFN + u - U_FFN
    if u <= U_LAST_DOWN:
        c, x = divmod(u - U_LOOP, CHUNK_UNITS)
        return T_LOOP + CHUNK_TILES * c + min(x, 2 * FFN_GROUP) + 4 * max(x - 2 * FFN_GROUP, 0)
    if u <= U_PROJ:
        return T_LAST_DOWN + 4 * (u - U_LAST_DOWN)
    if u <= U_GATE:
        return T_PROJ + 8 * (u - U_PROJ)
    return T_GATE + u - U_GATE


CONSTS = 12
CM_ROOT = U_OUT - 2
SB_ROOT = U_OUT + 4
K_PERIOD = 10
K_PER = 3
N_PAGES = SAMPLES * PAGES
LAST_K = [K_PERIOD + (PAGES * b + PAGES - 1) // K_PER for b in range(SAMPLES)]
SUM_END = [p + 1 for p in LAST_K]
REDUCE_END = [18, 22, 25, 28, 31, 34, 37, 40]

DIAG = lambda kb: slice(kb * P, (kb + 1) * P)
OFF = {0: 512, 1: 1024, 2: 896}
CELLS = 1280


def k_pages(period):
    if period < K_PERIOD:
        return range(0)
    first = K_PER * (period - K_PERIOD)
    return range(min(first, N_PAGES), min(first + K_PER, N_PAGES))


def build(nc, w_units, x_t, p_t, cache_k, cache_v, page_table, g_mix, g_out, g_ffn, g_ple, g_q, g_k,
          ln_g, ln_b, w_s_t, b_s, sb_bias, w_s00, y_t, k_t, v_t, chunk_v_t):
    q_rows_dram = nc.dram_tensor("q_rows_dram", (SAMPLES, HEADS * P), F32, kind="Internal").ap()

    with ExitStack() as ctx:
        def sb(name, shape, dt=F32, where=ctx):
            return where.enter_context(nc.sbuf_tensor(name, shape, dt))

        def sem(name):
            return ctx.enter_context(nc.semaphore(name))

        x_hi = sb("x_hi", [P, KT, TOK], F32R)
        x_lo = sb("x_lo", [P, KT, TOK], F32R)
        w_raw = sb("w_raw", [P, 2, SLOTS * P])
        w_hi = sb("w_hi", [P, 2, SLOTS * P], F32R)
        w_lo = sb("w_lo", [P, 2, SLOTS * P], F32R)

        with ExitStack() as early:
            k_ring = sb("k_ring", [P, 2, HEADS * P], where=early)
            q_rows = sb("q_rows", [P, HEADS * P], where=early)
            dot_s = sb("dot_s", [P, PAGES * HEADS], where=early)
            acc = sb("acc", [P, HEADS * P], where=early)
            v_ring = sb("v_ring", [P, 2, HEADS * P], where=early)
            sb("pad", [P, 32], where=early)
            keep = sb("keep", [P, CELLS], where=early)
            pool_sq = sb("pool_sq", [P, TOK], where=early)
            z_s = sb("z_s", [P, PAGES * HEADS], where=early)
            soft_s = sb("soft_s", [P, PAGES * HEADS], where=early)
            keep_s = sb("keep_s", [P, PAGES * HEADS], where=early)
            chunk_v = sb("chunk_v", [P, HEADS, SAMPLES], where=early)
        h = sb("h", [P, KT, TOK])
        H_KEYS, H_PAGES = 6, 12

        with ExitStack() as early:
            q = sb("q", [P, HEADS, TOK], where=early)
            o_cm = sb("o_cm", [P, HEADS, TOK], where=early)
        with ExitStack() as late:
            proj = sb("proj", [P, KT, TOK], where=late)
        act_hi = sb("act_hi", [P, 2, FFN_GROUP, TOK], F32R)
        act_lo = sb("act_lo", [P, 2, FFN_GROUP, TOK], F32R)

        ones = sb("ones", [P, P])
        later = sb("later", [P, P])
        causal = sb("causal", [P, P])
        ident = sb("ident", [P, P])
        eps = sb("eps", [P, 1])
        one = sb("one", [P, 1])
        gain_mix = sb("gain_mix", [P, KT])
        gain_out = sb("gain_out", [P, KT])
        gain_ffn = sb("gain_ffn", [P, KT])
        gain_ple = sb("gain_ple", [P, KT])
        gain_q = sb("gain_q", [P, 1])
        gain_k = sb("gain_k", [P, 1])
        lng = sb("lng", [P, HEADS])
        lnb = sb("lnb", [P, HEADS])
        bias = sb("bias", [P, HEADS])
        w00 = sb("w00", [P, HEADS])
        table = sb("table", [1, N_PAGES], I32)
        dot_pad = sb("dot_pad", [P, 1])
        a_s = sb("a_s", [P, 3, PAGES * HEADS])
        x_r = sb("x_r", [P, TOK])
        sq = sb("sq", [P, TOK])
        cm_r = sb("cm_r", [P, TOK])
        sb_r = sb("sb_r", [P, TOK])

        with ExitStack() as early:
            y = sb("y", [P, 2, TOK], where=early)
            v_tok = sb("v_tok", [P, 4, P], where=early)
            with ExitStack() as mlp:
                vg = sb("vg", [P, TOK], where=mlp)
                ug = sb("ug", [P, TOK], where=mlp)
                w_mix = sb("w_mix", [P, HEADS, P], where=mlp)
                b_mix = sb("b_mix", [P, HEADS, P], where=mlp)
            k_head = sb("k_head", [P, TOK], where=early)
            z = sb("z", [P, CELLS], where=early)
            soft = sb("soft", [P, CELLS], where=early)
        y_gate = sb("y_gate", [P, TOK])
        y_up = sb("y_up", [P, TOK])
        h_sq = sb("h_sq", [P, 2, TOK])
        h_sum = sb("h_sum", [P, TOK])
        h_r = sb("h_r", [P, TOK])
        p_raw = sb("p_raw", [P, 2, TOK])

        out_ps = ctx.enter_context(nc.psum_tensor("out_ps", [P, 4, 512], F32))
        pair_ps = ctx.enter_context(nc.psum_tensor("pair_ps", [P, 2, 512], F32))
        tok_ps = ctx.enter_context(nc.psum_tensor("tok_ps", [P, 512], F32))
        mix_ps = ctx.enter_context(nc.psum_tensor("mix_ps", [P, 512], F32))

        def tile_ps(t):
            return out_ps[:, 2 * (t % 2):2 * (t % 2) + 2, 0:HALF]

        def halves(x):
            return x.rearrange("p (a n) -> p a n", a=2)

        pair = pair_ps[:, :, 0:HALF]
        pair_flat = pair_ps[:, :, :].rearrange("p a n -> p (a n)")

        x_in = [sem(f"x_in{i}") for i in range(4)]
        w_in = [sem(f"w_in{i}") for i in range(2)]
        consts_in = sem("consts_in")
        table_in = sem("table_in")
        k_in = [sem(f"k_in{i}") for i in range(2)]
        v_in = [sem(f"v_in{i}") for i in range(2)]
        q_rows_out = sem("q_rows_out")
        q_rows_in = sem("q_rows_in")
        h_in = [sem(f"h_in{i}") for i in range(3)]
        p_in = sem("p_in")
        k_out = sem("k_out")
        v_out = sem("v_out")
        y_out = sem("y_out")
        chunk_out = sem("chunk_out")
        hi_done = sem("hi_done")
        x_hi_done = sem("x_hi_done")
        sq_done = sem("sq_done")
        gelu_done = sem("gelu_done")
        ln_done = sem("ln_done")
        rstd_done = sem("rstd_done")
        root_done = sem("root_done")
        soft_done = sem("soft_done")
        soft_s_done = sem("soft_s_done")
        a_done = sem("a_done")
        a_s_done = sem("a_s_done")
        act_step = sem("act_step")
        silu_done = sem("silu_done")
        act_hi_done = sem("act_hi_done")
        lo_done = sem("lo_done")
        x_lo_done = sem("x_lo_done")
        sum_done = sem("sum_done")
        out_read = sem("out_read")
        norm_done = sem("norm_done")
        centred = sem("centred")
        tok_read = sem("tok_read")
        mix_read = sem("mix_read")
        pair_read = sem("pair_read")
        r_done = sem("r_done")
        cm_done = sem("cm_done")
        k_used = sem("k_used")
        z_done = sem("z_done")
        z_s_done = sem("z_s_done")
        keep_done = sem("keep_done")
        keep_s_done = sem("keep_s_done")
        arg_done = sem("arg_done")
        arg_s_done = sem("arg_s_done")
        masked = sem("masked")
        vec_step = sem("vec_step")
        act_done = sem("act_done")
        act_lo_done = sem("act_lo_done")
        h_final = sem("h_final")
        built = sem("built")
        pool_step = sem("pool_step")
        v_used = sem("v_used")
        cm_sum_done = sem("cm_sum_done")
        sb_sum_done = sem("sb_sum_done")
        out_done = sem("out_done")
        x_sum_ready = sem("x_sum_ready")
        ms_ready = sem("ms_ready")
        mean_ready = sem("mean_ready")
        q_rows_ready = sem("q_rows_ready")
        turned = sem("turned")
        mixed = sem("mixed")
        z_ready = sem("z_ready")
        later_ready = sem("later_ready")
        later_s_ready = sem("later_s_ready")
        av_ready = sem("av_ready")
        o_s_ready = sem("o_s_ready")

        tok_jobs = []
        for u in range(U_OUT + 2):
            if U_MLP + 2 <= u <= U_KV and u % 2 == 0 or U_KV + 2 <= u <= U_OUT and u % 2 == 0:
                tok_jobs.append(("turn", u))
            if U_KV + 3 <= u <= U_OUT + 1 and u % 2 == 1:
                tok_jobs.append(("av", u))
            if u in REDUCE_END:
                tok_jobs.append(("reduce", u))
            if u in SUM_END:
                tok_jobs.append(("later", u))

        def reads_before(kind, u):
            return tok_jobs.index((kind, u))

        block = ctx.enter_context(nc.Block())

        @block.sync
        def _(sp):
            def load_unit(u):
                if u >= 2:
                    sp.wait_ge(lo_done, 2 * u - 2)
                sp.dma_start(w_raw[:, u % 2, :], w_units[u]).then_inc(w_in[u % 2], 16)

            def load_x(i):
                sp.dma_start(h[:, 4 * i:4 * i + 4, :], x_t[:, 4 * i:4 * i + 4, :]).then_inc(x_in[i], 16)

            def load_k(j):
                b, pg = divmod(j, PAGES)
                if pg == 0:
                    if b:
                        sp.wait_ge(k_used, HEADS * j)
                    sp.dma_start(q_rows[:, :], q_rows_dram[b:b + 1, :].to_broadcast([P, HEADS * P]))\
                        .then_inc(q_rows_in, 16)
                page = sp.value_load(table[0:1, j:j + 1], min_val=0, max_val=N_PHYS - 1)
                if j >= 2:
                    sp.wait_ge(k_used, HEADS * (j - 1))
                sp.dma_start(k_ring[:, j % 2, :],
                             cache_k[bass.ds(page, 1), :, :].rearrange("a p n -> (a p) n"))\
                    .then_inc(k_in[j % 2], 16)

            sp.dma_start(table[:, :], page_table).then_inc(table_in, 16)
            load_x(0)
            load_unit(0)
            for i in range(1, 4):
                load_x(i)
            load_unit(1)
            sp.wait_ge(table_in, 16)
            next_k = 0
            for u in range(U_FFN):
                load_unit(u + 2)
                if u == K_PERIOD - 1:
                    sp.wait_ge(pair_read, 1)
                    sp.dma_start(q_rows_dram, acc[0:SAMPLES, :]).then_inc(q_rows_out, 16)
                    sp.wait_ge(q_rows_out, 16)
                while u >= K_PERIOD - 1 and next_k < min(N_PAGES, K_PER * (u + 1 - K_PERIOD) + 2):
                    load_k(next_k)
                    next_k += 1
                if U_KV + 2 <= u <= U_OUT and u % 2 == 0:
                    i = (u - U_KV - 2) // 2
                    sp.wait_ge(norm_done, 2 * HEADS + i + 1)
                    sp.dma_start(k_t[i], k_head[:, :]).then_inc(k_out, 16)
                    sp.wait_ge(out_read, U_KV + 2 * i + 2)
                    sp.dma_start(v_t[i], y[:, 1, :]).then_inc(v_out, 16)
                if u == U_KV + 2:
                    sp.wait_ge(cm_done, HEADS)
                    sp.dma_start(chunk_v_t, chunk_v[:, :, :]).then_inc(chunk_out, 16)
                if u == LAST_K[-1] + 3:
                    sp.wait_ge(z_s_done, SAMPLES)
                    sp.dma_start(h[:, 0:H_KEYS, :], x_t[:, 0:H_KEYS, :]).then_inc(h_in[0], 16)
                if u == REDUCE_END[-1] + 2:
                    sp.wait_ge(tok_read, reads_before("reduce", REDUCE_END[-1]) + 1)
                    sp.dma_start(h[:, H_KEYS:H_PAGES, :], x_t[:, H_KEYS:H_PAGES, :]).then_inc(h_in[1], 16)
                if u == U_OUT + 3:
                    sp.wait_ge(av_ready, HEADS)
                    sp.wait_ge(sb_sum_done, 1)
                    sp.dma_start(h[:, H_PAGES:KT, :], x_t[:, H_PAGES:KT, :]).then_inc(h_in[2], 16)
                if u == U_OUT_SB:
                    sp.dma_start(p_raw[:, :, :], p_t).then_inc(p_in, 16)
            with sp.Fori((U_FFN + 2) // 2, UNITS // 2) as i:
                for s in range(2):
                    sp.wait_ge(lo_done, 4 * i + (2 * s - 2))
                    sp.dma_start(w_raw[:, s, :], w_units[bass.ds(2 * i + s, 1), :, :]
                                 .rearrange("a p n -> (a p) n")).then_inc(w_in[s], 16)
            for m in range(KT):
                sp.wait_ge(h_final, KT + m + 1)
                sp.dma_start(y_t[:, m, :], h[:, m, :]).then_inc(y_out, 16)
            sp.wait_ge(y_out, 16 * KT)
            sp.wait_ge(k_out, 16 * HEADS)
            sp.wait_ge(v_out, 16 * HEADS)
            sp.wait_ge(chunk_out, 16)

        @block.gpsimd
        def _(pool):
            steps = [0]

            def chained(ins):
                steps[0] += 1
                ins.then_inc(pool_step, 1)
                pool.wait_ge(pool_step, steps[0])

            chained(pool.memset(ones[:, :], 1.0))
            chained(pool.memset(eps[:, :], EPS))
            chained(pool.memset(one[:, :], 1.0))
            chained(pool.memset(cm_r[:, :], 0.0))
            chained(pool.memset(sb_r[:, :], 0.0))
            chained(pool.affine_select(out=later[:, :], in_=ones[:, :], compare_op=ALU.is_gt, fill=0.0,
                                       base=0, pattern=[[-1, P]], channel_multiplier=1))
            chained(pool.affine_select(out=causal[:, :], in_=ones[:, :], compare_op=ALU.is_gt, fill=0.0,
                                       base=0, pattern=[[1, P]], channel_multiplier=-1))
            chained(pool.affine_select(out=ident[:, :], in_=ones[:, :], compare_op=ALU.is_equal,
                                       fill=0.0, base=0, pattern=[[-1, P]], channel_multiplier=1))
            pool.wait_ge(consts_in, CONSTS * 16)
            pool.affine_select(out=w_mix[:, :, :], in_=w_mix[:, :, :], compare_op=ALU.is_ge, fill=0.0,
                               base=0, pattern=[[0, HEADS], [1, P]], channel_multiplier=-1)\
                .then_inc(built, 1)

            def load_v(j):
                page = pool.value_load(table[0:1, j:j + 1], min_val=0, max_val=N_PHYS - 1)
                if j >= 2:
                    pool.wait_ge(v_used, j - 1)
                pool.dma_start(v_ring[:, j % 2, :],
                               cache_v[bass.ds(page, 1), :, :].rearrange("a p n -> (a p) n"))\
                    .then_inc(v_in[j % 2], 16)

            def add_page(j):
                b, pg = divmod(j, PAGES)
                pool.wait_ge(v_in[j % 2], 16 * (j // 2 + 1))
                values = v_ring[:, j % 2, :].rearrange("p (h d) -> p h d", h=HEADS)
                weights = a_s[:, b % 3, pg * HEADS:(pg + 1) * HEADS].unsqueeze(2).to_broadcast([P, HEADS, P])
                if pg == 0:
                    if b == 0:
                        pool.wait_ge(q_rows_out, 16)
                    else:
                        pool.wait_ge(o_s_ready, b)
                    pool.wait_ge(a_s_done, b + 1)
                    pool.tensor_tensor(acc[:, :].rearrange("p (h d) -> p h d", h=HEADS), values, weights,
                                       ALU.mult).then_inc(v_used, 1)
                else:
                    chained(pool.tensor_tensor(values, values, weights, ALU.mult))
                    pool.wait_ge(v_used, j)
                    pool.tensor_tensor(acc[:, :], acc[:, :], v_ring[:, j % 2, :], ALU.add)\
                        .then_inc(v_used, 1)
                if j + 2 < N_PAGES:
                    load_v(j + 2)

            def add_squares(x, total, cols, done=pool_step):
                chained(pool.tensor_tensor(pool_sq[:, cols], x, x, ALU.mult))
                ins = pool.tensor_tensor(total[:, cols], total[:, cols], pool_sq[:, cols], ALU.add)
                if done is pool_step:
                    chained(ins)
                else:
                    ins.then_inc(done, 1)
                    pool.wait_ge(done, 1)

            jobs = [(LAST_K[j // PAGES] + 2 + j % PAGES * 0.25, "page", j) for j in range(N_PAGES)]
            jobs += [(U_MLP + 3.5 + 2 * i, "mlp", i) for i in range(HEADS)]
            jobs += [(U_KV + 3.7 + 2 * i, "attention", i) for i in range(HEADS)]
            pool.wait_ge(table_in, 16)
            pool.wait_ge(x_lo_done, KT)
            pool.wait_ge(sq_done, KT)
            load_v(0)
            load_v(1)
            for _, kind, i in sorted(jobs):
                if kind == "page":
                    add_page(i)
                elif kind == "mlp":
                    pool.wait_ge(cm_done, i + 1)
                    add_squares(o_cm[:, i, :], cm_r, slice(0, TOK), cm_sum_done if i == HEADS - 1 else pool_step)
                else:
                    pool.wait_ge(tok_read, reads_before("av", U_KV + 3 + 2 * i) + 1)
                    add_squares(q[:, i, 0:PROMPT], sb_r, slice(0, PROMPT))
            pool.wait_ge(tok_read, reads_before("reduce", REDUCE_END[-1]) + 1)
            for i in range(HEADS):
                add_squares(q[:, i, PROMPT:TOK], sb_r, slice(PROMPT, TOK),
                            sb_sum_done if i == HEADS - 1 else pool_step)

        @block.scalar
        def _(act):
            for dst, src in ((gain_mix[:, :], g_mix), (gain_out[:, :], g_out), (gain_ffn[:, :], g_ffn),
                             (gain_ple[:, :], g_ple), (gain_q[:, :], g_q), (gain_k[:, :], g_k),
                             (lng[:, :], ln_g), (lnb[:, :], ln_b), (w_mix[:, :, :], w_s_t),
                             (b_mix[:, :, :], b_s.to_broadcast([P, HEADS, P])),
                             (bias[:, :], sb_bias.to_broadcast([P, HEADS])),
                             (w00[:, :], w_s00.to_broadcast([P, HEADS]))):
                act.dma_start(dst, src).then_inc(consts_in, 16)

            steps = [0]

            def chained(ins):
                steps[0] += 1
                ins.then_inc(act_step, 1)
                act.wait_ge(act_step, steps[0])

            def split_w(u, it=0, landed=0, tiles=0):
                act.wait_ge(w_in[u % 2], it * landed + 16 * (u // 2 + 1))
                if u >= 2:
                    act.wait_ge(out_done, it * tiles + tiles_before(u - 1))
                for j in range(2):
                    cols = slice(j * 8 * P, (j + 1) * 8 * P)
                    act.activation(w_hi[:, u % 2, cols], w_raw[:, u % 2, cols], ACT.Copy)\
                        .then_inc(hi_done, 1)

            def split(dst, src, gain):
                act.activation(dst, src, ACT.Copy, scale=gain).then_inc(x_hi_done, 1)

            def root(n, features, dst):
                act.wait_ge(x_sum_ready, n + 1)
                act.activation(halves(dst), pair, ACT.Sqrt, bias=eps[:, 0:1], scale=1.0 / features)\
                    .then_inc(root_done, 1)

            def rstd(n):
                act.wait_ge(ms_ready, n + 1)
                act.activation(halves(sq[:, :]), pair, ACT.Ln, bias=eps[:, 0:1], scale=1.0 / P)\
                    .then_inc(ln_done, 1)
                act.wait_ge(ln_done, n + 1)
                act.activation(sq[:, :], sq[:, :], ACT.Exp, scale=-0.5).then_inc(rstd_done, 1)

            def square_head(n, src):
                if n:
                    act.wait_ge(norm_done, n)
                act.activation(sq[:, :], src, ACT.Square).then_inc(sq_done, 1)

            def soften(l, zz, done):
                chained(act.activation(l, zz, ACT.Abs))
                chained(act.activation(l, l, ACT.Exp, scale=-1.0))
                act.activation(l, l, ACT.Ln, bias=one[:, 0:1]).then_inc(done, 1)

            def square_residual(n, k):
                if k >= 2:
                    act.wait_ge(sum_done, n + k - 1)
                act.activation(h_sq[:, k % 2, :], h[:, k, :], ACT.Square).then_inc(sq_done, 1)

            act.wait_ge(consts_in, CONSTS * 16)
            act.wait_ge(built, 1)
            for k in range(KT):
                if k % 4 == 0:
                    act.wait_ge(x_in[k // 4], 16)
                split(x_hi[:, k, :], h[:, k, :], gain_mix[:, k:k + 1])
                if k == 3:
                    split_w(0)
                if k >= 2:
                    act.wait_ge(sum_done, k - 1)
                act.activation(y[:, k % 2, :], h[:, k, :], ACT.Square).then_inc(sq_done, 1)
            split_w(1)
            root(0, D_MODEL, x_r[:, :])

            for u in range(1, U_FFN):
                t = u - 1
                if u <= U_MLP:
                    act.wait_ge(out_read, t + 1)
                    square_head(t, y[:, t % 2, :])
                    split_w(u + 1)
                    rstd(t)
                elif u <= U_KV and u % 2 == 1:
                    i = (u - U_MLP - 1) // 2
                    act.wait_ge(out_read, t + 1)
                    if i:
                        act.wait_ge(tok_read, reads_before("turn", U_MLP + 2 * i) + 1)
                    act.activation(vg[:, :], y[:, t % 2, :], ACT.Gelu).then_inc(gelu_done, 1)
                    split_w(u + 1)
                    act.wait_ge(centred, i + 1)
                    square_head(HEADS + i, vg[:, :])
                elif u <= U_KV:
                    i = (u - U_MLP - 2) // 2
                    rstd(HEADS + i)
                    split_w(u + 1)
                    act.wait_ge(out_read, t + 1)
                    if i:
                        act.wait_ge(cm_done, i)
                    act.activation(ug[:, :], y[:, t % 2, :], ACT.Gelu).then_inc(gelu_done, 1)
                elif u < U_OUT and u % 2 == 1:
                    i = (u - U_KV - 1) // 2
                    act.wait_ge(out_read, t + 1)
                    square_head(2 * HEADS + i, y[:, t % 2, :])
                    if i:
                        act.wait_ge(arg_done, i)
                        act.activation(z[:, :], z[:, :], ACT.Exp).then_inc(a_done, 1)
                    split_w(u + 1)
                    rstd(2 * HEADS + i)
                elif u <= U_OUT:
                    i = (u - U_KV - 2) // 2
                    if u == U_OUT:
                        act.wait_ge(out_done, U_OUT)
                        for k in range(HEADS):
                            split(x_hi[:, HEADS + k, :], o_cm[:, k, :], gain_out[:, HEADS + k:HEADS + k + 1])
                    split_w(u + 1)
                    act.wait_ge(z_done, i + 1)
                    soften(soft[:, :], z[:, :], soft_done)
                elif u == U_OUT + 1:
                    act.wait_ge(arg_done, HEADS)
                    act.activation(z[:, :], z[:, :], ACT.Exp).then_inc(a_done, 1)
                    split_w(u + 1)
                else:
                    split_w(u + 1)
                if u > U_OUT_SB:
                    for k in range(2 * (u - U_OUT_SB - 1), 2 * (u - U_OUT_SB)):
                        act.wait_ge(h_final, k + 1)
                        if k < 8:
                            split(x_hi[:, 8 + k, :], h[:, k, :], gain_ffn[:, k:k + 1])
                        square_residual(KT, k)
                if u == CM_ROOT:
                    root(1, HEADS * P, cm_r[:, :])
                if u == SB_ROOT:
                    root(2, HEADS * P, sb_r[:, :])
                    for k in range(HEADS):
                        split(x_hi[:, k, :], q[:, k, :], gain_out[:, k:k + 1])
                if u in SUM_END:
                    b = SUM_END.index(u)
                    act.wait_ge(z_s_done, b + 1)
                    soften(soft_s[:, :], z_s[:, :], soft_s_done)
                if u - 1 in SUM_END:
                    b = SUM_END.index(u - 1)
                    act.wait_ge(arg_s_done, b + 1)
                    if b >= 3:
                        act.wait_ge(v_used, PAGES * (b - 2))
                    act.activation(a_s[:, b % 3, :], z_s[:, :], ACT.Exp).then_inc(a_s_done, 1)

            act.wait_ge(out_done, T_FFN)
            for k in range(8, KT):
                if k >= KT - 2:
                    act.wait_ge(h_final, k + 1)
                split(x_hi[:, k - 8, :], h[:, k, :], gain_ffn[:, k:k + 1])
            for k in range(KT - 2, KT):
                square_residual(KT, k)

            def gate_up(u, n, t, par, g, it=0):
                split_w(u + 1, it, 16 * CHUNK_UNITS, 2 * CHUNK_TILES)
                if u == U_FFN:
                    root(3, D_MODEL, h_r[:, :])
                act.wait_ge(out_read, it * (2 * CHUNK_TILES) + (t + 1))
                act.activation(y_gate[:, :], y_gate[:, :], ACT.Silu).then_inc(silu_done, 1)
                split_w(u + 2, it, 16 * CHUNK_UNITS, 2 * CHUNK_TILES)
                act.wait_ge(act_done, it * (2 * FFN_GROUP) + (n + 1))
                act.activation(act_hi[:, par, g, :], y_up[:, :], ACT.Copy).then_inc(act_hi_done, 1)

            for g in range(FFN_GROUP):
                gate_up(U_FFN + 2 * g, g, T_FFN + 2 * g, 0, g)
            with act.Fori(0, (FFN_CHUNKS - 1) // 2) as it:
                for half in range(2):
                    u0 = U_LOOP + half * CHUNK_UNITS
                    for g in range(FFN_GROUP):
                        gate_up(u0 + 2 * g, FFN_GROUP * (1 + half) + g, tiles_before(u0 + 2 * g), 1 - half, g, it)
                    for g in range(FFN_GROUP):
                        split_w(u0 + 2 * FFN_GROUP + g + 1, it, 16 * CHUNK_UNITS, 2 * CHUNK_TILES)

            act.wait_ge(p_in, 16)
            for k in range(2):
                act.activation(x_hi[:, k, :], p_raw[:, k, :], ACT.Copy).then_inc(x_hi_done, 1)
            for g in range(FFN_GROUP):
                split_w(U_LAST_DOWN + g + 1)
                for k in range(4 * g, 4 * g + 4):
                    act.wait_ge(out_read, T_LAST_DOWN + k + 1)
                    if k >= 2:
                        split(x_hi[:, k, :], h[:, k, :], gain_ple[:, k:k + 1])
                    square_residual(2 * KT, k)
            split_w(U_PROJ + 1)
            split_w(U_GATE)
            act.wait_ge(out_done, T_GATE)
            for k in range(2):
                split(x_hi[:, k, :], h[:, k, :], gain_ple[:, k:k + 1])
            root(4, D_MODEL, h_r[:, :])
            for m in range(KT):
                if U_GATE + m + 1 < UNITS:
                    split_w(U_GATE + m + 1)
                act.wait_ge(out_read, T_GATE + m + 1)
                act.activation(y_gate[:, :], y_gate[:, :], ACT.Sigmoid).then_inc(silu_done, 1)

        @block.vector
        def _(dve):
            count = {}

            def chained(ins, done=vec_step):
                count[done.name] = count.get(done.name, 0) + 1
                ins.then_inc(done, 1)
                dve.wait_ge(done, count[done.name])

            def low_w(u, j, it=0):
                dve.wait_ge(hi_done, it * (4 * CHUNK_UNITS) + (2 * u + j + 1))
                cols = slice(j * 8 * P, (j + 1) * 8 * P)
                dve.tensor_tensor(w_lo[:, u % 2, cols], w_raw[:, u % 2, cols], w_hi[:, u % 2, cols],
                                  ALU.subtract).then_inc(lo_done, 1)

            n_split = [0]

            def low_x(slot, src, gain):
                n_split[0] += 1
                dve.wait_ge(x_hi_done, n_split[0])
                dve.scalar_tensor_tensor(out=x_lo[:, slot, :], in0=src, scalar=gain, in1=x_hi[:, slot, :],
                                         op0=ALU.mult, op1=ALU.subtract).then_inc(x_lo_done, 1)

            def add_square(n_sq, k, src, total):
                dve.wait_ge(sq_done, n_sq + k + 1)
                if k == 0:
                    chained(dve.tensor_copy(total, src), sum_done)
                else:
                    chained(dve.tensor_tensor(total, total, src, ALU.add), sum_done)

            def invert(n, dst):
                dve.wait_ge(root_done, n + 1)
                chained(dve.reciprocal(dst, dst), r_done)

            def normalise(n, dst, src, gain, done=norm_done):
                dve.wait_ge(rstd_done, n + 1)
                chained(dve.scalar_tensor_tensor(out=dst, in0=src, scalar=gain, in1=sq[:, :],
                                                 op0=ALU.mult, op1=ALU.mult), done)

            def take(t, dst, r):
                dve.wait_ge(out_done, t + 1)
                chained(dve.tensor_tensor(halves(dst), tile_ps(t), halves(r), ALU.mult), out_read)

            def score_page(j):
                b, pg = divmod(j, PAGES)
                if pg == 0:
                    dve.wait_ge(q_rows_in, 16 * (b + 1))
                dve.wait_ge(k_in[j % 2], 16 * (j // 2 + 1))
                for hd in range(HEADS):
                    cols = slice(hd * P, (hd + 1) * P)
                    at = pg * HEADS + hd
                    dve.tensor_tensor_reduce(k_ring[:, j % 2, cols], k_ring[:, j % 2, cols],
                                             q_rows[:, cols], 1.0, 0.0, ALU.mult, ALU.add,
                                             dot_s[:, at:at + 1]).then_inc(k_used, 1)
                if pg == PAGES - 1:
                    dve.wait_ge(k_used, HEADS * (j + 1))
                    if b:
                        dve.wait_ge(a_s_done, b)
                    chained(dve.scalar_tensor_tensor(
                        out=z_s[:, :].rearrange("p (g h) -> p g h", h=HEADS),
                        in0=dot_s[:, :].rearrange("p (g h) -> p g h", h=HEADS), scalar=SCALE,
                        in1=bias[:, :].unsqueeze(1).to_broadcast([P, PAGES, HEADS]),
                        op0=ALU.mult, op1=ALU.add), z_s_done)

            def keep_sample(b):
                dve.wait_ge(soft_s_done, b + 1)
                chained(dve.scalar_tensor_tensor(out=keep_s[:, :], in0=z_s[:, :], scalar=0.0,
                                                 in1=soft_s[:, :], op0=ALU.max, op1=ALU.add))
                chained(dve.scalar_tensor_tensor(out=z_s[:, :], in0=z_s[:, :], scalar=0.0,
                                                 in1=soft_s[:, :], op0=ALU.min, op1=ALU.subtract))

                def page(x, pg):
                    return x[:, pg * HEADS:(pg + 1) * HEADS]

                chained(dve.tensor_copy(page(soft_s, PAGES - 2), page(keep_s, PAGES - 1)))
                for pg in range(PAGES - 3, -1, -1):
                    chained(dve.tensor_tensor(page(soft_s, pg), page(soft_s, pg + 1), page(keep_s, pg + 1),
                                              ALU.add), keep_s_done if pg == 0 else vec_step)

            def weigh_sample(b):
                dve.wait_ge(later_s_ready, b + 1)
                chained(dve.tensor_tensor(z_s[:, :], z_s[:, :], tok_ps[:, 0:PAGES * HEADS], ALU.subtract),
                        tok_read)
                chained(dve.tensor_copy(dot_pad[:, :], z_s[:, 0:1]), arg_s_done)

            def diagonal(x):
                return x[:, 0:PROMPT].rearrange("p (c n) -> p c n", c=4)

            causal4 = causal[:, :].unsqueeze(1).to_broadcast([P, 4, P])

            def logits(i):
                dve.wait_ge(z_ready, i + 1)
                chained(dve.tensor_scalar(z[:, 0:1024], pair_flat, SCALE, bias[:, i:i + 1],
                                          ALU.mult, ALU.add), pair_read)
                chained(dve.tensor_scalar(z[:, 1024:CELLS], mix_ps[:, 0:CELLS - 1024], SCALE,
                                          bias[:, i:i + 1], ALU.mult, ALU.add), z_done)

            def keep_head(i):
                dve.wait_ge(soft_done, i + 1)
                chained(dve.scalar_tensor_tensor(out=keep[:, :], in0=z[:, :], scalar=0.0, in1=soft[:, :],
                                                 op0=ALU.max, op1=ALU.add))
                chained(dve.scalar_tensor_tensor(out=z[:, :], in0=z[:, :], scalar=0.0, in1=soft[:, :],
                                                 op0=ALU.min, op1=ALU.subtract))
                chained(dve.tensor_tensor(diagonal(keep), diagonal(keep), causal4, ALU.mult))
                chained(dve.tensor_tensor(soft[:, 0:P], keep[:, DIAG(3)], keep[:, 896:1024], ALU.add))
                chained(dve.tensor_tensor(soft[:, P:2 * P], keep[:, DIAG(2)], keep[:, 1024:1152], ALU.add))
                chained(dve.tensor_tensor(soft[:, 2 * P:3 * P], soft[:, 0:P], keep[:, 1152:1280], ALU.add),
                        keep_done)

            def exponents(i):
                dve.wait_ge(later_ready, i + 1)
                chained(dve.tensor_tensor(z[:, 0:1024], z[:, 0:1024], pair_flat, ALU.subtract), pair_read)
                chained(dve.tensor_tensor(z[:, 1024:CELLS], z[:, 1024:CELLS], mix_ps[:, 0:CELLS - 1024],
                                          ALU.subtract), arg_done)

            def mask_weights(i):
                dve.wait_ge(a_done, i + 1)
                chained(dve.tensor_tensor(diagonal(z), diagonal(z), causal4, ALU.mult), masked)

            def take_attention(i):
                dve.wait_ge(av_ready, i + 1)
                chained(dve.tensor_copy(q[:, i, 0:PROMPT], tok_ps[:, :]), tok_read)

            def take_turned(n):
                dve.wait_ge(turned, n + 1)
                chained(dve.tensor_copy(v_tok[:, :, :].rearrange("p c n -> p (c n)"), tok_ps[:, :]), tok_read)

            def out_tile(n, r):
                m = n % KT
                if n in (0, H_KEYS, H_PAGES):
                    dve.wait_ge(h_in[(0, H_KEYS, H_PAGES).index(n)], 16)
                take(T_OUT + n, sq[:, :], r[:, :])
                chained(dve.tensor_tensor(h[:, m, :], h[:, m, :], sq[:, :], ALU.add),
                        h_final if n >= KT else vec_step)

            dve.wait_ge(built, 1)
            for k in range(KT):
                low_x(k, h[:, k, :], gain_mix[:, k:k + 1])
                if k == 3:
                    low_w(0, 0)
                    low_w(0, 1)
                add_square(0, k, y[:, k % 2, :], x_r[:, :])
            low_w(1, 0)
            low_w(1, 1)
            invert(0, x_r[:, :])

            for u in range(1, U_FFN):
                t = u - 1
                if u <= U_OUT:
                    if t > U_KV and t % 2 == 1 and t > U_KV + 2:
                        dve.wait_ge(v_out, 16 * ((t - U_KV - 1) // 2))
                    take(t, y[:, t % 2, :], x_r[:, :])
                else:
                    out_tile(2 * (u - U_OUT) - 1, cm_r if u <= U_OUT_SB else sb_r)
                if u - 1 in REDUCE_END:
                    b = REDUCE_END.index(u - 1)
                    dve.wait_ge(o_s_ready, b + 1)
                    if u - 1 in SUM_END:
                        dve.wait_ge(later_s_ready, SUM_END.index(u - 1) + 1)
                    chained(dve.tensor_copy(q[:, :, PROMPT + b], tok_ps[:, P:P + HEADS]), tok_read)
                if u - 1 in SUM_END:
                    weigh_sample(SUM_END.index(u - 1))

                if u <= U_MLP:
                    low_w(u + 1, 0)
                    low_w(u + 1, 1)
                    normalise(t, q[:, t, :], y[:, t % 2, :], gain_q[:, 0:1])
                elif u <= U_KV + 1 and u % 2 == 1:
                    if u == U_MLP + 1:
                        dve.wait_ge(q_rows_ready, 1)
                        chained(dve.tensor_copy(acc[0:SAMPLES, :], pair_flat[0:SAMPLES, :]), pair_read)
                    else:
                        i = (u - U_MLP - 3) // 2
                        dve.wait_ge(mixed, i + 1)
                        chained(dve.tensor_tensor(
                            o_cm[:, i, 0:PROMPT].rearrange("p (c n) -> p c n", c=4),
                            mix_ps[:, :].rearrange("p (c n) -> p c n", c=4),
                            b_mix[:, i, :].unsqueeze(1).to_broadcast([P, 4, P]), ALU.add), mix_read)
                        dve.wait_ge(gelu_done, 2 * i + 2)
                        chained(dve.tensor_tensor(o_cm[:, i, :], o_cm[:, i, :], ug[:, :], ALU.mult), cm_done)
                    low_w(u + 1, 0)
                    low_w(u + 1, 1)
                    if u < U_KV:
                        i = (u - U_MLP - 1) // 2
                        dve.wait_ge(mean_ready, i + 1)
                        dve.wait_ge(gelu_done, 2 * i + 1)
                        chained(dve.scalar_tensor_tensor(out=halves(vg[:, :]), in0=pair, scalar=-1.0 / P,
                                                         in1=halves(vg[:, :]), op0=ALU.mult, op1=ALU.add),
                                centred)
                elif u <= U_KV:
                    i = (u - U_MLP - 2) // 2
                    normalise(HEADS + i, vg[:, :], vg[:, :], lng[:, i:i + 1], vec_step)
                    chained(dve.tensor_scalar(vg[:, :], vg[:, :], lnb[:, i:i + 1], None, ALU.add), norm_done)
                    chained(dve.tensor_copy(chunk_v[:, i, :], vg[:, PROMPT:TOK]))
                    chained(dve.tensor_scalar(o_cm[:, i, PROMPT:TOK], vg[:, PROMPT:TOK], w00[:, i:i + 1],
                                              b_mix[:, i, 0:1], ALU.mult, ALU.add))
                    low_w(u + 1, 0)
                    low_w(u + 1, 1)
                    take_turned(i)
                elif u <= U_OUT and u % 2 == 0:
                    i = (u - U_KV - 2) // 2
                    if u == U_OUT:
                        for k in range(HEADS):
                            low_x(HEADS + k, o_cm[:, k, :], gain_out[:, HEADS + k:HEADS + k + 1])
                    logits(i)
                    low_w(u + 1, 0)
                    low_w(u + 1, 1)
                    keep_head(i)
                    take_turned(HEADS + i)
                else:
                    if u > U_OUT + 1:
                        low_w(u + 1, 0)
                        low_w(u + 1, 1)
                if U_KV < u <= U_OUT + 1 and u % 2 == 1:
                    i = (u - U_KV - 1) // 2
                    if i:
                        exponents(i - 1)
                        mask_weights(i - 1)
                    if u > U_KV + 1:
                        low_w(u + 1, 0)
                        low_w(u + 1, 1)
                    if u < U_OUT:
                        if i:
                            dve.wait_ge(k_out, 16 * i)
                        normalise(2 * HEADS + i, k_head[:, :], y[:, t % 2, :], gain_k[:, 0:1])
                    if i:
                        take_attention(i - 1)
                if u == CM_ROOT:
                    invert(1, cm_r[:, :])
                if u == SB_ROOT:
                    invert(2, sb_r[:, :])
                    for k in range(HEADS):
                        low_x(k, q[:, k, :], gain_out[:, k:k + 1])
                if u in SUM_END:
                    keep_sample(SUM_END.index(u))
                for j in k_pages(u):
                    score_page(j)
                if u > U_OUT_SB:
                    for k in range(2 * (u - U_OUT_SB - 1), 2 * (u - U_OUT_SB)):
                        if k < 8:
                            low_x(8 + k, h[:, k, :], gain_ffn[:, k:k + 1])
                        add_square(KT + 3 * HEADS, k, h_sq[:, k % 2, :], h_sum[:, :])
                if u >= U_OUT:
                    out_tile(2 * (u - U_OUT), cm_r if u < U_OUT_SB else sb_r)

            out_tile(2 * KT - 1, sb_r)
            for k in range(8, KT):
                low_x(k - 8, h[:, k, :], gain_ffn[:, k:k + 1])
            for k in range(KT - 2, KT):
                add_square(KT + 3 * HEADS, k, h_sq[:, k % 2, :], h_sum[:, :])

            def take_loop(t, dst, it):
                dve.wait_ge(out_done, it * (2 * CHUNK_TILES) + (t + 1))
                dve.tensor_tensor(halves(dst), tile_ps(t), halves(h_r[:, :]), ALU.mult).then_inc(out_read, 1)

            def gate_up(u, n, t, par, g, it=0):
                n_it = it * (2 * FFN_GROUP)
                low_w(u + 1, 0, it)
                low_w(u + 1, 1, it)
                if u == U_FFN:
                    invert(3, h_r[:, :])
                else:
                    dve.wait_ge(act_lo_done, n_it + n)
                take_loop(t, y_gate[:, :], it)
                low_w(u + 2, 0, it)
                low_w(u + 2, 1, it)
                take_loop(t + 1, y_up[:, :], it)
                dve.wait_ge(out_read, it * (2 * CHUNK_TILES) + (t + 2))
                dve.wait_ge(silu_done, n_it + (n + 1))
                dve.tensor_tensor(y_up[:, :], y_up[:, :], y_gate[:, :], ALU.mult).then_inc(act_done, 1)
                dve.wait_ge(act_hi_done, n_it + (n + 1))
                dve.tensor_tensor(act_lo[:, par, g, :], y_up[:, :], act_hi[:, par, g, :], ALU.subtract)\
                    .then_inc(act_lo_done, 1)

            def down_tile(t, m, it=0):
                dve.wait_ge(out_done, it * (2 * CHUNK_TILES) + (t + 1))
                dve.wait_ge(out_read, it * (2 * CHUNK_TILES) + t)
                dve.tensor_tensor(halves(h[:, m, :]), halves(h[:, m, :]), tile_ps(t), ALU.add)\
                    .then_inc(out_read, 1)

            for g in range(FFN_GROUP):
                gate_up(U_FFN + 2 * g, g, T_FFN + 2 * g, 0, g)
            with dve.Fori(0, (FFN_CHUNKS - 1) // 2) as it:
                for half in range(2):
                    u0 = U_LOOP + half * CHUNK_UNITS
                    for g in range(FFN_GROUP):
                        gate_up(u0 + 2 * g, FFN_GROUP * (1 + half) + g, tiles_before(u0 + 2 * g), 1 - half, g, it)
                    for g in range(FFN_GROUP):
                        u = u0 + 2 * FFN_GROUP + g
                        for j in range(4):
                            if j < 2:
                                low_w(u + 1, j, it)
                            down_tile(tiles_before(u) + j, 4 * g + j, it)

            for k in range(2):
                n_split[0] += 1
                dve.wait_ge(x_hi_done, n_split[0])
                dve.tensor_tensor(x_lo[:, k, :], p_raw[:, k, :], x_hi[:, k, :], ALU.subtract)\
                    .then_inc(x_lo_done, 1)
            for g in range(FFN_GROUP):
                for j in range(4):
                    k = 4 * g + j
                    if j < 2:
                        low_w(U_LAST_DOWN + g + 1, j)
                    down_tile(T_LAST_DOWN + k, k)
                    if k >= 2:
                        low_x(k, h[:, k, :], gain_ple[:, k:k + 1])
                    add_square(2 * KT + 3 * HEADS, k, h_sq[:, k % 2, :], h_sum[:, :])
            for m in range(KT):
                if m % 8 < 2:
                    low_w(U_PROJ + 1 + m // 8, m % 8)
                dve.wait_ge(out_done, T_PROJ + m + 1)
                dve.tensor_copy(halves(proj[:, m, :]), tile_ps(T_PROJ + m)).then_inc(out_read, 1)
            for k in range(2):
                low_x(k, h[:, k, :], gain_ple[:, k:k + 1])
            invert(4, h_r[:, :])
            count[out_read.name] = T_GATE
            for m in range(KT):
                if U_GATE + m + 1 < UNITS:
                    low_w(U_GATE + m + 1, 0)
                    low_w(U_GATE + m + 1, 1)
                take(T_GATE + m, y_gate[:, :], h_r[:, :])
                dve.wait_ge(silu_done, FFN_GROUP * FFN_CHUNKS + m + 1)
                chained(dve.tensor_tensor(y_gate[:, :], y_gate[:, :], proj[:, m, :], ALU.mult))
                chained(dve.tensor_tensor(h[:, m, :], h[:, m, :], y_gate[:, :], ALU.add), h_final)

        @block.tensor
        def _(pe):
            def block_products(u, blk, t, hi, lo, first, last):
                cols = slice(blk * P, (blk + 1) * P)
                terms = ((w_hi, hi), (w_hi, lo), (w_lo, hi))
                for n, (w, x) in enumerate(terms):
                    for a in range(2):
                        mm = pe.matmul(out_ps[:, 2 * (t % 2) + a, 0:HALF], w[:, u % 2, cols],
                                       x[:, a * HALF:(a + 1) * HALF],
                                       start=first and n == 0, stop=last and n == len(terms) - 1)
                if last:
                    mm.then_inc(out_done, 1)

            def unit(u, blocks, tiles, operand, each=None, it=0, between=None):
                per = SLOTS // tiles
                for b in range(SLOTS):
                    if b % 8 == 0:
                        pe.wait_ge(lo_done, it * (4 * CHUNK_UNITS) + (2 * u + b // 8 + 1))
                    if b == 8 and between:
                        between()
                    t = tiles_before(u) + b // per
                    if b % per == 0 and t >= 2:
                        pe.wait_ge(out_read, it * (2 * CHUNK_TILES) + (t - 1))
                    if each:
                        each(b)
                    hi, lo = operand(b)
                    block_products(u, b, t, hi, lo, b % per == 0, b % per == per - 1)

            pair_free = [None]
            mix_free = [None]

            def wait_free(free, reader):
                if free[0]:
                    pe.wait_ge(*free[0])
                free[0] = reader

            def sum_features(n, x, ready, done, reader):
                pe.wait_ge(ready, done)
                wait_free(pair_free, reader)
                for a in range(2):
                    mm = pe.matmul(pair_ps[:, a, 0:HALF], ones[:, :], x[:, a * HALF:(a + 1) * HALF],
                                   start=True, stop=True)
                return mm

            def turn(n, src, u):
                pe.wait_ge(tok_read, reads_before("turn", u))
                for c in range(4):
                    mm = pe.transpose(tok_ps[:, c * P:(c + 1) * P], src[:, c * P:(c + 1) * P], ident[:, :])
                mm.then_inc(turned, 1)

            def mix(i):
                pe.wait_ge(tok_read, reads_before("turn", U_MLP + 2 + 2 * i) + 1)
                wait_free(mix_free, (mix_read, i + 1))
                for c in range(4):
                    mm = pe.matmul(mix_ps[:, c * P:(c + 1) * P], v_tok[:, c, :], w_mix[:, i, :],
                                   start=True, stop=True)
                mm.then_inc(mixed, 1)

            def scores(i):
                pe.wait_ge(norm_done, 2 * HEADS + i + 1)
                wait_free(pair_free, (pair_read, 2 * i + 2))
                wait_free(mix_free, (z_done, i + 1))
                for kb in range(4):
                    key = k_head[:, kb * P:(kb + 1) * P]
                    mm = pe.matmul(pair_flat[:, DIAG(kb)], key, q[:, i, kb * P:(kb + 1) * P],
                                   start=True, stop=True)
                for kb in range(3):
                    n = (3 - kb) * P
                    key = k_head[:, kb * P:(kb + 1) * P]
                    dst = mix_ps[:, 0:n] if kb == 1 else pair_flat[:, OFF[kb]:OFF[kb] + n]
                    mm = pe.matmul(dst, key, q[:, i, PROMPT - n:PROMPT], start=True, stop=True)
                mm.then_inc(z_ready, 1)

            def sum_later(i):
                pe.wait_ge(keep_done, i + 1)
                wait_free(pair_free, (pair_read, 2 * i + 3))
                wait_free(mix_free, (arg_done, i + 1))
                pe.matmul(pair_flat[:, 0:512], later[:, :], keep[:, 0:512], start=True, stop=True)
                pe.matmul(pair_flat[:, 512:1024], later[:, :], keep[:, 512:1024], start=True, stop=False,
                          skip_group_check=True)
                for col, src in ((512, keep[:, DIAG(1)]), (640, soft[:, P:2 * P]),
                                 (768, soft[:, 2 * P:3 * P]), (896, keep[:, DIAG(3)])):
                    pe.matmul(pair_flat[:, col:col + P], ones[:, :], src, start=False, stop=col == 896,
                              skip_group_check=True)
                pe.matmul(mix_ps[:, 0:256], later[:, :], keep[:, 1024:CELLS], start=True, stop=False,
                          skip_group_check=True)
                pe.matmul(mix_ps[:, 0:P], ones[:, :], keep[:, DIAG(2)], start=False, stop=False,
                          skip_group_check=True)
                pe.matmul(mix_ps[:, P:2 * P], ones[:, :], soft[:, 0:P], start=False, stop=True,
                          skip_group_check=True).then_inc(later_ready, 1)

            def attend(i, u):
                pe.wait_ge(masked, i + 1)
                pe.wait_ge(tok_read, reads_before("av", u))
                for kb in range(4):
                    pe.matmul(tok_ps[:, DIAG(kb)], v_tok[:, kb, :], z[:, DIAG(kb)], start=kb == 0,
                              stop=False, skip_group_check=True)
                for kb in range(3):
                    n = (3 - kb) * P
                    mm = pe.matmul(tok_ps[:, PROMPT - n:PROMPT], v_tok[:, kb, :], z[:, OFF[kb]:OFF[kb] + n],
                                   start=False, stop=kb == 2, skip_group_check=True)
                mm.then_inc(av_ready, 1)

            def reduce_sample(b, u):
                pe.wait_ge(v_used, PAGES * (b + 1))
                pe.wait_ge(tok_read, reads_before("reduce", u))
                for hd in range(HEADS):
                    mm = pe.matmul(tok_ps[:, P + hd:P + hd + 1], acc[:, hd * P:(hd + 1) * P], ones[:, 0:1],
                                   start=True, stop=True)
                mm.then_inc(o_s_ready, 1)

            def sum_later_sample(b, u):
                pe.wait_ge(keep_s_done, b + 1)
                pe.wait_ge(tok_read, reads_before("later", u) - (u in REDUCE_END))
                n = (PAGES - 1) * HEADS
                pe.matmul(tok_ps[:, 0:PAGES * HEADS], later[:, :], keep_s[:, :], start=True, stop=False,
                          skip_group_check=True)
                pe.matmul(tok_ps[:, 0:n], ones[:, :], soft_s[:, 0:n], start=False, stop=True,
                          skip_group_check=True).then_inc(later_s_ready, 1)

            def in_operand(b):
                return x_hi[:, b, :], x_lo[:, b, :]

            pe.wait_ge(built, 1)
            unit(0, None, 1, in_operand, each=lambda b: pe.wait_ge(x_lo_done, b + 1))
            sum_features(0, x_r, sum_done, KT, (root_done, 1)).then_inc(x_sum_ready, 1)

            for u in range(1, U_FFN):
                def between():
                    if u <= U_MLP:
                        n = u - 1
                        sum_features(n, sq, sq_done, KT + n + 1, (ln_done, n + 1)).then_inc(ms_ready, 1)
                    elif u < U_KV and u % 2 == 1:
                        i = (u - U_MLP - 1) // 2
                        sum_features(i, vg, gelu_done, 2 * i + 1, (centred, i + 1)).then_inc(mean_ready, 1)
                    elif u <= U_KV:
                        i = (u - U_MLP - 2) // 2
                        pe.wait_ge(norm_done, HEADS + i + 1)
                        turn(i, vg, u)
                    elif u <= U_OUT + 1 and u % 2 == 1:
                        i = (u - U_KV - 1) // 2
                        if u < U_OUT:
                            n = 2 * HEADS + i
                            sum_features(n, sq, sq_done, KT + n + 1, (ln_done, n + 1)).then_inc(ms_ready, 1)
                        if i:
                            attend(i - 1, u)
                    elif u <= U_OUT:
                        i = (u - U_KV - 2) // 2
                        pe.wait_ge(out_read, u)
                        turn(HEADS + i, y[:, 1, :], u)
                        if u == CM_ROOT:
                            sum_features(1, cm_r, cm_sum_done, 1, (root_done, 2)).then_inc(x_sum_ready, 1)

                if u < U_OUT:
                    unit(u, None, 1, in_operand, between=between)
                else:
                    slot0 = HEADS if u < U_OUT_SB else 0
                    n0 = KT if u < U_OUT_SB else KT + HEADS
                    unit(u, None, 2, lambda b: in_operand(slot0 + b % 8), between=between,
                         each=(lambda b: pe.wait_ge(x_lo_done, n0 + b % 8 + 1))
                         if u in (U_OUT, U_OUT_SB) else None)
                if u == U_MLP:
                    pe.wait_ge(norm_done, HEADS)
                    wait_free(pair_free, (pair_read, 1))
                    for hd in range(HEADS):
                        mm = pe.transpose(pair_flat[0:SAMPLES, hd * P:(hd + 1) * P], q[:, hd, PROMPT:TOK],
                                          ident[:, :])
                    mm.then_inc(q_rows_ready, 1)
                elif U_MLP < u < U_KV and u % 2 == 1:
                    n = HEADS + (u - U_MLP - 1) // 2
                    sum_features(n, sq, sq_done, KT + n + 1, (ln_done, n + 1)).then_inc(ms_ready, 1)
                elif U_MLP < u <= U_KV:
                    mix((u - U_MLP - 2) // 2)
                elif U_KV < u < U_OUT and u % 2 == 1:
                    scores((u - U_KV - 1) // 2)
                elif U_KV < u <= U_OUT:
                    sum_later((u - U_KV - 2) // 2)
                if u in REDUCE_END:
                    reduce_sample(REDUCE_END.index(u), u)
                if u in SUM_END:
                    sum_later_sample(SUM_END.index(u), u)
                if u == SB_ROOT - 1:
                    sum_features(2, sb_r, sb_sum_done, 1, (root_done, 3)).then_inc(x_sum_ready, 1)

            def ffn_operand(b):
                return in_operand((b + 8) % KT)

            for u in range(U_FFN, U_LOOP):
                unit(u, None, 1, ffn_operand,
                     each=(lambda b: pe.wait_ge(x_lo_done, 2 * KT + b + 1)) if u == U_FFN else None)
                if u == U_FFN:
                    sum_features(3, h_sum, sum_done, 2 * KT, (root_done, 4)).then_inc(x_sum_ready, 1)

            def down_unit(u, par, it=0):
                unit(u, None, 4, lambda b: (act_hi[:, par, b % 4, :], act_lo[:, par, b % 4, :]), it=it)

            with pe.Fori(0, (FFN_CHUNKS - 1) // 2) as it:
                for half in range(2):
                    u0 = U_LOOP + half * CHUNK_UNITS
                    for x in range(2 * FFN_GROUP):
                        unit(u0 + x, None, 1, ffn_operand, it=it)
                    pe.wait_ge(act_lo_done, it * (2 * FFN_GROUP) + FFN_GROUP * (1 + half))
                    for g in range(FFN_GROUP):
                        down_unit(u0 + 2 * FFN_GROUP + g, half, it)
            pe.wait_ge(act_lo_done, FFN_GROUP * FFN_CHUNKS)
            for g in range(FFN_GROUP):
                down_unit(U_LAST_DOWN + g, (FFN_CHUNKS - 1) % 2)

            pe.wait_ge(x_lo_done, 3 * KT + 2)
            for s in range(2):
                unit(U_PROJ + s, None, 8, lambda b: in_operand(b % 2))
            sum_features(4, h_sum, sum_done, 3 * KT, (root_done, 5)).then_inc(x_sum_ready, 1)
            for m in range(KT):
                unit(U_GATE + m, None, 1, lambda b: in_operand((b + 2) % KT),
                     each=(lambda b: pe.wait_ge(x_lo_done, 3 * KT + 2 + b + 1)) if m == 0 else None)


def kernel(x_prompt, x_sample, cache_k, cache_v, page_table, p_prompt, p_sample, g_mix, w_in, g_q, g_k,
           sb_bias, sgu_ln_g, sgu_ln_b, w_s, b_s, g_out_sb, g_out_cm, w_out, g_ffn, w_gate, w_up, w_down,
           g_ple, w_ple_gate, w_ple_proj):
    import numpy as np
    import concourse.bacc as bacc
    from concourse.bass_utils import run_bass_kernel_spmd as run

    a = lambda x: np.asarray(x)

    def feature_major(prompt, sample):
        x = np.concatenate([a(prompt).reshape(PROMPT, -1), a(sample).reshape(SAMPLES, -1)])
        return x.T.reshape(-1, P, TOK).transpose(1, 0, 2)

    def by_partition(g):
        return a(g).reshape(-1, P).T

    def by_tile(w):
        return w.reshape(w.shape[0] // P, P, w.shape[1] // P, P).transpose(2, 1, 0, 3)

    tile_order = list(range(HEADS))
    tile_order += [x for i in range(HEADS) for x in (4 * HEADS + i, 3 * HEADS + i)]
    tile_order += [x for i in range(HEADS) for x in (HEADS + i, 2 * HEADS + i)]
    w_in_u = by_tile(a(w_in)[0])[tile_order].reshape(-1, P, SLOTS * P)
    w_out_u = a(w_out)[0].reshape(2, 8, P, 8, 2, P).transpose(0, 3, 2, 4, 1, 5)[::-1]
    w_out_u = w_out_u.reshape(-1, P, SLOTS * P)
    gate_up = np.stack([by_tile(a(w_gate)[0]), by_tile(a(w_up)[0])], axis=1)
    gate_up = gate_up.reshape(FFN_CHUNKS, 2 * FFN_GROUP, P, SLOTS * P)
    down = a(w_down)[0].reshape(FFN_CHUNKS, FFN_GROUP, P, 4, 4, P).transpose(0, 3, 2, 4, 1, 5)
    down = down.reshape(FFN_CHUNKS, FFN_GROUP, P, SLOTS * P)
    ffn = [gate_up[0]]
    for c in range(1, FFN_CHUNKS):
        ffn += [gate_up[c], down[c - 1]]
    ffn.append(down[-1])
    proj_u = a(w_ple_proj)[0].reshape(2, P, 2, 8, P).transpose(2, 1, 3, 0, 4).reshape(2, P, SLOTS * P)
    gate_t = by_tile(a(w_ple_gate)[0])
    gate_u = np.concatenate([gate_t[:, :, 2:], gate_t[:, :, :2]], axis=2).reshape(-1, P, SLOTS * P)
    arrays = {
        "w_units": np.concatenate([w_in_u, w_out_u, *ffn, proj_u, gate_u]),
        "x_t": feature_major(x_prompt, x_sample),
        "p_t": feature_major(p_prompt, p_sample),
        "cache_k": a(cache_k).reshape(N_PHYS, P, HEADS * P),
        "cache_v": a(cache_v).reshape(N_PHYS, P, HEADS * P),
        "page_table": a(page_table).reshape(1, N_PAGES),
        "g_mix": by_partition(g_mix),
        "g_out": np.concatenate([by_partition(g_out_sb), by_partition(g_out_cm)], axis=1),
        "g_ffn": by_partition(g_ffn),
        "g_ple": by_partition(g_ple),
        "g_q": a(g_q).reshape(P, 1),
        "g_k": a(g_k).reshape(P, 1),
        "ln_g": by_partition(sgu_ln_g),
        "ln_b": by_partition(sgu_ln_b),
        "w_s_t": a(w_s)[0].transpose(2, 0, 1),
        "b_s": a(b_s).reshape(1, HEADS, P),
        "sb_bias": a(sb_bias).reshape(1, HEADS),
        "w_s00": a(w_s)[0, :, 0, 0].reshape(1, HEADS),
    }
    arrays = {k: np.ascontiguousarray(v) for k, v in arrays.items()}
    outs = {"y_t": (P, KT, TOK), "k_t": (HEADS, P, TOK), "v_t": (HEADS, P, TOK),
            "chunk_v_t": (P, HEADS, SAMPLES)}
    nc = bacc.Bacc("TRN2", target_bir_lowering=False, num_devices=1)
    aps = {k: nc.dram_tensor(k, v.shape, mybir.dt.from_np(v.dtype), kind="ExternalInput").ap()
           for k, v in arrays.items()}
    aps |= {k: nc.dram_tensor(k, s, F32, kind="ExternalOutput").ap() for k, s in outs.items()}
    build(nc, **aps)
    got = run(nc, [arrays], core_ids=[0]).results[0]

    y = got["y_t"].transpose(2, 1, 0).reshape(TOK, D_MODEL)
    k = got["k_t"].transpose(2, 0, 1)
    v = got["v_t"].transpose(2, 0, 1)
    chunk = got["chunk_v_t"].transpose(2, 1, 0)
    new = (SAMPLES, 1, HEADS, P)
    return tuple(np.ascontiguousarray(x) for x in (
        y[:PROMPT].reshape(1, PROMPT, D_MODEL), y[PROMPT:].reshape(SAMPLES, 1, D_MODEL),
        k[:PROMPT].reshape(1, 1, PROMPT, HEADS, P), v[:PROMPT].reshape(1, 1, PROMPT, HEADS, P),
        k[PROMPT:].reshape(1, *new), v[PROMPT:].reshape(1, *new), chunk.reshape(1, *new)))
```

```python
from contextlib import ExitStack

import concourse.bass as bass
from concourse import mybir

F32 = mybir.dt.float32
F32R = mybir.dt.float32r
I32 = mybir.dt.int32
ALU = mybir.AluOpType
ACT = mybir.ActivationFunctionType

P = 128
D_MODEL = 2048
PROMPT = 512
SAMPLES = 8
TOK = PROMPT + SAMPLES
HALF = TOK // 2
HEADS = 8
PAGES = 8
N_PHYS = 80
D_FF = 5632
EPS = 1e-6
SCALE = float(P) ** -0.5

KT = D_MODEL // P
SLOTS = 16
FFN_GROUP = 4
FFN_CHUNKS = D_FF // P // FFN_GROUP

U_MLP = HEADS
U_KV = U_MLP + 2 * HEADS
U_OUT = U_KV + 2 * HEADS
U_OUT_SB = U_OUT + 8
U_FFN = U_OUT_SB + 8
U_LOOP = U_FFN + 2 * FFN_GROUP
CHUNK_UNITS = 3 * FFN_GROUP
U_LAST_DOWN = U_LOOP + CHUNK_UNITS * (FFN_CHUNKS - 1)
U_PROJ = U_LAST_DOWN + FFN_GROUP
U_GATE = U_PROJ + 2
UNITS = U_GATE + KT

T_OUT = U_OUT
T_OUT_SB = T_OUT + KT
T_FFN = T_OUT_SB + KT
T_LOOP = T_FFN + 2 * FFN_GROUP
CHUNK_TILES = 2 * FFN_GROUP + KT
T_LAST_DOWN = T_LOOP + CHUNK_TILES * (FFN_CHUNKS - 1)
T_PROJ = T_LAST_DOWN + KT
T_GATE = T_PROJ + KT



def tiles_before(u):
    if u <= U_OUT:
        return u
    if u <= U_FFN:
        return T_OUT + 2 * (u - U_OUT)
    if u <= U_LOOP:
        return T_FFN + u - U_FFN
    if u <= U_LAST_DOWN:
        c, x = divmod(u - U_LOOP, CHUNK_UNITS)
        return T_LOOP + CHUNK_TILES * c + min(x, 2 * FFN_GROUP) + 4 * max(x - 2 * FFN_GROUP, 0)
    if u <= U_PROJ:
        return T_LAST_DOWN + 4 * (u - U_LAST_DOWN)
    if u <= U_GATE:
        return T_PROJ + 8 * (u - U_PROJ)
    return T_GATE + u - U_GATE


X_PIECES = [0, 2, 4, 8, 12, 16]
POOL_SQUARES = 6
X_SQUARES = KT - POOL_SQUARES
POOL_LO = 2

CONSTS = 11
RING = 2
CM_ROOT = U_OUT - 2
SB_ROOT = U_OUT + 4
K_PERIOD = 10
K_PER = 3
N_PAGES = SAMPLES * PAGES
LAST_K = [K_PERIOD + (PAGES * b + PAGES - 1) // K_PER for b in range(SAMPLES)]
SUM_END = [p + 1 + (p + 1) % 2 for p in LAST_K]
REDUCE_END = [18, 22, 25, 28, 31, 34, 37, 40]

DIAG = lambda kb: slice(kb * P, (kb + 1) * P)
OFF = {0: 512, 1: 1024, 2: 896}
CELLS = 1280


def k_pages(period):
    if period < K_PERIOD:
        return range(0)
    first = K_PER * (period - K_PERIOD)
    return range(min(first, N_PAGES), min(first + K_PER, N_PAGES))


def build(nc, w_units, x_t, p_t, cache_k, cache_v, page_table, g_mix, g_out, g_ffn, g_ple, g_q, g_k,
          ln_g, ln_b, w_s_t, b_s, sb_bias, w_s00, y_t, k_t, v_t, chunk_v_t):
    q_rows_dram = nc.dram_tensor("q_rows_dram", (SAMPLES, HEADS * P), F32, kind="Internal").ap()

    with ExitStack() as ctx:
        def sb(name, shape, dt=F32, where=ctx):
            return where.enter_context(nc.sbuf_tensor(name, shape, dt))

        def sem(name):
            return ctx.enter_context(nc.semaphore(name))

        x_hi = sb("x_hi", [P, KT, TOK], F32R)
        x_lo = sb("x_lo", [P, KT, TOK], F32R)
        w_raw = sb("w_raw", [P, 2, SLOTS * P])
        w_hi = sb("w_hi", [P, 2, SLOTS * P], F32R)
        w_lo = sb("w_lo", [P, 2, SLOTS * P], F32R)

        with ExitStack() as early:
            k_ring = sb("k_ring", [P, RING, HEADS * P], where=early)
            q_rows = sb("q_rows", [P, HEADS * P], where=early)
            dot_s = sb("dot_s", [P, PAGES * HEADS], where=early)
            acc = sb("acc", [P, HEADS * P], where=early)
            v_ring = sb("v_ring", [P, RING, HEADS * P], where=early)
            sb("pad", [P, 32], where=early)
            keep = sb("keep", [P, CELLS], where=early)
            pool_sq = sb("pool_sq", [P, TOK], where=early)
            z_s = sb("z_s", [P, PAGES * HEADS], where=early)
            soft_s = sb("soft_s", [P, PAGES * HEADS], where=early)
            keep_s = sb("keep_s", [P, PAGES * HEADS], where=early)
            chunk_v = sb("chunk_v", [P, HEADS, SAMPLES], where=early)
        h = sb("h", [P, KT, TOK])
        H_KEYS, H_PAGES = 6, 12

        with ExitStack() as first:
            x_sq = sb("x_sq", [P, KT, TOK], where=first)
        with ExitStack() as early:
            q = sb("q", [P, HEADS, TOK], where=early)
            o_cm = sb("o_cm", [P, HEADS, TOK], where=early)
        with ExitStack() as late:
            proj = sb("proj", [P, KT, TOK], where=late)
        act_hi = sb("act_hi", [P, 2, FFN_GROUP, TOK], F32R)
        act_lo = sb("act_lo", [P, 2, FFN_GROUP, TOK], F32R)

        ones = sb("ones", [P, P])
        later = sb("later", [P, P])
        causal = sb("causal", [P, P])
        ident = sb("ident", [P, P])
        eps = sb("eps", [P, 1])
        one = sb("one", [P, 1])
        gain_mix = sb("gain_mix", [P, KT])
        gain_out = sb("gain_out", [P, KT])
        gain_ffn = sb("gain_ffn", [P, KT])
        gain_ple = sb("gain_ple", [P, KT])
        gain_q = sb("gain_q", [P, 1])
        gain_k = sb("gain_k", [P, 1])
        lng = sb("lng", [P, HEADS])
        lnb = sb("lnb", [P, HEADS])
        bias = sb("bias", [P, HEADS])
        w00 = sb("w00", [P, HEADS])
        table = sb("table", [1, N_PAGES], I32)
        dot_pad = sb("dot_pad", [P, 1])
        a_s = sb("a_s", [P, 3, PAGES * HEADS])
        x_r = sb("x_r", [P, TOK])
        sq = sb("sq", [P, TOK])
        cm_r = sb("cm_r", [P, TOK])
        sb_r = sb("sb_r", [P, TOK])

        with ExitStack() as early:
            y = sb("y", [P, 2, TOK], where=early)
            v_tok = sb("v_tok", [P, 4, P], where=early)
            with ExitStack() as mlp:
                vg = sb("vg", [P, TOK], where=mlp)
                ug = sb("ug", [P, TOK], where=mlp)
                w_mix = sb("w_mix", [P, HEADS, P], where=mlp)
                b_mix = sb("b_mix", [P, HEADS, P], where=mlp)
            k_head = sb("k_head", [P, TOK], where=early)
            z = sb("z", [P, CELLS], where=early)
            soft = sb("soft", [P, CELLS], where=early)
        y_gate = sb("y_gate", [P, TOK])
        y_up = sb("y_up", [P, TOK])
        h_sq = sb("h_sq", [P, 2, TOK])
        h_sum = sb("h_sum", [P, TOK])
        h_r = sb("h_r", [P, TOK])
        p_raw = sb("p_raw", [P, 2, TOK])

        out_ps = ctx.enter_context(nc.psum_tensor("out_ps", [P, 4, 512], F32))
        pair_ps = ctx.enter_context(nc.psum_tensor("pair_ps", [P, 2, 512], F32))
        tok_ps = ctx.enter_context(nc.psum_tensor("tok_ps", [P, 512], F32))
        mix_ps = ctx.enter_context(nc.psum_tensor("mix_ps", [P, 512], F32))

        def tile_ps(t):
            return out_ps[:, 2 * (t % 2):2 * (t % 2) + 2, 0:HALF]

        def halves(x):
            return x.rearrange("p (a n) -> p a n", a=2)

        pair = pair_ps[:, :, 0:HALF]
        pair_flat = pair_ps[:, :, :].rearrange("p a n -> p (a n)")

        x_in = [sem(f"x_in{i}") for i in range(len(X_PIECES) - 1)]
        w_in = [sem(f"w_in{i}") for i in range(2)]
        w_in_first = sem("w_in_first")
        gain_in = sem("gain_in")
        consts_in = sem("consts_in")
        table_in = sem("table_in")
        k_in = [sem(f"k_in{i}") for i in range(RING)]
        v_in = [sem(f"v_in{i}") for i in range(RING)]
        q_rows_out = sem("q_rows_out")
        q_rows_in = sem("q_rows_in")
        h_in = [sem(f"h_in{i}") for i in range(3)]
        p_in = sem("p_in")
        k_out = sem("k_out")
        v_out = sem("v_out")
        y_out = sem("y_out")
        chunk_out = sem("chunk_out")
        hi_done = sem("hi_done")
        x_hi_done = sem("x_hi_done")
        sq_done = sem("sq_done")
        gelu_done = sem("gelu_done")
        ln_done = sem("ln_done")
        rstd_done = sem("rstd_done")
        root_done = sem("root_done")
        soft_done = sem("soft_done")
        soft_s_done = sem("soft_s_done")
        a_done = sem("a_done")
        a_s_done = sem("a_s_done")
        act_step = sem("act_step")
        silu_done = sem("silu_done")
        act_hi_done = sem("act_hi_done")
        lo_done = sem("lo_done")
        x_lo_done = sem("x_lo_done")
        sum_done = sem("sum_done")
        out_read = sem("out_read")
        norm_done = sem("norm_done")
        centred = sem("centred")
        tok_read = sem("tok_read")
        mix_read = sem("mix_read")
        pair_read = sem("pair_read")
        r_done = sem("r_done")
        cm_done = sem("cm_done")
        k_used = sem("k_used")
        z_done = sem("z_done")
        z_s_done = sem("z_s_done")
        keep_done = sem("keep_done")
        keep_s_done = sem("keep_s_done")
        arg_done = sem("arg_done")
        arg_s_done = sem("arg_s_done")
        masked = sem("masked")
        vec_step = sem("vec_step")
        act_done = sem("act_done")
        act_lo_done = sem("act_lo_done")
        h_final = sem("h_final")
        built = sem("built")
        pool_lo_done = sem("pool_lo_done")
        pool_sum_done = sem("pool_sum_done")
        pool_step = sem("pool_step")
        v_used = sem("v_used")
        cm_sum_done = sem("cm_sum_done")
        sb_sum_done = sem("sb_sum_done")
        out_done = sem("out_done")
        x_sum_ready = sem("x_sum_ready")
        ms_ready = sem("ms_ready")
        mean_ready = sem("mean_ready")
        q_rows_ready = sem("q_rows_ready")
        turned = sem("turned")
        mixed = sem("mixed")
        z_ready = sem("z_ready")
        later_ready = sem("later_ready")
        later_s_ready = sem("later_s_ready")
        av_ready = sem("av_ready")
        o_s_ready = sem("o_s_ready")

        tok_jobs = []
        for u in range(U_OUT + 2):
            if U_MLP + 2 <= u <= U_KV and u % 2 == 0 or U_KV + 2 <= u <= U_OUT and u % 2 == 0:
                tok_jobs.append(("turn", u))
            if U_KV + 3 <= u <= U_OUT + 1 and u % 2 == 1:
                tok_jobs.append(("av", u))
            if u in REDUCE_END:
                tok_jobs.append(("reduce", u))
            if u in SUM_END:
                tok_jobs.append(("later", u))

        def reads_before(kind, u):
            return tok_jobs.index((kind, u))

        block = ctx.enter_context(nc.Block())

        @block.sync
        def _(sp):
            def load_unit(u):
                if u in (2, 3):
                    sp.wait_ge(lo_done, u - 1)
                    sp.wait_ge(pool_lo_done, u - 1)
                elif u > 3:
                    sp.wait_ge(lo_done, 2 * u - 2 - POOL_LO)
                sp.dma_start(w_raw[:, u % 2, :], w_units[u]).then_inc(w_in[u % 2], 16)

            def load_x(i):
                tiles = slice(X_PIECES[i], X_PIECES[i + 1])
                sp.dma_start(h[:, tiles, :], x_t[:, tiles, :]).then_inc(x_in[i], 16)

            def load_k(j):
                b, pg = divmod(j, PAGES)
                if pg == 0:
                    if b:
                        sp.wait_ge(k_used, HEADS * j)
                    sp.dma_start(q_rows[:, :], q_rows_dram[b:b + 1, :].to_broadcast([P, HEADS * P]))\
                        .then_inc(q_rows_in, 16)
                page = sp.value_load(table[0:1, j:j + 1], min_val=0, max_val=N_PHYS - 1)
                if j >= RING:
                    sp.wait_ge(k_used, HEADS * (j - RING + 1))
                sp.dma_start(k_ring[:, j % RING, :],
                             cache_k[bass.ds(page, 1), :, :].rearrange("a p n -> (a p) n"))\
                    .then_inc(k_in[j % RING], 16)

            load_x(0)
            half = SLOTS * P // 2
            sp.dma_start(w_raw[:, 0, 0:half], w_units[0, :, 0:half]).then_inc(w_in_first, 16)
            load_x(1)
            sp.dma_start(w_raw[:, 0, half:], w_units[0, :, half:]).then_inc(w_in[0], 16)
            for i in range(2, len(X_PIECES) - 1):
                load_x(i)
            load_unit(1)
            sp.dma_start(table[:, :], page_table).then_inc(table_in, 16)
            for dst, src in ((gain_out[:, :], g_out), (gain_ffn[:, :], g_ffn),
                             (gain_ple[:, :], g_ple), (gain_q[:, :], g_q), (gain_k[:, :], g_k),
                             (lng[:, :], ln_g), (lnb[:, :], ln_b), (w_mix[:, :, :], w_s_t),
                             (b_mix[:, :, :], b_s.to_broadcast([P, HEADS, P])),
                             (bias[:, :], sb_bias.to_broadcast([P, HEADS])),
                             (w00[:, :], w_s00.to_broadcast([P, HEADS]))):
                sp.dma_start(dst, src).then_inc(consts_in, 16)
            sp.wait_ge(table_in, 16)
            next_k = 0
            for u in range(U_FFN):
                load_unit(u + 2)
                if u == K_PERIOD - 1:
                    sp.wait_ge(pair_read, 1)
                    sp.dma_start(q_rows_dram, acc[0:SAMPLES, :]).then_inc(q_rows_out, 16)
                    sp.wait_ge(q_rows_out, 16)
                while u >= K_PERIOD - 1 and next_k < min(N_PAGES, K_PER * (u + 1 - K_PERIOD) + RING):
                    load_k(next_k)
                    next_k += 1
                if U_KV + 2 <= u <= U_OUT and u % 2 == 0:
                    i = (u - U_KV - 2) // 2
                    sp.wait_ge(norm_done, 2 * HEADS + i + 1)
                    sp.dma_start(k_t[i], k_head[:, :]).then_inc(k_out, 16)
                    sp.wait_ge(out_read, U_KV + 2 * i + 2)
                    sp.dma_start(v_t[i], y[:, 1, :]).then_inc(v_out, 16)
                if u == U_KV + 2:
                    sp.wait_ge(cm_done, HEADS)
                    sp.dma_start(chunk_v_t, chunk_v[:, :, :]).then_inc(chunk_out, 16)
                if u == LAST_K[-1] + 3:
                    sp.wait_ge(z_s_done, SAMPLES)
                    sp.dma_start(h[:, 0:H_KEYS, :], x_t[:, 0:H_KEYS, :]).then_inc(h_in[0], 16)
                if u == REDUCE_END[-1] + 2:
                    sp.wait_ge(tok_read, reads_before("reduce", REDUCE_END[-1]) + 1)
                    sp.dma_start(h[:, H_KEYS:H_PAGES, :], x_t[:, H_KEYS:H_PAGES, :]).then_inc(h_in[1], 16)
                if u == U_OUT + 3:
                    sp.wait_ge(av_ready, HEADS)
                    sp.wait_ge(sb_sum_done, 1)
                    sp.dma_start(h[:, H_PAGES:KT, :], x_t[:, H_PAGES:KT, :]).then_inc(h_in[2], 16)
                if u == U_OUT_SB:
                    sp.dma_start(p_raw[:, :, :], p_t).then_inc(p_in, 16)
            with sp.Fori((U_FFN + 2) // 2, UNITS // 2) as i:
                for s in range(2):
                    sp.wait_ge(lo_done, 4 * i + (2 * s - 2 - POOL_LO))
                    sp.dma_start(w_raw[:, s, :], w_units[bass.ds(2 * i + s, 1), :, :]
                                 .rearrange("a p n -> (a p) n")).then_inc(w_in[s], 16)
            for m in range(KT):
                sp.wait_ge(h_final, KT + m + 1)
                sp.dma_start(y_t[:, m, :], h[:, m, :]).then_inc(y_out, 16)
            sp.wait_ge(y_out, 16 * KT)
            sp.wait_ge(k_out, 16 * HEADS)
            sp.wait_ge(v_out, 16 * HEADS)
            sp.wait_ge(chunk_out, 16)

        @block.gpsimd
        def _(pool):
            steps = [0]

            def chained(ins):
                steps[0] += 1
                ins.then_inc(pool_step, 1)
                pool.wait_ge(pool_step, steps[0])

            chained(pool.memset(ones[:, :], 1.0))
            chained(pool.memset(eps[:, :], EPS))
            chained(pool.memset(one[:, :], 1.0))
            chained(pool.memset(cm_r[:, :], 0.0))
            chained(pool.memset(sb_r[:, :], 0.0))
            chained(pool.affine_select(out=later[:, :], in_=ones[:, :], compare_op=ALU.is_gt, fill=0.0,
                                       base=0, pattern=[[-1, P]], channel_multiplier=1))
            chained(pool.affine_select(out=causal[:, :], in_=ones[:, :], compare_op=ALU.is_gt, fill=0.0,
                                       base=0, pattern=[[1, P]], channel_multiplier=-1))
            chained(pool.affine_select(out=ident[:, :], in_=ones[:, :], compare_op=ALU.is_equal,
                                       fill=0.0, base=0, pattern=[[-1, P]], channel_multiplier=1))
            pool.memset(one[:, :], 1.0).then_inc(built, 1)

            def low_w(u, j):
                pool.wait_ge(hi_done, 2 * u + j + 1)
                cols = slice(j * 8 * P, (j + 1) * 8 * P)
                pool.tensor_tensor(w_lo[:, u, cols], w_raw[:, u, cols], w_hi[:, u, cols], ALU.subtract)\
                    .then_inc(pool_lo_done, 1)

            def square_input(k):
                ins = pool.tensor_tensor(x_sq[:, k, :], h[:, k, :], h[:, k, :], ALU.mult)
                chained(ins)
                if k:
                    ins = pool.tensor_tensor(x_sq[:, 0, :], x_sq[:, 0, :], x_sq[:, k, :], ALU.add)
                    if k == POOL_SQUARES - 1:
                        ins.then_inc(pool_sum_done, 1)
                    else:
                        chained(ins)

            pool.wait_ge(x_in[0], 16)
            square_input(0)
            low_w(0, 1)
            pool.wait_ge(x_in[1], 16)
            square_input(1)
            square_input(2)
            square_input(3)
            pool.wait_ge(x_in[2], 16)
            square_input(4)
            low_w(1, 1)
            square_input(5)
            pool.wait_ge(consts_in, CONSTS * 16)
            pool.affine_select(out=w_mix[:, :, :], in_=w_mix[:, :, :], compare_op=ALU.is_ge, fill=0.0,
                               base=0, pattern=[[0, HEADS], [1, P]], channel_multiplier=-1)\
                .then_inc(built, 1)

            def load_v(j):
                page = pool.value_load(table[0:1, j:j + 1], min_val=0, max_val=N_PHYS - 1)
                if j >= RING:
                    pool.wait_ge(v_used, j - RING + 1)
                pool.dma_start(v_ring[:, j % RING, :],
                               cache_v[bass.ds(page, 1), :, :].rearrange("a p n -> (a p) n"))\
                    .then_inc(v_in[j % RING], 16)

            def add_page(j):
                b, pg = divmod(j, PAGES)
                pool.wait_ge(v_in[j % RING], 16 * (j // RING + 1))
                values = v_ring[:, j % RING, :].rearrange("p (h d) -> p h d", h=HEADS)
                weights = a_s[:, b % 3, pg * HEADS:(pg + 1) * HEADS].unsqueeze(2).to_broadcast([P, HEADS, P])
                if pg == 0:
                    if b == 0:
                        pool.wait_ge(q_rows_out, 16)
                    else:
                        pool.wait_ge(o_s_ready, b)
                    pool.wait_ge(a_s_done, b + 1)
                    pool.tensor_tensor(acc[:, :].rearrange("p (h d) -> p h d", h=HEADS), values, weights,
                                       ALU.mult).then_inc(v_used, 1)
                else:
                    chained(pool.tensor_tensor(values, values, weights, ALU.mult))
                    pool.wait_ge(v_used, j)
                    pool.tensor_tensor(acc[:, :], acc[:, :], v_ring[:, j % RING, :], ALU.add)\
                        .then_inc(v_used, 1)
                if j + RING < N_PAGES:
                    load_v(j + RING)

            def add_squares(x, total, cols, done=pool_step):
                chained(pool.tensor_tensor(pool_sq[:, cols], x, x, ALU.mult))
                ins = pool.tensor_tensor(total[:, cols], total[:, cols], pool_sq[:, cols], ALU.add)
                if done is pool_step:
                    chained(ins)
                else:
                    ins.then_inc(done, 1)
                    pool.wait_ge(done, 1)

            jobs = [(SUM_END[j // PAGES] + 1 + j % PAGES * 0.25, "page", j) for j in range(N_PAGES)]
            jobs += [(U_MLP + 3.5 + 2 * i, "mlp", i) for i in range(HEADS)]
            jobs += [(U_KV + 3.7 + 2 * i, "attention", i) for i in range(HEADS)]
            pool.wait_ge(table_in, 16)
            pool.wait_ge(x_lo_done, KT)
            pool.wait_ge(sq_done, X_SQUARES)
            for j in range(RING):
                load_v(j)
            for _, kind, i in sorted(jobs):
                if kind == "page":
                    add_page(i)
                elif kind == "mlp":
                    pool.wait_ge(cm_done, i + 1)
                    add_squares(o_cm[:, i, :], cm_r, slice(0, TOK), cm_sum_done if i == HEADS - 1 else pool_step)
                else:
                    pool.wait_ge(tok_read, reads_before("av", U_KV + 3 + 2 * i) + 1)
                    add_squares(q[:, i, 0:PROMPT], sb_r, slice(0, PROMPT))
            pool.wait_ge(tok_read, reads_before("reduce", REDUCE_END[-1]) + 1)
            for i in range(HEADS):
                add_squares(q[:, i, PROMPT:TOK], sb_r, slice(PROMPT, TOK),
                            sb_sum_done if i == HEADS - 1 else pool_step)

        @block.scalar
        def _(act):
            act.dma_start(gain_mix[:, :], g_mix).then_inc(gain_in, 16)

            steps = [0]

            def chained(ins):
                steps[0] += 1
                ins.then_inc(act_step, 1)
                act.wait_ge(act_step, steps[0])

            def high_w(u, j):
                cols = slice(j * 8 * P, (j + 1) * 8 * P)
                act.activation(w_hi[:, u % 2, cols], w_raw[:, u % 2, cols], ACT.Copy).then_inc(hi_done, 1)

            def split_w(u, it=0, landed=0, tiles=0):
                act.wait_ge(w_in[u % 2], it * landed + 16 * (u // 2 + 1))
                if u >= 2:
                    act.wait_ge(out_done, it * tiles + tiles_before(u - 1))
                for j in range(2):
                    high_w(u, j)

            def split(dst, src, gain):
                act.activation(dst, src, ACT.Copy, scale=gain).then_inc(x_hi_done, 1)

            def root(n, features, dst):
                act.wait_ge(x_sum_ready, n + 1)
                act.activation(halves(dst), pair, ACT.Sqrt, bias=eps[:, 0:1], scale=1.0 / features)\
                    .then_inc(root_done, 1)

            def rstd(n):
                act.wait_ge(ms_ready, n + 1)
                act.activation(halves(sq[:, :]), pair, ACT.Ln, bias=eps[:, 0:1], scale=1.0 / P)\
                    .then_inc(ln_done, 1)
                act.wait_ge(ln_done, n + 1)
                act.activation(sq[:, :], sq[:, :], ACT.Exp, scale=-0.5).then_inc(rstd_done, 1)

            def square_head(n, src):
                if n:
                    act.wait_ge(norm_done, n)
                act.activation(sq[:, :], src, ACT.Square).then_inc(sq_done, 1)

            def soften(jobs):
                for l, zz, _ in jobs:
                    chained(act.activation(l, zz, ACT.Abs))
                for l, _, _ in jobs:
                    chained(act.activation(l, l, ACT.Exp, scale=-1.0))
                for l, _, done in jobs:
                    act.activation(l, l, ACT.Ln, bias=one[:, 0:1]).then_inc(done, 1)

            def weights_of_sample(u):
                if u - 1 in SUM_END:
                    b = SUM_END.index(u - 1)
                    act.wait_ge(arg_s_done, b + 1)
                    if b >= 3:
                        act.wait_ge(v_used, PAGES * (b - 2))
                    act.activation(a_s[:, b % 3, :], z_s[:, :], ACT.Exp).then_inc(a_s_done, 1)

            def sample_job(u):
                if u not in SUM_END:
                    return []
                act.wait_ge(z_s_done, SUM_END.index(u) + 1)
                return [(soft_s[:, :], z_s[:, :], soft_s_done)]

            def square_residual(n, k):
                if k >= 2:
                    act.wait_ge(sum_done, n + k - 1)
                act.activation(h_sq[:, k % 2, :], h[:, k, :], ACT.Square).then_inc(sq_done, 1)

            act.wait_ge(built, 1)
            act.activation(y[:, 0, 0:1], one[:, 0:1], ACT.Copy)
            act.wait_ge(gain_in, 16)
            for k in range(KT):
                if k in X_PIECES:
                    act.wait_ge(x_in[X_PIECES.index(k)], 16)
                split(x_hi[:, k, :], h[:, k, :], gain_mix[:, k:k + 1])
                if k == 1:
                    act.wait_ge(w_in_first, 16)
                    high_w(0, 0)
                if k == 3:
                    act.wait_ge(w_in[0], 16)
                    high_w(0, 1)
            split_w(1)
            for k in range(POOL_SQUARES, KT):
                act.activation(x_sq[:, k, :], h[:, k, :], ACT.Square).then_inc(sq_done, 1)
            split_w(2)
            chained(act.activation(y[:, 0, 1:2], one[:, 0:1], ACT.Sqrt))
            act.wait_ge(built, 2)
            root(0, D_MODEL, x_r[:, :])

            for u in range(1, U_FFN):
                t = u - 1
                if u <= U_MLP:
                    if u == 2:
                        split_w(u + 1)
                    act.wait_ge(out_read, t + 1)
                    square_head(t, y[:, t % 2, :])
                    if u > 2:
                        split_w(u + 1)
                    rstd(t)
                elif u <= U_KV and u % 2 == 1:
                    i = (u - U_MLP - 1) // 2
                    act.wait_ge(out_read, t + 1)
                    if i:
                        act.wait_ge(tok_read, reads_before("turn", U_MLP + 2 * i) + 1)
                    act.activation(vg[:, :], y[:, t % 2, :], ACT.Gelu).then_inc(gelu_done, 1)
                    split_w(u + 1)
                    weights_of_sample(u)
                    act.wait_ge(centred, i + 1)
                    square_head(HEADS + i, vg[:, :])
                elif u <= U_KV:
                    i = (u - U_MLP - 2) // 2
                    rstd(HEADS + i)
                    soften(sample_job(u))
                    split_w(u + 1)
                    act.wait_ge(out_read, t + 1)
                    if i:
                        act.wait_ge(cm_done, i)
                    act.activation(ug[:, :], y[:, t % 2, :], ACT.Gelu).then_inc(gelu_done, 1)
                elif u < U_OUT and u % 2 == 1:
                    i = (u - U_KV - 1) // 2
                    act.wait_ge(out_read, t + 1)
                    square_head(2 * HEADS + i, y[:, t % 2, :])
                    if i:
                        act.wait_ge(arg_done, i)
                        act.activation(z[:, :], z[:, :], ACT.Exp).then_inc(a_done, 1)
                    weights_of_sample(u)
                    split_w(u + 1)
                    rstd(2 * HEADS + i)
                elif u <= U_OUT:
                    i = (u - U_KV - 2) // 2
                    if u == U_OUT:
                        act.wait_ge(out_done, U_OUT)
                        for k in range(HEADS):
                            split(x_hi[:, HEADS + k, :], o_cm[:, k, :], gain_out[:, HEADS + k:HEADS + k + 1])
                    split_w(u + 1)
                    act.wait_ge(z_done, i + 1)
                    soften([(soft[:, :], z[:, :], soft_done)] + sample_job(u))
                elif u == U_OUT + 1:
                    act.wait_ge(arg_done, HEADS)
                    act.activation(z[:, :], z[:, :], ACT.Exp).then_inc(a_done, 1)
                    split_w(u + 1)
                else:
                    split_w(u + 1)
                if u > U_OUT_SB:
                    for k in range(2 * (u - U_OUT_SB - 1), 2 * (u - U_OUT_SB)):
                        act.wait_ge(h_final, k + 1)
                        if k < 8:
                            split(x_hi[:, 8 + k, :], h[:, k, :], gain_ffn[:, k:k + 1])
                        square_residual(1, k)
                if u == CM_ROOT:
                    root(1, HEADS * P, cm_r[:, :])
                if u == SB_ROOT:
                    root(2, HEADS * P, sb_r[:, :])
                    for k in range(HEADS):
                        split(x_hi[:, k, :], q[:, k, :], gain_out[:, k:k + 1])

            act.wait_ge(out_done, T_FFN)
            for k in range(8, KT):
                if k >= KT - 2:
                    act.wait_ge(h_final, k + 1)
                split(x_hi[:, k - 8, :], h[:, k, :], gain_ffn[:, k:k + 1])
            for k in range(KT - 2, KT):
                square_residual(1, k)

            def gate_up(u, n, t, par, g, it=0):
                split_w(u + 1, it, 16 * CHUNK_UNITS, 2 * CHUNK_TILES)
                if u == U_FFN:
                    root(3, D_MODEL, h_r[:, :])
                act.wait_ge(out_read, it * (2 * CHUNK_TILES) + (t + 1))
                act.activation(y_gate[:, :], y_gate[:, :], ACT.Silu).then_inc(silu_done, 1)
                split_w(u + 2, it, 16 * CHUNK_UNITS, 2 * CHUNK_TILES)
                act.wait_ge(act_done, it * (2 * FFN_GROUP) + (n + 1))
                act.activation(act_hi[:, par, g, :], y_up[:, :], ACT.Copy).then_inc(act_hi_done, 1)

            for g in range(FFN_GROUP):
                gate_up(U_FFN + 2 * g, g, T_FFN + 2 * g, 0, g)
            with act.Fori(0, (FFN_CHUNKS - 1) // 2) as it:
                for half in range(2):
                    u0 = U_LOOP + half * CHUNK_UNITS
                    for g in range(FFN_GROUP):
                        gate_up(u0 + 2 * g, FFN_GROUP * (1 + half) + g, tiles_before(u0 + 2 * g), 1 - half, g, it)
                    for g in range(FFN_GROUP):
                        split_w(u0 + 2 * FFN_GROUP + g + 1, it, 16 * CHUNK_UNITS, 2 * CHUNK_TILES)

            act.wait_ge(p_in, 16)
            for k in range(2):
                act.activation(x_hi[:, k, :], p_raw[:, k, :], ACT.Copy).then_inc(x_hi_done, 1)
            for g in range(FFN_GROUP):
                split_w(U_LAST_DOWN + g + 1)
                for k in range(4 * g, 4 * g + 4):
                    act.wait_ge(out_read, T_LAST_DOWN + k + 1)
                    if k >= 2:
                        split(x_hi[:, k, :], h[:, k, :], gain_ple[:, k:k + 1])
                    square_residual(1 + KT, k)
            split_w(U_PROJ + 1)
            split_w(U_GATE)
            act.wait_ge(out_done, T_GATE)
            for k in range(2):
                split(x_hi[:, k, :], h[:, k, :], gain_ple[:, k:k + 1])
            root(4, D_MODEL, h_r[:, :])
            for m in range(KT):
                if U_GATE + m + 1 < UNITS:
                    split_w(U_GATE + m + 1)
                act.wait_ge(out_read, T_GATE + m + 1)
                act.activation(y_gate[:, :], y_gate[:, :], ACT.Sigmoid).then_inc(silu_done, 1)

        @block.vector
        def _(dve):
            count = {}

            def chained(ins, done=vec_step):
                count[done.name] = count.get(done.name, 0) + 1
                ins.then_inc(done, 1)
                dve.wait_ge(done, count[done.name])

            def low_w(u, j, it=0):
                dve.wait_ge(hi_done, it * (4 * CHUNK_UNITS) + (2 * u + j + 1))
                cols = slice(j * 8 * P, (j + 1) * 8 * P)
                dve.tensor_tensor(w_lo[:, u % 2, cols], w_raw[:, u % 2, cols], w_hi[:, u % 2, cols],
                                  ALU.subtract).then_inc(lo_done, 1)

            n_split = [0]

            def low_x(slot, src, gain):
                n_split[0] += 1
                dve.wait_ge(x_hi_done, n_split[0])
                dve.scalar_tensor_tensor(out=x_lo[:, slot, :], in0=src, scalar=gain, in1=x_hi[:, slot, :],
                                         op0=ALU.mult, op1=ALU.subtract).then_inc(x_lo_done, 1)

            def add_square(n_sq, k, src, total):
                dve.wait_ge(sq_done, n_sq + k + 1)
                if k == 0:
                    chained(dve.tensor_copy(total, src), sum_done)
                else:
                    chained(dve.tensor_tensor(total, total, src, ALU.add), sum_done)

            def invert(n, dst):
                dve.wait_ge(root_done, n + 1)
                chained(dve.reciprocal(dst, dst), r_done)

            def normalise(n, dst, src, gain, done=norm_done):
                dve.wait_ge(rstd_done, n + 1)
                chained(dve.scalar_tensor_tensor(out=dst, in0=src, scalar=gain, in1=sq[:, :],
                                                 op0=ALU.mult, op1=ALU.mult), done)

            def take(t, dst, r):
                dve.wait_ge(out_done, t + 1)
                chained(dve.tensor_tensor(halves(dst), tile_ps(t), halves(r), ALU.mult), out_read)

            def score_page(j):
                b, pg = divmod(j, PAGES)
                if pg == 0:
                    dve.wait_ge(q_rows_in, 16 * (b + 1))
                dve.wait_ge(k_in[j % RING], 16 * (j // RING + 1))
                for hd in range(HEADS):
                    cols = slice(hd * P, (hd + 1) * P)
                    at = pg * HEADS + hd
                    dve.tensor_tensor_reduce(k_ring[:, j % RING, cols], k_ring[:, j % RING, cols],
                                             q_rows[:, cols], 1.0, 0.0, ALU.mult, ALU.add,
                                             dot_s[:, at:at + 1]).then_inc(k_used, 1)
                if pg == PAGES - 1:
                    dve.wait_ge(k_used, HEADS * (j + 1))
                    if b:
                        dve.wait_ge(a_s_done, b)
                    chained(dve.scalar_tensor_tensor(
                        out=z_s[:, :].rearrange("p (g h) -> p g h", h=HEADS),
                        in0=dot_s[:, :].rearrange("p (g h) -> p g h", h=HEADS), scalar=SCALE,
                        in1=bias[:, :].unsqueeze(1).to_broadcast([P, PAGES, HEADS]),
                        op0=ALU.mult, op1=ALU.add), z_s_done)

            def keep_sample(b):
                dve.wait_ge(soft_s_done, b + 1)
                chained(dve.scalar_tensor_tensor(out=keep_s[:, :], in0=z_s[:, :], scalar=0.0,
                                                 in1=soft_s[:, :], op0=ALU.max, op1=ALU.add))
                chained(dve.scalar_tensor_tensor(out=z_s[:, :], in0=z_s[:, :], scalar=0.0,
                                                 in1=soft_s[:, :], op0=ALU.min, op1=ALU.subtract))

                def page(x, pg):
                    return x[:, pg * HEADS:(pg + 1) * HEADS]

                chained(dve.tensor_copy(page(soft_s, PAGES - 2), page(keep_s, PAGES - 1)))
                for pg in range(PAGES - 3, -1, -1):
                    chained(dve.tensor_tensor(page(soft_s, pg), page(soft_s, pg + 1), page(keep_s, pg + 1),
                                              ALU.add), keep_s_done if pg == 0 else vec_step)

            def weigh_sample(b):
                dve.wait_ge(later_s_ready, b + 1)
                chained(dve.tensor_tensor(z_s[:, :], z_s[:, :], tok_ps[:, 0:PAGES * HEADS], ALU.subtract),
                        tok_read)
                chained(dve.tensor_copy(dot_pad[:, :], z_s[:, 0:1]), arg_s_done)

            def diagonal(x):
                return x[:, 0:PROMPT].rearrange("p (c n) -> p c n", c=4)

            causal4 = causal[:, :].unsqueeze(1).to_broadcast([P, 4, P])

            def logits(i):
                dve.wait_ge(z_ready, i + 1)
                chained(dve.tensor_scalar(z[:, 0:1024], pair_flat, SCALE, bias[:, i:i + 1],
                                          ALU.mult, ALU.add), pair_read)
                chained(dve.tensor_scalar(z[:, 1024:CELLS], mix_ps[:, 0:CELLS - 1024], SCALE,
                                          bias[:, i:i + 1], ALU.mult, ALU.add), z_done)

            def keep_head(i):
                dve.wait_ge(soft_done, i + 1)
                chained(dve.scalar_tensor_tensor(out=keep[:, :], in0=z[:, :], scalar=0.0, in1=soft[:, :],
                                                 op0=ALU.max, op1=ALU.add))
                chained(dve.scalar_tensor_tensor(out=z[:, :], in0=z[:, :], scalar=0.0, in1=soft[:, :],
                                                 op0=ALU.min, op1=ALU.subtract))
                chained(dve.tensor_tensor(diagonal(keep), diagonal(keep), causal4, ALU.mult))
                chained(dve.tensor_tensor(soft[:, 0:P], keep[:, DIAG(3)], keep[:, 896:1024], ALU.add))
                chained(dve.tensor_tensor(soft[:, P:2 * P], keep[:, DIAG(2)], keep[:, 1024:1152], ALU.add))
                chained(dve.tensor_tensor(soft[:, 2 * P:3 * P], soft[:, 0:P], keep[:, 1152:1280], ALU.add),
                        keep_done)

            def exponents(i):
                dve.wait_ge(later_ready, i + 1)
                chained(dve.tensor_tensor(z[:, 0:1024], z[:, 0:1024], pair_flat, ALU.subtract), pair_read)
                chained(dve.tensor_tensor(z[:, 1024:CELLS], z[:, 1024:CELLS], mix_ps[:, 0:CELLS - 1024],
                                          ALU.subtract), arg_done)

            def mask_weights(i):
                dve.wait_ge(a_done, i + 1)
                chained(dve.tensor_tensor(diagonal(z), diagonal(z), causal4, ALU.mult), masked)

            def take_attention(i):
                dve.wait_ge(av_ready, i + 1)
                chained(dve.tensor_copy(q[:, i, 0:PROMPT], tok_ps[:, :]), tok_read)

            def take_turned(n):
                dve.wait_ge(turned, n + 1)
                chained(dve.tensor_copy(v_tok[:, :, :].rearrange("p c n -> p (c n)"), tok_ps[:, :]), tok_read)

            def out_tile(n, r):
                m = n % KT
                if n in (0, H_KEYS, H_PAGES):
                    dve.wait_ge(h_in[(0, H_KEYS, H_PAGES).index(n)], 16)
                take(T_OUT + n, sq[:, :], r[:, :])
                chained(dve.tensor_tensor(h[:, m, :], h[:, m, :], sq[:, :], ALU.add),
                        h_final if n >= KT else vec_step)

            dve.wait_ge(gain_in, 16)
            for k in range(KT):
                low_x(k, h[:, k, :], gain_mix[:, k:k + 1])
                if k == 1:
                    low_w(0, 0)
            low_w(1, 0)
            first = POOL_SQUARES
            for k in range(first + 2, KT, 2):
                dve.wait_ge(sq_done, k + 2 - first)
                chained(dve.tensor_tensor(x_sq[:, first:first + 2, :], x_sq[:, first:first + 2, :],
                                          x_sq[:, k:k + 2, :], ALU.add))
            chained(dve.tensor_tensor(x_r[:, :], x_sq[:, first, :], x_sq[:, first + 1, :], ALU.add))
            dve.wait_ge(pool_sum_done, 1)
            chained(dve.tensor_tensor(x_r[:, :], x_r[:, :], x_sq[:, 0, :], ALU.add), sum_done)
            low_w(2, 0)
            low_w(2, 1)
            dve.wait_ge(built, 2)
            invert(0, x_r[:, :])

            for u in range(1, U_FFN):
                t = u - 1
                pages = list(k_pages(u))

                def score_next():
                    if pages:
                        score_page(pages.pop(0))

                if u <= U_OUT:
                    if t > U_KV and t % 2 == 1 and t > U_KV + 2:
                        dve.wait_ge(v_out, 16 * ((t - U_KV - 1) // 2))
                    take(t, y[:, t % 2, :], x_r[:, :])
                else:
                    out_tile(2 * (u - U_OUT) - 1, cm_r if u <= U_OUT_SB else sb_r)
                if u - 1 in REDUCE_END:
                    b = REDUCE_END.index(u - 1)
                    dve.wait_ge(o_s_ready, b + 1)
                    if u - 1 in SUM_END:
                        dve.wait_ge(later_s_ready, SUM_END.index(u - 1) + 1)
                    chained(dve.tensor_copy(q[:, :, PROMPT + b], tok_ps[:, P:P + HEADS]), tok_read)
                if u - 1 in SUM_END:
                    weigh_sample(SUM_END.index(u - 1))

                if u <= U_MLP:
                    if u > 1:
                        low_w(u + 1, 0)
                        low_w(u + 1, 1)
                    normalise(t, q[:, t, :], y[:, t % 2, :], gain_q[:, 0:1])
                elif u <= U_KV + 1 and u % 2 == 1:
                    if u == U_MLP + 1:
                        dve.wait_ge(q_rows_ready, 1)
                        chained(dve.tensor_copy(acc[0:SAMPLES, :], pair_flat[0:SAMPLES, :]), pair_read)
                    else:
                        i = (u - U_MLP - 3) // 2
                        score_next()
                        dve.wait_ge(mixed, i + 1)
                        chained(dve.tensor_tensor(
                            o_cm[:, i, 0:PROMPT].rearrange("p (c n) -> p c n", c=4),
                            mix_ps[:, :].rearrange("p (c n) -> p c n", c=4),
                            b_mix[:, i, :].unsqueeze(1).to_broadcast([P, 4, P]), ALU.add), mix_read)
                        dve.wait_ge(gelu_done, 2 * i + 2)
                        chained(dve.tensor_tensor(o_cm[:, i, :], o_cm[:, i, :], ug[:, :], ALU.mult), cm_done)
                    low_w(u + 1, 0)
                    low_w(u + 1, 1)
                    score_next()
                    if u < U_KV:
                        i = (u - U_MLP - 1) // 2
                        dve.wait_ge(mean_ready, i + 1)
                        dve.wait_ge(gelu_done, 2 * i + 1)
                        chained(dve.scalar_tensor_tensor(out=halves(vg[:, :]), in0=pair, scalar=-1.0 / P,
                                                         in1=halves(vg[:, :]), op0=ALU.mult, op1=ALU.add),
                                centred)
                elif u <= U_KV:
                    i = (u - U_MLP - 2) // 2
                    normalise(HEADS + i, vg[:, :], vg[:, :], lng[:, i:i + 1], vec_step)
                    chained(dve.tensor_scalar(vg[:, :], vg[:, :], lnb[:, i:i + 1], None, ALU.add), norm_done)
                    chained(dve.tensor_copy(chunk_v[:, i, :], vg[:, PROMPT:TOK]))
                    chained(dve.tensor_scalar(o_cm[:, i, PROMPT:TOK], vg[:, PROMPT:TOK], w00[:, i:i + 1],
                                              b_mix[:, i, 0:1], ALU.mult, ALU.add))
                    low_w(u + 1, 0)
                    low_w(u + 1, 1)
                    score_next()
                    take_turned(i)
                elif u <= U_OUT and u % 2 == 0:
                    i = (u - U_KV - 2) // 2
                    if u == U_OUT:
                        for k in range(HEADS):
                            low_x(HEADS + k, o_cm[:, k, :], gain_out[:, HEADS + k:HEADS + k + 1])
                    logits(i)
                    score_next()
                    low_w(u + 1, 0)
                    low_w(u + 1, 1)
                    score_next()
                    keep_head(i)
                    take_turned(HEADS + i)
                else:
                    if u > U_OUT + 1:
                        low_w(u + 1, 0)
                        low_w(u + 1, 1)
                if U_KV < u <= U_OUT + 1 and u % 2 == 1:
                    i = (u - U_KV - 1) // 2
                    if i:
                        exponents(i - 1)
                        score_next()
                        mask_weights(i - 1)
                    if u > U_KV + 1:
                        low_w(u + 1, 0)
                        low_w(u + 1, 1)
                    if u < U_OUT:
                        if i:
                            dve.wait_ge(k_out, 16 * i)
                        normalise(2 * HEADS + i, k_head[:, :], y[:, t % 2, :], gain_k[:, 0:1])
                    if i:
                        take_attention(i - 1)
                if u == CM_ROOT:
                    invert(1, cm_r[:, :])
                if u == SB_ROOT:
                    invert(2, sb_r[:, :])
                    for k in range(HEADS):
                        low_x(k, q[:, k, :], gain_out[:, k:k + 1])
                if u in SUM_END:
                    keep_sample(SUM_END.index(u))
                while pages:
                    score_next()
                if u > U_OUT_SB:
                    for k in range(2 * (u - U_OUT_SB - 1), 2 * (u - U_OUT_SB)):
                        if k < 8:
                            low_x(8 + k, h[:, k, :], gain_ffn[:, k:k + 1])
                        add_square(X_SQUARES + 3 * HEADS, k, h_sq[:, k % 2, :], h_sum[:, :])
                if u >= U_OUT:
                    out_tile(2 * (u - U_OUT), cm_r if u < U_OUT_SB else sb_r)

            out_tile(2 * KT - 1, sb_r)
            for k in range(8, KT):
                low_x(k - 8, h[:, k, :], gain_ffn[:, k:k + 1])
            for k in range(KT - 2, KT):
                add_square(X_SQUARES + 3 * HEADS, k, h_sq[:, k % 2, :], h_sum[:, :])

            def take_loop(t, dst, it):
                dve.wait_ge(out_done, it * (2 * CHUNK_TILES) + (t + 1))
                dve.tensor_tensor(halves(dst), tile_ps(t), halves(h_r[:, :]), ALU.mult).then_inc(out_read, 1)

            def gate_up(u, n, t, par, g, it=0):
                n_it = it * (2 * FFN_GROUP)
                low_w(u + 1, 0, it)
                low_w(u + 1, 1, it)
                if u == U_FFN:
                    invert(3, h_r[:, :])
                else:
                    dve.wait_ge(act_lo_done, n_it + n)
                take_loop(t, y_gate[:, :], it)
                low_w(u + 2, 0, it)
                low_w(u + 2, 1, it)
                take_loop(t + 1, y_up[:, :], it)
                dve.wait_ge(out_read, it * (2 * CHUNK_TILES) + (t + 2))
                dve.wait_ge(silu_done, n_it + (n + 1))
                dve.tensor_tensor(y_up[:, :], y_up[:, :], y_gate[:, :], ALU.mult).then_inc(act_done, 1)
                dve.wait_ge(act_hi_done, n_it + (n + 1))
                dve.tensor_tensor(act_lo[:, par, g, :], y_up[:, :], act_hi[:, par, g, :], ALU.subtract)\
                    .then_inc(act_lo_done, 1)

            def down_tile(t, m, it=0):
                dve.wait_ge(out_done, it * (2 * CHUNK_TILES) + (t + 1))
                dve.wait_ge(out_read, it * (2 * CHUNK_TILES) + t)
                dve.tensor_tensor(halves(h[:, m, :]), halves(h[:, m, :]), tile_ps(t), ALU.add)\
                    .then_inc(out_read, 1)

            for g in range(FFN_GROUP):
                gate_up(U_FFN + 2 * g, g, T_FFN + 2 * g, 0, g)
            with dve.Fori(0, (FFN_CHUNKS - 1) // 2) as it:
                for half in range(2):
                    u0 = U_LOOP + half * CHUNK_UNITS
                    for g in range(FFN_GROUP):
                        gate_up(u0 + 2 * g, FFN_GROUP * (1 + half) + g, tiles_before(u0 + 2 * g), 1 - half, g, it)
                    for g in range(FFN_GROUP):
                        u = u0 + 2 * FFN_GROUP + g
                        for j in range(4):
                            if j < 2:
                                low_w(u + 1, j, it)
                            down_tile(tiles_before(u) + j, 4 * g + j, it)

            for k in range(2):
                n_split[0] += 1
                dve.wait_ge(x_hi_done, n_split[0])
                dve.tensor_tensor(x_lo[:, k, :], p_raw[:, k, :], x_hi[:, k, :], ALU.subtract)\
                    .then_inc(x_lo_done, 1)
            for g in range(FFN_GROUP):
                for j in range(4):
                    k = 4 * g + j
                    if j < 2:
                        low_w(U_LAST_DOWN + g + 1, j)
                    down_tile(T_LAST_DOWN + k, k)
                    if k >= 2:
                        low_x(k, h[:, k, :], gain_ple[:, k:k + 1])
                    add_square(X_SQUARES + 3 * HEADS + KT, k, h_sq[:, k % 2, :], h_sum[:, :])
            for m in range(KT):
                if m % 8 < 2:
                    low_w(U_PROJ + 1 + m // 8, m % 8)
                dve.wait_ge(out_done, T_PROJ + m + 1)
                dve.tensor_copy(halves(proj[:, m, :]), tile_ps(T_PROJ + m)).then_inc(out_read, 1)
            for k in range(2):
                low_x(k, h[:, k, :], gain_ple[:, k:k + 1])
            invert(4, h_r[:, :])
            count[out_read.name] = T_GATE
            for m in range(KT):
                if U_GATE + m + 1 < UNITS:
                    low_w(U_GATE + m + 1, 0)
                    low_w(U_GATE + m + 1, 1)
                take(T_GATE + m, y_gate[:, :], h_r[:, :])
                dve.wait_ge(silu_done, FFN_GROUP * FFN_CHUNKS + m + 1)
                chained(dve.tensor_tensor(y_gate[:, :], y_gate[:, :], proj[:, m, :], ALU.mult))
                chained(dve.tensor_tensor(h[:, m, :], h[:, m, :], y_gate[:, :], ALU.add), h_final)

        @block.tensor
        def _(pe):
            def block_products(u, blk, t, hi, lo, first, last):
                cols = slice(blk * P, (blk + 1) * P)
                terms = ((w_hi, hi), (w_hi, lo), (w_lo, hi))
                for n, (w, x) in enumerate(terms):
                    for a in range(2):
                        mm = pe.matmul(out_ps[:, 2 * (t % 2) + a, 0:HALF], w[:, u % 2, cols],
                                       x[:, a * HALF:(a + 1) * HALF],
                                       start=first and n == 0, stop=last and n == len(terms) - 1)
                if last:
                    mm.then_inc(out_done, 1)

            def unit(u, tiles, operand, each=None, it=0, between=None):
                per = SLOTS // tiles
                for b in range(SLOTS):
                    if b % 8 == 0 and u >= 2:
                        pe.wait_ge(lo_done, it * (4 * CHUNK_UNITS) + (2 * u + b // 8 + 1 - POOL_LO))
                    elif b % 8 == 0:
                        pe.wait_ge(pool_lo_done if b else lo_done, u + 1)
                    if b == (12 if u == 1 else 8) and between:
                        between()
                    t = tiles_before(u) + b // per
                    if b % per == 0 and t >= 2:
                        pe.wait_ge(out_read, it * (2 * CHUNK_TILES) + (t - 1))
                    if each:
                        each(b)
                    hi, lo = operand(b)
                    block_products(u, b, t, hi, lo, b % per == 0, b % per == per - 1)

            pair_free = [None]
            mix_free = [None]

            def wait_free(free, reader):
                if free[0]:
                    pe.wait_ge(*free[0])
                free[0] = reader

            def sum_features(n, x, ready, done, reader):
                pe.wait_ge(ready, done)
                wait_free(pair_free, reader)
                for a in range(2):
                    mm = pe.matmul(pair_ps[:, a, 0:HALF], ones[:, :], x[:, a * HALF:(a + 1) * HALF],
                                   start=True, stop=True)
                return mm

            def turn(n, src, u):
                pe.wait_ge(tok_read, reads_before("turn", u))
                for c in range(4):
                    mm = pe.transpose(tok_ps[:, c * P:(c + 1) * P], src[:, c * P:(c + 1) * P], ident[:, :])
                mm.then_inc(turned, 1)

            def mix(i):
                pe.wait_ge(built, 2)
                pe.wait_ge(tok_read, reads_before("turn", U_MLP + 2 + 2 * i) + 1)
                wait_free(mix_free, (mix_read, i + 1))
                for c in range(4):
                    mm = pe.matmul(mix_ps[:, c * P:(c + 1) * P], v_tok[:, c, :], w_mix[:, i, :],
                                   start=True, stop=True)
                mm.then_inc(mixed, 1)

            def scores(i):
                pe.wait_ge(norm_done, 2 * HEADS + i + 1)
                wait_free(pair_free, (pair_read, 2 * i + 2))
                wait_free(mix_free, (z_done, i + 1))
                for kb in range(4):
                    key = k_head[:, kb * P:(kb + 1) * P]
                    mm = pe.matmul(pair_flat[:, DIAG(kb)], key, q[:, i, kb * P:(kb + 1) * P],
                                   start=True, stop=True)
                for kb in range(3):
                    n = (3 - kb) * P
                    key = k_head[:, kb * P:(kb + 1) * P]
                    dst = mix_ps[:, 0:n] if kb == 1 else pair_flat[:, OFF[kb]:OFF[kb] + n]
                    mm = pe.matmul(dst, key, q[:, i, PROMPT - n:PROMPT], start=True, stop=True)
                mm.then_inc(z_ready, 1)

            def sum_later(i):
                pe.wait_ge(keep_done, i + 1)
                wait_free(pair_free, (pair_read, 2 * i + 3))
                wait_free(mix_free, (arg_done, i + 1))
                pe.matmul(pair_flat[:, 0:512], later[:, :], keep[:, 0:512], start=True, stop=True)
                pe.matmul(pair_flat[:, 512:1024], later[:, :], keep[:, 512:1024], start=True, stop=False,
                          skip_group_check=True)
                for col, src in ((512, keep[:, DIAG(1)]), (640, soft[:, P:2 * P]),
                                 (768, soft[:, 2 * P:3 * P]), (896, keep[:, DIAG(3)])):
                    pe.matmul(pair_flat[:, col:col + P], ones[:, :], src, start=False, stop=col == 896,
                              skip_group_check=True)
                pe.matmul(mix_ps[:, 0:256], later[:, :], keep[:, 1024:CELLS], start=True, stop=False,
                          skip_group_check=True)
                pe.matmul(mix_ps[:, 0:P], ones[:, :], keep[:, DIAG(2)], start=False, stop=False,
                          skip_group_check=True)
                pe.matmul(mix_ps[:, P:2 * P], ones[:, :], soft[:, 0:P], start=False, stop=True,
                          skip_group_check=True).then_inc(later_ready, 1)

            def attend(i, u):
                pe.wait_ge(masked, i + 1)
                pe.wait_ge(tok_read, reads_before("av", u))
                for kb in range(4):
                    pe.matmul(tok_ps[:, DIAG(kb)], v_tok[:, kb, :], z[:, DIAG(kb)], start=kb == 0,
                              stop=False, skip_group_check=True)
                for kb in range(3):
                    n = (3 - kb) * P
                    mm = pe.matmul(tok_ps[:, PROMPT - n:PROMPT], v_tok[:, kb, :], z[:, OFF[kb]:OFF[kb] + n],
                                   start=False, stop=kb == 2, skip_group_check=True)
                mm.then_inc(av_ready, 1)

            def reduce_sample(b, u):
                pe.wait_ge(v_used, PAGES * (b + 1))
                pe.wait_ge(tok_read, reads_before("reduce", u))
                for hd in range(HEADS):
                    mm = pe.matmul(tok_ps[:, P + hd:P + hd + 1], acc[:, hd * P:(hd + 1) * P], ones[:, 0:1],
                                   start=True, stop=True)
                mm.then_inc(o_s_ready, 1)

            def sum_later_sample(b, u):
                pe.wait_ge(keep_s_done, b + 1)
                pe.wait_ge(tok_read, reads_before("later", u) - (u in REDUCE_END))
                n = (PAGES - 1) * HEADS
                pe.matmul(tok_ps[:, 0:PAGES * HEADS], later[:, :], keep_s[:, :], start=True, stop=False,
                          skip_group_check=True)
                pe.matmul(tok_ps[:, 0:n], ones[:, :], soft_s[:, 0:n], start=False, stop=True,
                          skip_group_check=True).then_inc(later_s_ready, 1)

            def in_operand(b):
                return x_hi[:, b, :], x_lo[:, b, :]

            unit(0, 1, in_operand, each=lambda b: pe.wait_ge(x_lo_done, b + 1))
            pe.wait_ge(built, 1)

            for u in range(1, U_FFN):
                def between():
                    if u == 1:
                        sum_features(0, x_r, sum_done, 1, (root_done, 1)).then_inc(x_sum_ready, 1)
                    elif u <= U_MLP:
                        n = u - 1 if u > 2 else 0
                        sum_features(n, sq, sq_done, X_SQUARES + n + 1, (ln_done, n + 1)).then_inc(ms_ready, 1)
                    elif u < U_KV and u % 2 == 1:
                        i = (u - U_MLP - 1) // 2
                        sum_features(i, vg, gelu_done, 2 * i + 1, (centred, i + 1)).then_inc(mean_ready, 1)
                    elif u <= U_KV:
                        i = (u - U_MLP - 2) // 2
                        pe.wait_ge(norm_done, HEADS + i + 1)
                        turn(i, vg, u)
                    elif u <= U_OUT + 1 and u % 2 == 1:
                        i = (u - U_KV - 1) // 2
                        if u < U_OUT:
                            n = 2 * HEADS + i
                            sum_features(n, sq, sq_done, X_SQUARES + n + 1, (ln_done, n + 1)).then_inc(ms_ready, 1)
                        if i:
                            attend(i - 1, u)
                    elif u <= U_OUT:
                        i = (u - U_KV - 2) // 2
                        pe.wait_ge(out_read, u)
                        turn(HEADS + i, y[:, 1, :], u)
                        if u == CM_ROOT:
                            sum_features(1, cm_r, cm_sum_done, 1, (root_done, 2)).then_inc(x_sum_ready, 1)

                if u < U_OUT:
                    unit(u, 1, in_operand, between=between)
                else:
                    slot0 = HEADS if u < U_OUT_SB else 0
                    n0 = KT if u < U_OUT_SB else KT + HEADS
                    unit(u, 2, lambda b: in_operand(slot0 + b % 8), between=between,
                         each=(lambda b: pe.wait_ge(x_lo_done, n0 + b % 8 + 1))
                         if u in (U_OUT, U_OUT_SB) else None)
                if u == 2:
                    sum_features(1, sq, sq_done, X_SQUARES + 2, (ln_done, 2)).then_inc(ms_ready, 1)
                elif u == U_MLP:
                    pe.wait_ge(norm_done, HEADS)
                    wait_free(pair_free, (pair_read, 1))
                    for hd in range(HEADS):
                        mm = pe.transpose(pair_flat[0:SAMPLES, hd * P:(hd + 1) * P], q[:, hd, PROMPT:TOK],
                                          ident[:, :])
                    mm.then_inc(q_rows_ready, 1)
                elif U_MLP < u < U_KV and u % 2 == 1:
                    n = HEADS + (u - U_MLP - 1) // 2
                    sum_features(n, sq, sq_done, X_SQUARES + n + 1, (ln_done, n + 1)).then_inc(ms_ready, 1)
                elif U_MLP < u <= U_KV:
                    mix((u - U_MLP - 2) // 2)
                elif U_KV < u < U_OUT and u % 2 == 1:
                    scores((u - U_KV - 1) // 2)
                elif U_KV < u <= U_OUT:
                    sum_later((u - U_KV - 2) // 2)
                if u in REDUCE_END:
                    reduce_sample(REDUCE_END.index(u), u)
                if u in SUM_END:
                    sum_later_sample(SUM_END.index(u), u)
                if u == SB_ROOT - 1:
                    sum_features(2, sb_r, sb_sum_done, 1, (root_done, 3)).then_inc(x_sum_ready, 1)

            def ffn_operand(b):
                return in_operand((b + 8) % KT)

            for u in range(U_FFN, U_LOOP):
                unit(u, 1, ffn_operand,
                     each=(lambda b: pe.wait_ge(x_lo_done, 2 * KT + b + 1)) if u == U_FFN else None)
                if u == U_FFN:
                    sum_features(3, h_sum, sum_done, 1 + KT, (root_done, 4)).then_inc(x_sum_ready, 1)

            def down_unit(u, par, it=0):
                unit(u, 4, lambda b: (act_hi[:, par, b % 4, :], act_lo[:, par, b % 4, :]), it=it)

            with pe.Fori(0, (FFN_CHUNKS - 1) // 2) as it:
                for half in range(2):
                    u0 = U_LOOP + half * CHUNK_UNITS
                    for x in range(2 * FFN_GROUP):
                        unit(u0 + x, 1, ffn_operand, it=it)
                    pe.wait_ge(act_lo_done, it * (2 * FFN_GROUP) + FFN_GROUP * (1 + half))
                    for g in range(FFN_GROUP):
                        down_unit(u0 + 2 * FFN_GROUP + g, half, it)
            pe.wait_ge(act_lo_done, FFN_GROUP * FFN_CHUNKS)
            for g in range(FFN_GROUP):
                down_unit(U_LAST_DOWN + g, (FFN_CHUNKS - 1) % 2)

            pe.wait_ge(x_lo_done, 3 * KT + 2)
            for s in range(2):
                unit(U_PROJ + s, 8, lambda b: in_operand(b % 2))
            sum_features(4, h_sum, sum_done, 1 + 2 * KT, (root_done, 5)).then_inc(x_sum_ready, 1)
            for m in range(KT):
                unit(U_GATE + m, 1, lambda b: in_operand((b + 2) % KT),
                     each=(lambda b: pe.wait_ge(x_lo_done, 3 * KT + 2 + b + 1)) if m == 0 else None)


def kernel(x_prompt, x_sample, cache_k, cache_v, page_table, p_prompt, p_sample, g_mix, w_in, g_q, g_k,
           sb_bias, sgu_ln_g, sgu_ln_b, w_s, b_s, g_out_sb, g_out_cm, w_out, g_ffn, w_gate, w_up, w_down,
           g_ple, w_ple_gate, w_ple_proj):
    import numpy as np
    import concourse.bacc as bacc
    from concourse.bass_utils import run_bass_kernel_spmd as run

    a = lambda x: np.asarray(x)

    def feature_major(prompt, sample):
        x = np.concatenate([a(prompt).reshape(PROMPT, -1), a(sample).reshape(SAMPLES, -1)])
        return x.T.reshape(-1, P, TOK).transpose(1, 0, 2)

    def by_partition(g):
        return a(g).reshape(-1, P).T

    def by_tile(w):
        return w.reshape(w.shape[0] // P, P, w.shape[1] // P, P).transpose(2, 1, 0, 3)

    tile_order = list(range(HEADS))
    tile_order += [x for i in range(HEADS) for x in (4 * HEADS + i, 3 * HEADS + i)]
    tile_order += [x for i in range(HEADS) for x in (HEADS + i, 2 * HEADS + i)]
    w_in_u = by_tile(a(w_in)[0])[tile_order].reshape(-1, P, SLOTS * P)
    w_out_u = a(w_out)[0].reshape(2, 8, P, 8, 2, P).transpose(0, 3, 2, 4, 1, 5)[::-1]
    w_out_u = w_out_u.reshape(-1, P, SLOTS * P)
    gate_up = np.stack([by_tile(a(w_gate)[0]), by_tile(a(w_up)[0])], axis=1)
    gate_up = gate_up.reshape(FFN_CHUNKS, 2 * FFN_GROUP, P, SLOTS * P)
    down = a(w_down)[0].reshape(FFN_CHUNKS, FFN_GROUP, P, 4, 4, P).transpose(0, 3, 2, 4, 1, 5)
    down = down.reshape(FFN_CHUNKS, FFN_GROUP, P, SLOTS * P)
    ffn = [gate_up[0]]
    for c in range(1, FFN_CHUNKS):
        ffn += [gate_up[c], down[c - 1]]
    ffn.append(down[-1])
    proj_u = a(w_ple_proj)[0].reshape(2, P, 2, 8, P).transpose(2, 1, 3, 0, 4).reshape(2, P, SLOTS * P)
    gate_t = by_tile(a(w_ple_gate)[0])
    gate_u = np.concatenate([gate_t[:, :, 2:], gate_t[:, :, :2]], axis=2).reshape(-1, P, SLOTS * P)
    arrays = {
        "w_units": np.concatenate([w_in_u, w_out_u, *ffn, proj_u, gate_u]),
        "x_t": feature_major(x_prompt, x_sample),
        "p_t": feature_major(p_prompt, p_sample),
        "cache_k": a(cache_k).reshape(N_PHYS, P, HEADS * P),
        "cache_v": a(cache_v).reshape(N_PHYS, P, HEADS * P),
        "page_table": a(page_table).reshape(1, N_PAGES),
        "g_mix": by_partition(g_mix),
        "g_out": np.concatenate([by_partition(g_out_sb), by_partition(g_out_cm)], axis=1),
        "g_ffn": by_partition(g_ffn),
        "g_ple": by_partition(g_ple),
        "g_q": a(g_q).reshape(P, 1),
        "g_k": a(g_k).reshape(P, 1),
        "ln_g": by_partition(sgu_ln_g),
        "ln_b": by_partition(sgu_ln_b),
        "w_s_t": a(w_s)[0].transpose(2, 0, 1),
        "b_s": a(b_s).reshape(1, HEADS, P),
        "sb_bias": a(sb_bias).reshape(1, HEADS),
        "w_s00": a(w_s)[0, :, 0, 0].reshape(1, HEADS),
    }
    arrays = {k: np.ascontiguousarray(v) for k, v in arrays.items()}
    outs = {"y_t": (P, KT, TOK), "k_t": (HEADS, P, TOK), "v_t": (HEADS, P, TOK),
            "chunk_v_t": (P, HEADS, SAMPLES)}
    nc = bacc.Bacc("TRN2", target_bir_lowering=False, num_devices=1)
    aps = {k: nc.dram_tensor(k, v.shape, mybir.dt.from_np(v.dtype), kind="ExternalInput").ap()
           for k, v in arrays.items()}
    aps |= {k: nc.dram_tensor(k, s, F32, kind="ExternalOutput").ap() for k, s in outs.items()}
    build(nc, **aps)
    got = run(nc, [arrays], core_ids=[0]).results[0]

    y = got["y_t"].transpose(2, 1, 0).reshape(TOK, D_MODEL)
    k = got["k_t"].transpose(2, 0, 1)
    v = got["v_t"].transpose(2, 0, 1)
    chunk = got["chunk_v_t"].transpose(2, 1, 0)
    new = (SAMPLES, 1, HEADS, P)
    return tuple(np.ascontiguousarray(x) for x in (
        y[:PROMPT].reshape(1, PROMPT, D_MODEL), y[PROMPT:].reshape(SAMPLES, 1, D_MODEL),
        k[:PROMPT].reshape(1, 1, PROMPT, HEADS, P), v[:PROMPT].reshape(1, 1, PROMPT, HEADS, P),
        k[PROMPT:].reshape(1, *new), v[PROMPT:].reshape(1, *new), chunk.reshape(1, *new)))
```

```python
from contextlib import ExitStack

import concourse.bass as bass
from concourse import mybir

F32 = mybir.dt.float32
F32R = mybir.dt.float32r
I32 = mybir.dt.int32
ALU = mybir.AluOpType
ACT = mybir.ActivationFunctionType

P = 128
D_MODEL = 2048
PROMPT = 512
SAMPLES = 8
TOK = PROMPT + SAMPLES
HALF = TOK // 2
HEADS = 8
PAGES = 8
N_PHYS = 80
D_FF = 5632
EPS = 1e-6
SCALE = float(P) ** -0.5

KT = D_MODEL // P
SLOTS = 16
FFN_GROUP = 4
FFN_CHUNKS = D_FF // P // FFN_GROUP

U_MLP = HEADS
U_KV = U_MLP + 2 * HEADS
U_OUT = U_KV + 2 * HEADS
U_OUT_SB = U_OUT + 8
U_FFN = U_OUT_SB + 8
U_LOOP = U_FFN + 2 * FFN_GROUP
CHUNK_UNITS = 3 * FFN_GROUP
U_LAST_DOWN = U_LOOP + CHUNK_UNITS * (FFN_CHUNKS - 1)
U_PROJ = U_LAST_DOWN + FFN_GROUP
U_GATE = U_PROJ + 2
UNITS = U_GATE + KT

T_OUT = U_OUT
T_OUT_SB = T_OUT + KT
T_FFN = T_OUT_SB + KT
T_LOOP = T_FFN + 2 * FFN_GROUP
CHUNK_TILES = 2 * FFN_GROUP + KT
T_LAST_DOWN = T_LOOP + CHUNK_TILES * (FFN_CHUNKS - 1)
T_PROJ = T_LAST_DOWN + KT
T_GATE = T_PROJ + KT



def tiles_before(u):
    if u <= U_OUT:
        return u
    if u <= U_FFN:
        return T_OUT + 2 * (u - U_OUT)
    if u <= U_LOOP:
        return T_FFN + u - U_FFN
    if u <= U_LAST_DOWN:
        c, x = divmod(u - U_LOOP, CHUNK_UNITS)
        return T_LOOP + CHUNK_TILES * c + min(x, 2 * FFN_GROUP) + 4 * max(x - 2 * FFN_GROUP, 0)
    if u <= U_PROJ:
        return T_LAST_DOWN + 4 * (u - U_LAST_DOWN)
    if u <= U_GATE:
        return T_PROJ + 8 * (u - U_PROJ)
    return T_GATE + u - U_GATE


X_PIECES = [0, 2, 4, 8, 12, 16]
POOL_SQUARES = 6
X_SQUARES = KT - POOL_SQUARES
POOL_LO = 2

K_PER = (3, 2)
CONSTS = 11
RING = 2
CM_ROOT = U_OUT - 2
SB_ROOT = U_OUT + 5
SB_SPLITS = {U_OUT_SB - 3 + i: range(3 * i, min(3 * i + 3, HEADS)) for i in range(3)}
K_PERIOD = 10
K_WIDE = K_PER[0] * (U_KV - K_PERIOD)
N_PAGES = SAMPLES * PAGES


def k_period(j):
    return K_PERIOD + j // K_PER[0] if j < K_WIDE else U_KV + (j - K_WIDE) // K_PER[1]


LAST_K = [k_period(PAGES * b + PAGES - 1) for b in range(SAMPLES)]
SUM_END = [p + 1 + (p + 1) % 2 for p in LAST_K]
REDUCE_END = [18, 22, 25, 28, 31, 34, 37, 40]

DIAG = lambda kb: slice(kb * P, (kb + 1) * P)
OFF = {0: 512, 1: 1024, 2: 896}
CELLS = 1280


def k_pages(period):
    return [j for j in range(N_PAGES) if k_period(j) == period]


K_SLOT = [j % 3 if j < K_WIDE else j % 2 for j in range(N_PAGES)]


def k_turn(j):
    return K_SLOT[:j].count(K_SLOT[j])


def k_before(j):
    if j >= K_WIDE:
        return max([i for i in range(j) if K_SLOT[i] == K_SLOT[j]])
    return j - 3 if j >= 3 else None


def build(nc, w_units, x_t, p_t, cache_k, cache_v, page_table, g_mix, g_out, g_ffn, g_ple, g_q, g_k,
          ln_g, ln_b, w_s_t, b_s, sb_bias, w_s00, y_t, k_t, v_t, chunk_v_t):
    q_rows_dram = nc.dram_tensor("q_rows_dram", (SAMPLES, HEADS * P), F32, kind="Internal").ap()

    with ExitStack() as ctx:
        def sb(name, shape, dt=F32, where=ctx):
            return where.enter_context(nc.sbuf_tensor(name, shape, dt))

        def sem(name):
            return ctx.enter_context(nc.semaphore(name))

        x_hi = sb("x_hi", [P, KT, TOK], F32R)
        x_lo = sb("x_lo", [P, KT, TOK], F32R)
        w_raw = sb("w_raw", [P, 2, SLOTS * P])
        w_hi = sb("w_hi", [P, 2, SLOTS * P], F32R)
        w_lo = sb("w_lo", [P, 2, SLOTS * P], F32R)

        with ExitStack() as early:
            k_ring = sb("k_ring", [P, RING, HEADS * P], where=early)
            q_rows = sb("q_rows", [P, HEADS * P], where=early)
            dot_s = sb("dot_s", [P, PAGES * HEADS], where=early)
            acc = sb("acc", [P, HEADS * P], where=early)
            v_ring = sb("v_ring", [P, RING, HEADS * P], where=early)
            sb("pad", [P, 32], where=early)
            with ExitStack() as before_keep:
                k_third = sb("k_third", [P, HEADS * P], where=before_keep)
            keep = sb("keep", [P, CELLS], where=early)
            pool_sq = sb("pool_sq", [P, TOK], where=early)
            z_s = sb("z_s", [P, PAGES * HEADS], where=early)
            soft_s = sb("soft_s", [P, PAGES * HEADS], where=early)
            keep_s = sb("keep_s", [P, PAGES * HEADS], where=early)
            chunk_v = sb("chunk_v", [P, HEADS, SAMPLES], where=early)
        h = sb("h", [P, KT, TOK])
        H_KEYS, H_PAGES = 6, 12

        with ExitStack() as first:
            x_sq = sb("x_sq", [P, KT, TOK], where=first)
        with ExitStack() as early:
            q = sb("q", [P, HEADS, TOK], where=early)
            o_cm = sb("o_cm", [P, HEADS, TOK], where=early)
        with ExitStack() as late:
            proj = sb("proj", [P, KT, TOK], where=late)
        act_hi = sb("act_hi", [P, 2, FFN_GROUP, TOK], F32R)
        act_lo = sb("act_lo", [P, 2, FFN_GROUP, TOK], F32R)

        ones = sb("ones", [P, P])
        later = sb("later", [P, P])
        causal = sb("causal", [P, P])
        ident = sb("ident", [P, P])
        eps = sb("eps", [P, 1])
        one = sb("one", [P, 1])
        gain_mix = sb("gain_mix", [P, KT])
        gain_out = sb("gain_out", [P, KT])
        gain_ffn = sb("gain_ffn", [P, KT])
        gain_ple = sb("gain_ple", [P, KT])
        gain_q = sb("gain_q", [P, 1])
        gain_k = sb("gain_k", [P, 1])
        lng = sb("lng", [P, HEADS])
        lnb = sb("lnb", [P, HEADS])
        bias = sb("bias", [P, HEADS])
        w00 = sb("w00", [P, HEADS])
        table = sb("table", [1, N_PAGES], I32)
        dot_pad = sb("dot_pad", [P, 1])
        a_s = sb("a_s", [P, 3, PAGES * HEADS])
        x_r = sb("x_r", [P, TOK])
        sq = sb("sq", [P, TOK])
        cm_r = sb("cm_r", [P, TOK])
        sb_r = sb("sb_r", [P, TOK])

        with ExitStack() as early:
            y = sb("y", [P, 2, TOK], where=early)
            v_tok = sb("v_tok", [P, 4, P], where=early)
            with ExitStack() as mlp:
                vg = sb("vg", [P, TOK], where=mlp)
                ug = sb("ug", [P, TOK], where=mlp)
                w_mix = sb("w_mix", [P, HEADS, P], where=mlp)
                b_mix = sb("b_mix", [P, HEADS, P], where=mlp)
            k_head = sb("k_head", [P, TOK], where=early)
            z = sb("z", [P, CELLS], where=early)
            soft = sb("soft", [P, CELLS], where=early)
        y_gate = sb("y_gate", [P, TOK])
        y_up = sb("y_up", [P, TOK])
        h_sq = sb("h_sq", [P, 2, TOK])
        h_sum = sb("h_sum", [P, TOK])
        h_r = sb("h_r", [P, TOK])
        p_raw = sb("p_raw", [P, 2, TOK])

        out_ps = ctx.enter_context(nc.psum_tensor("out_ps", [P, 4, 512], F32))
        pair_ps = ctx.enter_context(nc.psum_tensor("pair_ps", [P, 2, 512], F32))
        tok_ps = ctx.enter_context(nc.psum_tensor("tok_ps", [P, 512], F32))
        mix_ps = ctx.enter_context(nc.psum_tensor("mix_ps", [P, 512], F32))

        def tile_ps(t):
            return out_ps[:, 2 * (t % 2):2 * (t % 2) + 2, 0:HALF]

        def k_slot(j):
            return k_third[:, :] if K_SLOT[j] == 2 else k_ring[:, K_SLOT[j], :]

        def halves(x):
            return x.rearrange("p (a n) -> p a n", a=2)

        pair = pair_ps[:, :, 0:HALF]
        pair_flat = pair_ps[:, :, :].rearrange("p a n -> p (a n)")

        x_in = [sem(f"x_in{i}") for i in range(len(X_PIECES) - 1)]
        w_in = [sem(f"w_in{i}") for i in range(2)]
        w_in_first = sem("w_in_first")
        gain_in = sem("gain_in")
        consts_in = sem("consts_in")
        table_in = sem("table_in")
        k_in = [sem(f"k_in{i}") for i in range(3)]
        v_in = [sem(f"v_in{i}") for i in range(RING)]
        q_rows_out = sem("q_rows_out")
        q_rows_in = sem("q_rows_in")
        h_in = [sem(f"h_in{i}") for i in range(3)]
        p_in = sem("p_in")
        k_out = sem("k_out")
        v_out = sem("v_out")
        y_out = sem("y_out")
        chunk_out = sem("chunk_out")
        hi_done = sem("hi_done")
        x_hi_done = sem("x_hi_done")
        sq_done = sem("sq_done")
        gelu_done = sem("gelu_done")
        ln_done = sem("ln_done")
        rstd_done = sem("rstd_done")
        root_done = sem("root_done")
        z_done = sem("z_done")
        soft_done = sem("soft_done")
        soft_s_done = sem("soft_s_done")
        a_done = sem("a_done")
        a_s_done = sem("a_s_done")
        act_step = sem("act_step")
        silu_done = sem("silu_done")
        act_hi_done = sem("act_hi_done")
        lo_done = sem("lo_done")
        x_lo_done = sem("x_lo_done")
        sum_done = sem("sum_done")
        out_read = sem("out_read")
        norm_done = sem("norm_done")
        centred = sem("centred")
        tok_read = sem("tok_read")
        mix_read = sem("mix_read")
        pair_read = sem("pair_read")
        r_done = sem("r_done")
        cm_done = sem("cm_done")
        k_used = sem("k_used")
        z_s_done = sem("z_s_done")
        keep_done = sem("keep_done")
        keep_s_done = sem("keep_s_done")
        arg_done = sem("arg_done")
        arg_s_done = sem("arg_s_done")
        masked = sem("masked")
        vec_step = sem("vec_step")
        act_done = sem("act_done")
        act_lo_done = sem("act_lo_done")
        h_final = sem("h_final")
        built = sem("built")
        pool_lo_done = sem("pool_lo_done")
        pool_sum_done = sem("pool_sum_done")
        pool_step = sem("pool_step")
        v_used = sem("v_used")
        h_sum_done = sem("h_sum_done")
        cm_sum_done = sem("cm_sum_done")
        sb_sum_done = sem("sb_sum_done")
        out_done = sem("out_done")
        x_sum_ready = sem("x_sum_ready")
        ms_ready = sem("ms_ready")
        mean_ready = sem("mean_ready")
        q_rows_ready = sem("q_rows_ready")
        turned = sem("turned")
        mixed = sem("mixed")
        z_ready = sem("z_ready")
        later_ready = sem("later_ready")
        later_s_ready = sem("later_s_ready")
        av_ready = sem("av_ready")
        o_s_ready = sem("o_s_ready")

        tok_jobs = []
        for u in range(U_OUT + 2):
            if u - 1 in SUM_END:
                tok_jobs.append(("later", u - 1))
            if U_MLP + 2 <= u <= U_KV and u % 2 == 0 or U_KV + 2 <= u <= U_OUT and u % 2 == 0:
                tok_jobs.append(("turn", u))
            if U_KV + 3 <= u <= U_OUT + 1 and u % 2 == 1:
                tok_jobs.append(("av", u))
            if u in REDUCE_END:
                tok_jobs.append(("reduce", u))

        turns = [u for kind, u in tok_jobs if kind == "turn"]

        def reads_before(kind, u):
            return tok_jobs.index((kind, u))

        block = ctx.enter_context(nc.Block())

        @block.sync
        def _(sp):
            def load_unit(u):
                if u in (2, 3):
                    sp.wait_ge(lo_done, u - 1)
                    sp.wait_ge(pool_lo_done, u - 1)
                elif u > 3:
                    sp.wait_ge(lo_done, 2 * u - 2 - POOL_LO)
                sp.dma_start(w_raw[:, u % 2, :], w_units[u]).then_inc(w_in[u % 2], 16)

            def load_x(i):
                tiles = slice(X_PIECES[i], X_PIECES[i + 1])
                sp.dma_start(h[:, tiles, :], x_t[:, tiles, :]).then_inc(x_in[i], 16)

            def load_q_rows(b):
                if b:
                    sp.wait_ge(k_used, HEADS * PAGES * b)
                sp.dma_start(q_rows[:, :], q_rows_dram[b:b + 1, :].to_broadcast([P, HEADS * P]))\
                    .then_inc(q_rows_in, 16)

            def load_k(j):
                if j == 0:
                    load_q_rows(0)
                elif (k_before(j) or 0) % PAGES == PAGES - 1:
                    load_q_rows(k_before(j) // PAGES + 1)
                page = sp.value_load(table[0:1, j:j + 1], min_val=0, max_val=N_PHYS - 1)
                if k_before(j) is not None:
                    sp.wait_ge(k_used, HEADS * (k_before(j) + 1))
                sp.dma_start(k_slot(j),
                             cache_k[bass.ds(page, 1), :, :].rearrange("a p n -> (a p) n"))\
                    .then_inc(k_in[K_SLOT[j]], 16)

            load_x(0)
            half = SLOTS * P // 2
            sp.dma_start(w_raw[:, 0, 0:half], w_units[0, :, 0:half]).then_inc(w_in_first, 16)
            load_x(1)
            sp.dma_start(w_raw[:, 0, half:], w_units[0, :, half:]).then_inc(w_in[0], 16)
            for i in range(2, len(X_PIECES) - 1):
                load_x(i)
            load_unit(1)
            sp.dma_start(table[:, :], page_table).then_inc(table_in, 16)
            for dst, src in ((gain_out[:, :], g_out), (gain_ffn[:, :], g_ffn),
                             (gain_ple[:, :], g_ple), (gain_q[:, :], g_q), (gain_k[:, :], g_k),
                             (lng[:, :], ln_g), (lnb[:, :], ln_b), (w_mix[:, :, :], w_s_t),
                             (b_mix[:, :, :], b_s.to_broadcast([P, HEADS, P])),
                             (bias[:, :], sb_bias.to_broadcast([P, HEADS])),
                             (w00[:, :], w_s00.to_broadcast([P, HEADS]))):
                sp.dma_start(dst, src).then_inc(consts_in, 16)
            load_unit(2)
            sp.wait_ge(table_in, 16)
            next_k = 0
            for u in range(U_FFN):
                if u < U_FFN - 1:
                    load_unit(u + 3)
                if u == K_PERIOD - 1:
                    sp.wait_ge(pair_read, 1)
                    sp.dma_start(q_rows_dram, acc[0:SAMPLES, :]).then_inc(q_rows_out, 16)
                    sp.wait_ge(q_rows_out, 16)
                while u >= K_PERIOD - 1 and next_k < N_PAGES and \
                        (k_before(next_k) is None or k_period(k_before(next_k)) <= u):
                    load_k(next_k)
                    next_k += 1
                if U_KV + 2 <= u <= U_OUT and u % 2 == 0:
                    i = (u - U_KV - 2) // 2
                    sp.wait_ge(norm_done, 2 * HEADS + i + 1)
                    sp.dma_start(k_t[i], k_head[:, :]).then_inc(k_out, 16)
                    sp.wait_ge(out_read, U_KV + 2 * i + 2)
                    sp.dma_start(v_t[i], y[:, 1, :]).then_inc(v_out, 16)
                if u == U_KV + 2:
                    sp.wait_ge(cm_done, HEADS)
                    sp.dma_start(chunk_v_t, chunk_v[:, :, :]).then_inc(chunk_out, 16)
                if u == LAST_K[-1] + 3:
                    sp.wait_ge(z_s_done, SAMPLES)
                    sp.dma_start(h[:, 0:H_KEYS, :], x_t[:, 0:H_KEYS, :]).then_inc(h_in[0], 16)
                if u == REDUCE_END[-1] + 2:
                    sp.wait_ge(tok_read, reads_before("reduce", REDUCE_END[-1]) + 1)
                    sp.dma_start(h[:, H_KEYS:H_PAGES, :], x_t[:, H_KEYS:H_PAGES, :]).then_inc(h_in[1], 16)
                if u == U_OUT + 4:
                    sp.wait_ge(av_ready, HEADS)
                    sp.wait_ge(sb_sum_done, 1)
                    sp.dma_start(h[:, H_PAGES:KT, :], x_t[:, H_PAGES:KT, :]).then_inc(h_in[2], 16)
                if u == U_OUT_SB:
                    sp.dma_start(p_raw[:, :, :], p_t).then_inc(p_in, 16)
            with sp.Fori((U_FFN + 2) // 2, UNITS // 2) as i:
                for s in range(2):
                    sp.wait_ge(lo_done, 4 * i + (2 * s - 2 - POOL_LO))
                    sp.dma_start(w_raw[:, s, :], w_units[bass.ds(2 * i + s, 1), :, :]
                                 .rearrange("a p n -> (a p) n")).then_inc(w_in[s], 16)
            for m in range(KT):
                sp.wait_ge(h_final, KT + m + 1)
                sp.dma_start(y_t[:, m, :], h[:, m, :]).then_inc(y_out, 16)
            sp.wait_ge(y_out, 16 * KT)
            sp.wait_ge(k_out, 16 * HEADS)
            sp.wait_ge(v_out, 16 * HEADS)
            sp.wait_ge(chunk_out, 16)

        @block.gpsimd
        def _(pool):
            steps = [0]

            def chained(ins):
                steps[0] += 1
                ins.then_inc(pool_step, 1)
                pool.wait_ge(pool_step, steps[0])

            chained(pool.memset(ones[:, :], 1.0))
            chained(pool.memset(eps[:, :], EPS))
            chained(pool.memset(cm_r[:, :], 0.0))
            chained(pool.memset(sb_r[:, :], 0.0))
            chained(pool.affine_select(out=later[:, :], in_=ones[:, :], compare_op=ALU.is_gt, fill=0.0,
                                       base=0, pattern=[[-1, P]], channel_multiplier=1))
            chained(pool.affine_select(out=causal[:, :], in_=ones[:, :], compare_op=ALU.is_gt, fill=0.0,
                                       base=0, pattern=[[1, P]], channel_multiplier=-1))
            chained(pool.affine_select(out=ident[:, :], in_=ones[:, :], compare_op=ALU.is_equal,
                                       fill=0.0, base=0, pattern=[[-1, P]], channel_multiplier=1))
            pool.memset(one[:, :], 1.0).then_inc(built, 1)

            def low_w(u, j):
                pool.wait_ge(hi_done, 2 * u + j + 1)
                cols = slice(j * 8 * P, (j + 1) * 8 * P)
                pool.tensor_tensor(w_lo[:, u, cols], w_raw[:, u, cols], w_hi[:, u, cols], ALU.subtract)\
                    .then_inc(pool_lo_done, 1)

            def square_input(k):
                ins = pool.tensor_tensor(x_sq[:, k, :], h[:, k, :], h[:, k, :], ALU.mult)
                chained(ins)
                if k:
                    ins = pool.tensor_tensor(x_sq[:, 0, :], x_sq[:, 0, :], x_sq[:, k, :], ALU.add)
                    if k == POOL_SQUARES - 1:
                        ins.then_inc(pool_sum_done, 1)
                    else:
                        chained(ins)

            pool.wait_ge(x_in[0], 16)
            square_input(0)
            low_w(0, 1)
            pool.wait_ge(x_in[1], 16)
            square_input(1)
            square_input(2)
            square_input(3)
            pool.wait_ge(x_in[2], 16)
            square_input(4)
            low_w(1, 1)
            square_input(5)
            pool.wait_ge(consts_in, CONSTS * 16)
            pool.affine_select(out=w_mix[:, :, :], in_=w_mix[:, :, :], compare_op=ALU.is_ge, fill=0.0,
                               base=0, pattern=[[0, HEADS], [1, P]], channel_multiplier=-1)\
                .then_inc(built, 1)

            def load_v(j):
                page = pool.value_load(table[0:1, j:j + 1], min_val=0, max_val=N_PHYS - 1)
                if j >= RING:
                    pool.wait_ge(v_used, j - RING + 1)
                pool.dma_start(v_ring[:, j % RING, :],
                               cache_v[bass.ds(page, 1), :, :].rearrange("a p n -> (a p) n"))\
                    .then_inc(v_in[j % RING], 16)

            def add_page(j):
                b, pg = divmod(j, PAGES)
                pool.wait_ge(v_in[j % RING], 16 * (j // RING + 1))
                values = v_ring[:, j % RING, :].rearrange("p (h d) -> p h d", h=HEADS)
                weights = a_s[:, b % 3, pg * HEADS:(pg + 1) * HEADS].unsqueeze(2).to_broadcast([P, HEADS, P])
                if pg == 0:
                    if b == 0:
                        pool.wait_ge(q_rows_out, 16)
                    else:
                        pool.wait_ge(o_s_ready, b)
                    pool.wait_ge(a_s_done, b + 1)
                    pool.tensor_tensor(acc[:, :].rearrange("p (h d) -> p h d", h=HEADS), values, weights,
                                       ALU.mult).then_inc(v_used, 1)
                else:
                    chained(pool.tensor_tensor(values, values, weights, ALU.mult))
                    pool.wait_ge(v_used, j)
                    pool.tensor_tensor(acc[:, :], acc[:, :], v_ring[:, j % RING, :], ALU.add)\
                        .then_inc(v_used, 1)
                if j + RING < N_PAGES:
                    load_v(j + RING)

            def add_squares(x, total, cols, done=pool_step):
                chained(pool.tensor_tensor(pool_sq[:, cols], x, x, ALU.mult))
                ins = pool.tensor_tensor(total[:, cols], total[:, cols], pool_sq[:, cols], ALU.add)
                if done is pool_step:
                    chained(ins)
                else:
                    ins.then_inc(done, 1)
                    pool.wait_ge(done, 1)

            jobs = [(SUM_END[j // PAGES] + 1 + j % PAGES * 0.25, "page", j) for j in range(N_PAGES)]
            jobs += [(U_MLP + 3.5 + 2 * i, "mlp", i) for i in range(HEADS)]
            jobs += [(U_KV + 3.7 + 2 * i, "attention", i) for i in range(HEADS)]
            pool.wait_ge(table_in, 16)
            pool.wait_ge(x_lo_done, KT)
            pool.wait_ge(sq_done, X_SQUARES)
            for j in range(RING):
                load_v(j)
            for _, kind, i in sorted(jobs):
                if kind == "page":
                    add_page(i)
                elif kind == "mlp":
                    pool.wait_ge(cm_done, i + 1)
                    add_squares(o_cm[:, i, :], cm_r, slice(0, TOK), cm_sum_done if i == HEADS - 1 else pool_step)
                else:
                    pool.wait_ge(tok_read, reads_before("av", U_KV + 3 + 2 * i) + 1)
                    add_squares(q[:, i, 0:PROMPT], sb_r, slice(0, PROMPT))
            pool.wait_ge(tok_read, reads_before("reduce", REDUCE_END[-1]) + 1)
            for i in range(HEADS):
                add_squares(q[:, i, PROMPT:TOK], sb_r, slice(PROMPT, TOK),
                            sb_sum_done if i == HEADS - 1 else pool_step)

            for n in range(2):
                if n:
                    pool.wait_ge(x_sum_ready, 4)
                for k in range(KT):
                    pool.wait_ge(sq_done, X_SQUARES + 3 * HEADS + n * KT + k + 1)
                    if k:
                        ins = pool.tensor_tensor(h_sum[:, :], h_sum[:, :], h_sq[:, k % 2, :], ALU.add)
                    else:
                        ins = pool.tensor_copy(h_sum[:, :], h_sq[:, 0, :])
                    ins.then_inc(h_sum_done, 1)
                    pool.wait_ge(h_sum_done, n * KT + k + 1)

        @block.scalar
        def _(act):
            act.dma_start(gain_mix[:, :], g_mix).then_inc(gain_in, 16)

            steps = [0]

            def chained(ins):
                steps[0] += 1
                ins.then_inc(act_step, 1)
                act.wait_ge(act_step, steps[0])

            def high_w(u, j):
                cols = slice(j * 8 * P, (j + 1) * 8 * P)
                act.activation(w_hi[:, u % 2, cols], w_raw[:, u % 2, cols], ACT.Copy).then_inc(hi_done, 1)

            def split_w(u, it=0, landed=0, tiles=0):
                act.wait_ge(w_in[u % 2], it * landed + 16 * (u // 2 + 1))
                if u >= 2:
                    act.wait_ge(out_done, it * tiles + tiles_before(u - 1))
                for j in range(2):
                    high_w(u, j)

            def split(dst, src, gain):
                act.activation(dst, src, ACT.Copy, scale=gain).then_inc(x_hi_done, 1)

            def root(n, features, dst):
                act.wait_ge(x_sum_ready, n + 1)
                act.activation(halves(dst), pair, ACT.Sqrt, bias=eps[:, 0:1], scale=1.0 / features)\
                    .then_inc(root_done, 1)

            def rstd(n):
                act.wait_ge(ms_ready, n + 1)
                act.activation(halves(sq[:, :]), pair, ACT.Ln, bias=eps[:, 0:1], scale=1.0 / P)\
                    .then_inc(ln_done, 1)
                act.wait_ge(ln_done, n + 1)
                act.activation(sq[:, :], sq[:, :], ACT.Exp, scale=-0.5).then_inc(rstd_done, 1)

            def square_head(n, src):
                if n:
                    act.wait_ge(norm_done, n)
                act.activation(sq[:, :], src, ACT.Square).then_inc(sq_done, 1)

            def logits(i):
                act.wait_ge(z_ready, i + 1)
                if i:
                    act.wait_ge(av_ready, i)
                chained(act.activation(z[:, 0:1024], pair_flat, ACT.Identity, bias=bias[:, i:i + 1],
                                       scale=SCALE))
                act.activation(z[:, 1024:CELLS], mix_ps[:, 0:CELLS - 1024], ACT.Identity,
                               bias=bias[:, i:i + 1], scale=SCALE).then_inc(z_done, 1)

            def take_turned(u):
                act.wait_ge(turned, turns.index(u) + 1)
                act.activation(v_tok[:, :, :].rearrange("p c n -> p (c n)"), tok_ps[:, :], ACT.Copy)\
                    .then_inc(tok_read, 1)

            def take_attention(i):
                act.wait_ge(av_ready, i + 1)
                act.activation(q[:, i, 0:PROMPT], tok_ps[:, :], ACT.Copy).then_inc(tok_read, 1)

            def soften(jobs):
                for l, zz, _ in jobs:
                    chained(act.activation(l, zz, ACT.Abs))
                for l, _, _ in jobs:
                    chained(act.activation(l, l, ACT.Exp, scale=-1.0))
                for l, _, done in jobs:
                    act.activation(l, l, ACT.Ln, bias=one[:, 0:1]).then_inc(done, 1)

            def weights_of_sample(u):
                if u - 1 in SUM_END:
                    b = SUM_END.index(u - 1)
                    act.wait_ge(arg_s_done, b + 1)
                    if b >= 3:
                        act.wait_ge(v_used, PAGES * (b - 2))
                    act.activation(a_s[:, b % 3, :], z_s[:, :], ACT.Exp).then_inc(a_s_done, 1)

            def sample_job(u):
                if u not in SUM_END:
                    return []
                act.wait_ge(z_s_done, SUM_END.index(u) + 1)
                return [(soft_s[:, :], z_s[:, :], soft_s_done)]

            def square_residual(n, k):
                if k >= 2:
                    act.wait_ge(h_sum_done, n + k - 1)
                act.activation(h_sq[:, k % 2, :], h[:, k, :], ACT.Square).then_inc(sq_done, 1)

            act.wait_ge(built, 1)
            act.activation(y[:, 0, 0:1], one[:, 0:1], ACT.Copy)
            act.wait_ge(gain_in, 16)
            for k in range(KT):
                if k in X_PIECES:
                    act.wait_ge(x_in[X_PIECES.index(k)], 16)
                split(x_hi[:, k, :], h[:, k, :], gain_mix[:, k:k + 1])
                if k == 1:
                    act.wait_ge(w_in_first, 16)
                    high_w(0, 0)
                if k == 3:
                    act.wait_ge(w_in[0], 16)
                    high_w(0, 1)
            split_w(1)
            for k in range(POOL_SQUARES, KT):
                act.activation(x_sq[:, k, :], h[:, k, :], ACT.Square).then_inc(sq_done, 1)
            split_w(2)
            chained(act.activation(y[:, 0, 1:2], one[:, 0:1], ACT.Sqrt))
            act.wait_ge(built, 2)
            root(0, D_MODEL, x_r[:, :])

            for u in range(1, U_FFN):
                t = u - 1
                if u <= U_MLP:
                    if u == 2:
                        split_w(u + 1)
                    act.wait_ge(out_read, t + 1)
                    square_head(t, y[:, t % 2, :])
                    if u > 2:
                        split_w(u + 1)
                    rstd(t)
                elif u <= U_KV and u % 2 == 1:
                    i = (u - U_MLP - 1) // 2
                    act.wait_ge(out_read, t + 1)
                    if i:
                        act.wait_ge(tok_read, reads_before("turn", U_MLP + 2 * i) + 1)
                    act.activation(vg[:, :], y[:, t % 2, :], ACT.Gelu).then_inc(gelu_done, 1)
                    split_w(u + 1)
                    weights_of_sample(u)
                    act.wait_ge(centred, i + 1)
                    square_head(HEADS + i, vg[:, :])
                elif u <= U_KV:
                    i = (u - U_MLP - 2) // 2
                    rstd(HEADS + i)
                    soften(sample_job(u))
                    split_w(u + 1)
                    if i:
                        act.wait_ge(mixed, i)
                    take_turned(u)
                    act.wait_ge(out_read, t + 1)
                    if i:
                        act.wait_ge(cm_done, i)
                    act.activation(ug[:, :], y[:, t % 2, :], ACT.Gelu).then_inc(gelu_done, 1)
                elif u < U_OUT and u % 2 == 1:
                    i = (u - U_KV - 1) // 2
                    split_w(u + 1)
                    act.wait_ge(out_read, t + 1)
                    square_head(2 * HEADS + i, y[:, t % 2, :])
                    if i:
                        act.wait_ge(arg_done, i)
                        act.activation(z[:, :], z[:, :], ACT.Exp).then_inc(a_done, 1)
                        weights_of_sample(u)
                    rstd(2 * HEADS + i)
                    if not i:
                        weights_of_sample(u)
                    if i:
                        take_attention(i - 1)
                elif u <= U_OUT:
                    i = (u - U_KV - 2) // 2
                    if u == U_OUT:
                        act.wait_ge(out_done, U_OUT)
                        for k in range(HEADS):
                            split(x_hi[:, HEADS + k, :], o_cm[:, k, :], gain_out[:, HEADS + k:HEADS + k + 1])
                    split_w(u + 1)
                    logits(i)
                    act.wait_ge(z_done, i + 1)
                    soften([(soft[:, :], z[:, :], soft_done)] + sample_job(u))
                    if i:
                        act.wait_ge(av_ready, i)
                    else:
                        act.wait_ge(mixed, HEADS)
                    take_turned(u)
                elif u == U_OUT + 2:
                    split_w(u + 1)
                    act.wait_ge(arg_done, HEADS)
                    act.activation(z[:, :], z[:, :], ACT.Exp).then_inc(a_done, 1)
                else:
                    split_w(u + 1)
                if u == U_OUT + 3:
                    take_attention(HEADS - 1)
                if u > U_OUT_SB:
                    for k in range(2 * (u - U_OUT_SB - 1), 2 * (u - U_OUT_SB)):
                        act.wait_ge(h_final, k + 1)
                        if k < 8:
                            split(x_hi[:, 8 + k, :], h[:, k, :], gain_ffn[:, k:k + 1])
                        square_residual(0, k)
                if u == CM_ROOT:
                    root(1, HEADS * P, cm_r[:, :])
                if u == SB_ROOT:
                    root(2, HEADS * P, sb_r[:, :])
                if u in SB_SPLITS:
                    for k in SB_SPLITS[u]:
                        split(x_hi[:, k, :], q[:, k, :], gain_out[:, k:k + 1])

            act.wait_ge(out_done, T_FFN)
            for k in range(8, KT):
                if k >= KT - 2:
                    act.wait_ge(h_final, k + 1)
                split(x_hi[:, k - 8, :], h[:, k, :], gain_ffn[:, k:k + 1])
            for k in range(KT - 2, KT):
                square_residual(0, k)

            def gate_up(u, n, t, par, g, it=0):
                split_w(u + 1, it, 16 * CHUNK_UNITS, 2 * CHUNK_TILES)
                if u == U_FFN:
                    root(3, D_MODEL, h_r[:, :])
                act.wait_ge(out_read, it * (2 * CHUNK_TILES) + (t + 1))
                act.activation(y_gate[:, :], y_gate[:, :], ACT.Silu).then_inc(silu_done, 1)
                split_w(u + 2, it, 16 * CHUNK_UNITS, 2 * CHUNK_TILES)
                act.wait_ge(act_done, it * (2 * FFN_GROUP) + (n + 1))
                act.activation(act_hi[:, par, g, :], y_up[:, :], ACT.Copy).then_inc(act_hi_done, 1)

            for g in range(FFN_GROUP):
                gate_up(U_FFN + 2 * g, g, T_FFN + 2 * g, 0, g)
            with act.Fori(0, (FFN_CHUNKS - 1) // 2) as it:
                for half in range(2):
                    u0 = U_LOOP + half * CHUNK_UNITS
                    for g in range(FFN_GROUP):
                        gate_up(u0 + 2 * g, FFN_GROUP * (1 + half) + g, tiles_before(u0 + 2 * g), 1 - half, g, it)
                    for g in range(FFN_GROUP):
                        split_w(u0 + 2 * FFN_GROUP + g + 1, it, 16 * CHUNK_UNITS, 2 * CHUNK_TILES)

            act.wait_ge(p_in, 16)
            for k in range(2):
                act.activation(x_hi[:, k, :], p_raw[:, k, :], ACT.Copy).then_inc(x_hi_done, 1)
            for g in range(FFN_GROUP):
                split_w(U_LAST_DOWN + g + 1)
                for k in range(4 * g, 4 * g + 4):
                    act.wait_ge(out_read, T_LAST_DOWN + k + 1)
                    if k >= 2:
                        split(x_hi[:, k, :], h[:, k, :], gain_ple[:, k:k + 1])
                    square_residual(KT, k)
            split_w(U_PROJ + 1)
            split_w(U_GATE)
            act.wait_ge(out_done, T_GATE)
            for k in range(2):
                split(x_hi[:, k, :], h[:, k, :], gain_ple[:, k:k + 1])
            root(4, D_MODEL, h_r[:, :])
            for m in range(KT):
                if U_GATE + m + 1 < UNITS:
                    split_w(U_GATE + m + 1)
                act.wait_ge(out_read, T_GATE + m + 1)
                act.activation(y_gate[:, :], y_gate[:, :], ACT.Sigmoid).then_inc(silu_done, 1)

        @block.vector
        def _(dve):
            count = {}

            def chained(ins, done=vec_step):
                count[done.name] = count.get(done.name, 0) + 1
                ins.then_inc(done, 1)
                dve.wait_ge(done, count[done.name])

            def low_w(u, j, it=0):
                dve.wait_ge(hi_done, it * (4 * CHUNK_UNITS) + (2 * u + j + 1))
                cols = slice(j * 8 * P, (j + 1) * 8 * P)
                dve.tensor_tensor(w_lo[:, u % 2, cols], w_raw[:, u % 2, cols], w_hi[:, u % 2, cols],
                                  ALU.subtract).then_inc(lo_done, 1)

            n_split = [0]

            def low_x(slot, src, gain):
                n_split[0] += 1
                dve.wait_ge(x_hi_done, n_split[0])
                dve.scalar_tensor_tensor(out=x_lo[:, slot, :], in0=src, scalar=gain, in1=x_hi[:, slot, :],
                                         op0=ALU.mult, op1=ALU.subtract).then_inc(x_lo_done, 1)

            def invert(n, dst):
                dve.wait_ge(root_done, n + 1)
                chained(dve.reciprocal(dst, dst), r_done)

            def normalise(n, dst, src, gain, done=norm_done):
                dve.wait_ge(rstd_done, n + 1)
                chained(dve.scalar_tensor_tensor(out=dst, in0=src, scalar=gain, in1=sq[:, :],
                                                 op0=ALU.mult, op1=ALU.mult), done)

            def take(t, dst, r):
                dve.wait_ge(out_done, t + 1)
                chained(dve.tensor_tensor(halves(dst), tile_ps(t), halves(r), ALU.mult), out_read)

            def score_page(j):
                b, pg = divmod(j, PAGES)
                if pg == 0:
                    dve.wait_ge(q_rows_in, 16 * (b + 1))
                dve.wait_ge(k_in[K_SLOT[j]], 16 * (k_turn(j) + 1))
                for hd in range(HEADS):
                    cols = slice(hd * P, (hd + 1) * P)
                    at = pg * HEADS + hd
                    dve.tensor_tensor_reduce(k_slot(j)[:, cols], k_slot(j)[:, cols],
                                             q_rows[:, cols], 1.0, 0.0, ALU.mult, ALU.add,
                                             dot_s[:, at:at + 1]).then_inc(k_used, 1)
                if pg == PAGES - 1:
                    dve.wait_ge(k_used, HEADS * (j + 1))
                    if b:
                        dve.wait_ge(a_s_done, b)
                    chained(dve.scalar_tensor_tensor(
                        out=z_s[:, :].rearrange("p (g h) -> p g h", h=HEADS),
                        in0=dot_s[:, :].rearrange("p (g h) -> p g h", h=HEADS), scalar=SCALE,
                        in1=bias[:, :].unsqueeze(1).to_broadcast([P, PAGES, HEADS]),
                        op0=ALU.mult, op1=ALU.add), z_s_done)

            def keep_sample(b):
                dve.wait_ge(soft_s_done, b + 1)
                chained(dve.scalar_tensor_tensor(out=keep_s[:, :], in0=z_s[:, :], scalar=0.0,
                                                 in1=soft_s[:, :], op0=ALU.max, op1=ALU.add))
                chained(dve.scalar_tensor_tensor(out=z_s[:, :], in0=z_s[:, :], scalar=0.0,
                                                 in1=soft_s[:, :], op0=ALU.min, op1=ALU.subtract))

                def page(x, pg):
                    return x[:, pg * HEADS:(pg + 1) * HEADS]

                chained(dve.tensor_copy(page(soft_s, PAGES - 2), page(keep_s, PAGES - 1)))
                for pg in range(PAGES - 3, -1, -1):
                    chained(dve.tensor_tensor(page(soft_s, pg), page(soft_s, pg + 1), page(keep_s, pg + 1),
                                              ALU.add), keep_s_done if pg == 0 else vec_step)

            def take_reduced(u):
                if u - 1 in REDUCE_END:
                    b = REDUCE_END.index(u - 1)
                    dve.wait_ge(o_s_ready, b + 1)
                    count[tok_read.name] = reads_before("reduce", u - 1)
                    chained(dve.tensor_copy(q[:, :, PROMPT + b], tok_ps[:, P:P + HEADS]), tok_read)

            def weigh_sample(b):
                dve.wait_ge(later_s_ready, b + 1)
                count[tok_read.name] = reads_before("later", SUM_END[b])
                chained(dve.tensor_tensor(z_s[:, :], z_s[:, :], tok_ps[:, 0:PAGES * HEADS], ALU.subtract),
                        tok_read)
                chained(dve.tensor_copy(dot_pad[:, :], z_s[:, 0:1]), arg_s_done)

            def diagonal(x):
                return x[:, 0:PROMPT].rearrange("p (c n) -> p c n", c=4)

            causal4 = causal[:, :].unsqueeze(1).to_broadcast([P, 4, P])

            def keep_head(i):
                dve.wait_ge(soft_done, i + 1)
                chained(dve.scalar_tensor_tensor(out=keep[:, :], in0=z[:, :], scalar=0.0, in1=soft[:, :],
                                                 op0=ALU.max, op1=ALU.add))
                chained(dve.scalar_tensor_tensor(out=z[:, :], in0=z[:, :], scalar=0.0, in1=soft[:, :],
                                                 op0=ALU.min, op1=ALU.subtract))
                chained(dve.tensor_tensor(diagonal(keep), diagonal(keep), causal4, ALU.mult))
                chained(dve.tensor_tensor(soft[:, 0:P], keep[:, DIAG(3)], keep[:, 896:1024], ALU.add))
                chained(dve.tensor_tensor(soft[:, P:2 * P], keep[:, DIAG(2)], keep[:, 1024:1152], ALU.add))
                chained(dve.tensor_tensor(soft[:, 2 * P:3 * P], soft[:, 0:P], keep[:, 1152:1280], ALU.add),
                        keep_done)

            def exponents(i):
                dve.wait_ge(later_ready, i + 1)
                chained(dve.tensor_tensor(z[:, 0:1024], z[:, 0:1024], pair_flat, ALU.subtract), pair_read)
                chained(dve.tensor_tensor(z[:, 1024:CELLS], z[:, 1024:CELLS], mix_ps[:, 0:CELLS - 1024],
                                          ALU.subtract), arg_done)

            def mask_weights(i):
                dve.wait_ge(a_done, i + 1)
                chained(dve.tensor_tensor(diagonal(z), diagonal(z), causal4, ALU.mult), masked)

            def out_tile(n, r):
                m = n % KT
                if n in (0, H_KEYS, H_PAGES):
                    dve.wait_ge(h_in[(0, H_KEYS, H_PAGES).index(n)], 16)
                take(T_OUT + n, sq[:, :], r[:, :])
                chained(dve.tensor_tensor(h[:, m, :], h[:, m, :], sq[:, :], ALU.add),
                        h_final if n >= KT else vec_step)

            dve.wait_ge(gain_in, 16)
            for k in range(KT):
                low_x(k, h[:, k, :], gain_mix[:, k:k + 1])
                if k == 1:
                    low_w(0, 0)
            low_w(1, 0)
            first = POOL_SQUARES
            for k in range(first + 2, KT, 2):
                dve.wait_ge(sq_done, k + 2 - first)
                chained(dve.tensor_tensor(x_sq[:, first:first + 2, :], x_sq[:, first:first + 2, :],
                                          x_sq[:, k:k + 2, :], ALU.add))
            chained(dve.tensor_tensor(x_r[:, :], x_sq[:, first, :], x_sq[:, first + 1, :], ALU.add))
            dve.wait_ge(pool_sum_done, 1)
            chained(dve.tensor_tensor(x_r[:, :], x_r[:, :], x_sq[:, 0, :], ALU.add), sum_done)
            low_w(2, 0)
            low_w(2, 1)
            dve.wait_ge(built, 2)
            invert(0, x_r[:, :])

            for u in range(1, U_FFN):
                t = u - 1
                pages = list(k_pages(u))

                def score_next(early=False):
                    if pages and not (early and pages[0] % PAGES in (0, PAGES - 1)):
                        score_page(pages.pop(0))

                if u <= U_OUT:
                    if t > U_KV and t % 2 == 1 and t > U_KV + 2:
                        dve.wait_ge(v_out, 16 * ((t - U_KV - 1) // 2))
                    take(t, y[:, t % 2, :], x_r[:, :])
                else:
                    out_tile(2 * (u - U_OUT) - 1, cm_r if u <= U_OUT_SB else sb_r)

                if u <= U_MLP:
                    if u > 1:
                        low_w(u + 1, 0)
                        low_w(u + 1, 1)
                    normalise(t, q[:, t, :], y[:, t % 2, :], gain_q[:, 0:1])
                elif u <= U_KV + 1 and u % 2 == 1:
                    if u == U_MLP + 1:
                        dve.wait_ge(q_rows_ready, 1)
                        chained(dve.tensor_copy(acc[0:SAMPLES, :], pair_flat[0:SAMPLES, :]), pair_read)
                    else:
                        i = (u - U_MLP - 3) // 2
                        dve.wait_ge(mixed, i + 1)
                        chained(dve.tensor_tensor(
                            o_cm[:, i, 0:PROMPT].rearrange("p (c n) -> p c n", c=4),
                            mix_ps[:, :].rearrange("p (c n) -> p c n", c=4),
                            b_mix[:, i, :].unsqueeze(1).to_broadcast([P, 4, P]), ALU.add), mix_read)
                        dve.wait_ge(gelu_done, 2 * i + 2)
                        chained(dve.tensor_tensor(o_cm[:, i, :], o_cm[:, i, :], ug[:, :], ALU.mult), cm_done)
                    score_next(early=True)
                    low_w(u + 1, 0)
                    low_w(u + 1, 1)
                    take_reduced(u)
                    if u - 1 in SUM_END:
                        weigh_sample(SUM_END.index(u - 1))
                    if u < U_KV:
                        i = (u - U_MLP - 1) // 2
                        dve.wait_ge(mean_ready, i + 1)
                        dve.wait_ge(gelu_done, 2 * i + 1)
                        chained(dve.scalar_tensor_tensor(out=halves(vg[:, :]), in0=pair, scalar=-1.0 / P,
                                                         in1=halves(vg[:, :]), op0=ALU.mult, op1=ALU.add),
                                centred)
                elif u <= U_KV:
                    i = (u - U_MLP - 2) // 2
                    score_next(early=True)
                    normalise(HEADS + i, vg[:, :], vg[:, :], lng[:, i:i + 1], vec_step)
                    chained(dve.tensor_scalar(vg[:, :], vg[:, :], lnb[:, i:i + 1], None, ALU.add), norm_done)
                    chained(dve.tensor_copy(chunk_v[:, i, :], vg[:, PROMPT:TOK]))
                    chained(dve.tensor_scalar(o_cm[:, i, PROMPT:TOK], vg[:, PROMPT:TOK], w00[:, i:i + 1],
                                              b_mix[:, i, 0:1], ALU.mult, ALU.add))
                    low_w(u + 1, 0)
                    low_w(u + 1, 1)
                    take_reduced(u)
                elif u <= U_OUT and u % 2 == 0:
                    i = (u - U_KV - 2) // 2
                    if u == U_OUT:
                        for k in range(HEADS):
                            low_x(HEADS + k, o_cm[:, k, :], gain_out[:, HEADS + k:HEADS + k + 1])
                    low_w(u + 1, 0)
                    low_w(u + 1, 1)
                    take_reduced(u)
                    score_next()
                    if u < U_OUT:
                        keep_head(i)
                    if u in SUM_END:
                        keep_sample(SUM_END.index(u))
                else:
                    if u > U_OUT:
                        low_w(u + 1, 0)
                        low_w(u + 1, 1)
                        take_reduced(u)
                    if u == U_OUT + 1:
                        keep_head(HEADS - 1)
                if u == U_OUT + 2:
                    exponents(HEADS - 1)
                    mask_weights(HEADS - 1)
                if U_KV < u < U_OUT and u % 2 == 1:
                    i = (u - U_KV - 1) // 2
                    if u > U_KV + 1:
                        low_w(u + 1, 0)
                        low_w(u + 1, 1)
                        take_reduced(u)
                    if i:
                        exponents(i - 1)
                        if u - 1 in SUM_END:
                            weigh_sample(SUM_END.index(u - 1))
                        score_next()
                        mask_weights(i - 1)
                    if i:
                        dve.wait_ge(k_out, 16 * i)
                    normalise(2 * HEADS + i, k_head[:, :], y[:, t % 2, :], gain_k[:, 0:1])
                if u == CM_ROOT:
                    invert(1, cm_r[:, :])
                if u == SB_ROOT:
                    invert(2, sb_r[:, :])
                if u in SB_SPLITS:
                    for k in SB_SPLITS[u]:
                        low_x(k, q[:, k, :], gain_out[:, k:k + 1])
                if u in SUM_END and u <= U_KV:
                    keep_sample(SUM_END.index(u))
                while pages:
                    score_next()
                if u > U_OUT_SB:
                    for k in range(2 * (u - U_OUT_SB - 1), 2 * (u - U_OUT_SB)):
                        if k < 8:
                            low_x(8 + k, h[:, k, :], gain_ffn[:, k:k + 1])
                if u >= U_OUT:
                    out_tile(2 * (u - U_OUT), cm_r if u < U_OUT_SB else sb_r)

            out_tile(2 * KT - 1, sb_r)
            for k in range(8, KT):
                low_x(k - 8, h[:, k, :], gain_ffn[:, k:k + 1])

            def take_loop(t, dst, it):
                dve.wait_ge(out_done, it * (2 * CHUNK_TILES) + (t + 1))
                dve.tensor_tensor(halves(dst), tile_ps(t), halves(h_r[:, :]), ALU.mult).then_inc(out_read, 1)

            def gate_up(u, n, t, par, g, it=0):
                n_it = it * (2 * FFN_GROUP)
                low_w(u + 1, 0, it)
                low_w(u + 1, 1, it)
                if u == U_FFN:
                    invert(3, h_r[:, :])
                else:
                    dve.wait_ge(act_lo_done, n_it + n)
                take_loop(t, y_gate[:, :], it)
                low_w(u + 2, 0, it)
                low_w(u + 2, 1, it)
                take_loop(t + 1, y_up[:, :], it)
                dve.wait_ge(out_read, it * (2 * CHUNK_TILES) + (t + 2))
                dve.wait_ge(silu_done, n_it + (n + 1))
                dve.tensor_tensor(y_up[:, :], y_up[:, :], y_gate[:, :], ALU.mult).then_inc(act_done, 1)
                dve.wait_ge(act_hi_done, n_it + (n + 1))
                dve.tensor_tensor(act_lo[:, par, g, :], y_up[:, :], act_hi[:, par, g, :], ALU.subtract)\
                    .then_inc(act_lo_done, 1)

            def down_tile(t, m, it=0):
                dve.wait_ge(out_done, it * (2 * CHUNK_TILES) + (t + 1))
                dve.wait_ge(out_read, it * (2 * CHUNK_TILES) + t)
                dve.tensor_tensor(halves(h[:, m, :]), halves(h[:, m, :]), tile_ps(t), ALU.add)\
                    .then_inc(out_read, 1)

            for g in range(FFN_GROUP):
                gate_up(U_FFN + 2 * g, g, T_FFN + 2 * g, 0, g)
            with dve.Fori(0, (FFN_CHUNKS - 1) // 2) as it:
                for half in range(2):
                    u0 = U_LOOP + half * CHUNK_UNITS
                    for g in range(FFN_GROUP):
                        gate_up(u0 + 2 * g, FFN_GROUP * (1 + half) + g, tiles_before(u0 + 2 * g), 1 - half, g, it)
                    for g in range(FFN_GROUP):
                        u = u0 + 2 * FFN_GROUP + g
                        for j in range(4):
                            if j < 2:
                                low_w(u + 1, j, it)
                            down_tile(tiles_before(u) + j, 4 * g + j, it)

            for k in range(2):
                n_split[0] += 1
                dve.wait_ge(x_hi_done, n_split[0])
                dve.tensor_tensor(x_lo[:, k, :], p_raw[:, k, :], x_hi[:, k, :], ALU.subtract)\
                    .then_inc(x_lo_done, 1)
            for k in range(KT):
                if k % 4 < 2:
                    low_w(U_LAST_DOWN + k // 4 + 1, k % 4)
                down_tile(T_LAST_DOWN + k, k)
                if k >= 3:
                    low_x(k - 1, h[:, k - 1, :], gain_ple[:, k - 1:k])
            low_x(KT - 1, h[:, KT - 1, :], gain_ple[:, KT - 1:KT])
            for m in range(KT):
                if m % 8 in (4, 5):
                    low_w(U_PROJ + 1 + m // 8, m % 8 - 4)
                dve.wait_ge(out_done, T_PROJ + m + 1)
                dve.tensor_copy(halves(proj[:, m, :]), tile_ps(T_PROJ + m)).then_inc(out_read, 1)
            for k in range(2):
                low_x(k, h[:, k, :], gain_ple[:, k:k + 1])
            invert(4, h_r[:, :])
            count[out_read.name] = T_GATE
            for m in range(KT):
                if U_GATE + m + 1 < UNITS:
                    low_w(U_GATE + m + 1, 0)
                    low_w(U_GATE + m + 1, 1)
                take(T_GATE + m, y_gate[:, :], h_r[:, :])
                dve.wait_ge(silu_done, FFN_GROUP * FFN_CHUNKS + m + 1)
                chained(dve.tensor_tensor(y_gate[:, :], y_gate[:, :], proj[:, m, :], ALU.mult))
                chained(dve.tensor_tensor(h[:, m, :], h[:, m, :], y_gate[:, :], ALU.add), h_final)

        @block.tensor
        def _(pe):
            def block_products(u, blk, t, hi, lo, first, last):
                cols = slice(blk * P, (blk + 1) * P)
                terms = ((w_hi, hi), (w_hi, lo), (w_lo, hi))
                for n, (w, x) in enumerate(terms):
                    for a in range(2):
                        mm = pe.matmul(out_ps[:, 2 * (t % 2) + a, 0:HALF], w[:, u % 2, cols],
                                       x[:, a * HALF:(a + 1) * HALF],
                                       start=first and n == 0, stop=last and n == len(terms) - 1)
                if last:
                    mm.then_inc(out_done, 1)

            def unit(u, tiles, operand, each=None, it=0, between={}):
                per = SLOTS // tiles
                for b in range(SLOTS):
                    if b % 8 == 0 and u >= 2:
                        pe.wait_ge(lo_done, it * (4 * CHUNK_UNITS) + (2 * u + b // 8 + 1 - POOL_LO))
                    elif b % 8 == 0:
                        pe.wait_ge(pool_lo_done if b else lo_done, u + 1)
                    if b in between:
                        between[b]()
                    t = tiles_before(u) + b // per
                    if b % per == 0 and t >= 2:
                        pe.wait_ge(out_read, it * (2 * CHUNK_TILES) + (t - 1))
                    if each:
                        each(b)
                    hi, lo = operand(b)
                    block_products(u, b, t, hi, lo, b % per == 0, b % per == per - 1)

            pair_free = [None]
            mix_free = [None]

            def wait_free(free, reader):
                if free[0]:
                    pe.wait_ge(*free[0])
                free[0] = reader

            def sum_features(x, ready, done, reader):
                pe.wait_ge(ready, done)
                wait_free(pair_free, reader)
                for a in range(2):
                    mm = pe.matmul(pair_ps[:, a, 0:HALF], ones[:, :], x[:, a * HALF:(a + 1) * HALF],
                                   start=True, stop=True)
                return mm

            def sum_head(n):
                sum_features(sq, sq_done, X_SQUARES + n + 1, (ln_done, n + 1)).then_inc(ms_ready, 1)

            def turn(src, u, ready, done):
                pe.wait_ge(ready, done)
                pe.wait_ge(tok_read, reads_before("turn", u))
                for c in range(4):
                    mm = pe.transpose(tok_ps[:, c * P:(c + 1) * P], src[:, c * P:(c + 1) * P], ident[:, :])
                mm.then_inc(turned, 1)

            def mix(i):
                pe.wait_ge(built, 2)
                pe.wait_ge(tok_read, reads_before("turn", U_MLP + 2 + 2 * i) + 1)
                wait_free(mix_free, (mix_read, i + 1))
                for c in range(4):
                    mm = pe.matmul(mix_ps[:, c * P:(c + 1) * P], v_tok[:, c, :], w_mix[:, i, :],
                                   start=True, stop=True)
                mm.then_inc(mixed, 1)

            def scores(i):
                pe.wait_ge(norm_done, 2 * HEADS + i + 1)
                wait_free(pair_free, (z_done, i + 1))
                wait_free(mix_free, (z_done, i + 1))
                for kb in range(4):
                    key = k_head[:, kb * P:(kb + 1) * P]
                    mm = pe.matmul(pair_flat[:, DIAG(kb)], key, q[:, i, kb * P:(kb + 1) * P],
                                   start=True, stop=True)
                for kb in range(3):
                    n = (3 - kb) * P
                    key = k_head[:, kb * P:(kb + 1) * P]
                    dst = mix_ps[:, 0:n] if kb == 1 else pair_flat[:, OFF[kb]:OFF[kb] + n]
                    mm = pe.matmul(dst, key, q[:, i, PROMPT - n:PROMPT], start=True, stop=True)
                mm.then_inc(z_ready, 1)

            def sum_later(i):
                pe.wait_ge(keep_done, i + 1)
                wait_free(pair_free, (pair_read, i + 2))
                wait_free(mix_free, (arg_done, i + 1))
                pe.matmul(pair_flat[:, 0:512], later[:, :], keep[:, 0:512], start=True, stop=True)
                pe.matmul(pair_flat[:, 512:1024], later[:, :], keep[:, 512:1024], start=True, stop=False,
                          skip_group_check=True)
                for col, src in ((512, keep[:, DIAG(1)]), (640, soft[:, P:2 * P]),
                                 (768, soft[:, 2 * P:3 * P]), (896, keep[:, DIAG(3)])):
                    pe.matmul(pair_flat[:, col:col + P], ones[:, :], src, start=False, stop=col == 896,
                              skip_group_check=True)
                pe.matmul(mix_ps[:, 0:256], later[:, :], keep[:, 1024:CELLS], start=True, stop=False,
                          skip_group_check=True)
                pe.matmul(mix_ps[:, 0:P], ones[:, :], keep[:, DIAG(2)], start=False, stop=False,
                          skip_group_check=True)
                pe.matmul(mix_ps[:, P:2 * P], ones[:, :], soft[:, 0:P], start=False, stop=True,
                          skip_group_check=True).then_inc(later_ready, 1)

            def attend(i, u):
                pe.wait_ge(masked, i + 1)
                pe.wait_ge(tok_read, reads_before("av", u))
                for kb in range(4):
                    pe.matmul(tok_ps[:, DIAG(kb)], v_tok[:, kb, :], z[:, DIAG(kb)], start=kb == 0,
                              stop=False, skip_group_check=True)
                for kb in range(3):
                    n = (3 - kb) * P
                    mm = pe.matmul(tok_ps[:, PROMPT - n:PROMPT], v_tok[:, kb, :], z[:, OFF[kb]:OFF[kb] + n],
                                   start=False, stop=kb == 2, skip_group_check=True)
                mm.then_inc(av_ready, 1)

            def reduce_sample(b, u):
                pe.wait_ge(v_used, PAGES * (b + 1))
                pe.wait_ge(tok_read, reads_before("reduce", u))
                for hd in range(HEADS):
                    mm = pe.matmul(tok_ps[:, P + hd:P + hd + 1], acc[:, hd * P:(hd + 1) * P], ones[:, 0:1],
                                   start=True, stop=True)
                mm.then_inc(o_s_ready, 1)

            def sum_later_sample(b, u):
                pe.wait_ge(keep_s_done, b + 1)
                pe.wait_ge(tok_read, reads_before("later", u))
                n = (PAGES - 1) * HEADS
                pe.matmul(tok_ps[:, 0:PAGES * HEADS], later[:, :], keep_s[:, :], start=True, stop=False,
                          skip_group_check=True)
                pe.matmul(tok_ps[:, 0:n], ones[:, :], soft_s[:, 0:n], start=False, stop=True,
                          skip_group_check=True).then_inc(later_s_ready, 1)

            def in_operand(b):
                return x_hi[:, b, :], x_lo[:, b, :]

            unit(0, 1, in_operand, each=lambda b: pe.wait_ge(x_lo_done, b + 1))
            pe.wait_ge(built, 1)

            for u in range(1, U_FFN):
                between = {}
                if u == 1:
                    between[12] = lambda: sum_features(x_r, sum_done, 1, (root_done, 1))\
                        .then_inc(x_sum_ready, 1)
                elif u <= U_MLP:
                    between[8] = lambda n=u - 1 if u > 2 else 0: sum_head(n)
                elif u < U_KV and u % 2 == 1:
                    i = (u - U_MLP - 1) // 2
                    between[6] = lambda i=i: sum_features(vg, gelu_done, 2 * i + 1, (centred, i + 1))\
                        .then_inc(mean_ready, 1)
                elif u <= U_KV:
                    between[10] = lambda i=(u - U_MLP - 2) // 2, u=u: turn(vg, u, norm_done, HEADS + i + 1)
                elif u < U_OUT and u % 2 == 1:
                    i = (u - U_KV - 1) // 2
                    if i:
                        between[2] = lambda i=i: sum_later(i - 1)
                        between[12] = lambda i=i, u=u: attend(i - 1, u)
                    between[6 if i else 5] = lambda i=i: sum_head(2 * HEADS + i)
                elif u <= U_OUT:
                    between[8] = lambda u=u: turn(y[:, 1, :], u, out_read, u)
                    if u == CM_ROOT:
                        between[10] = lambda: sum_features(cm_r, cm_sum_done, 1, (root_done, 2))\
                            .then_inc(x_sum_ready, 1)
                elif u == U_OUT + 2:
                    between[10] = lambda: attend(HEADS - 1, U_OUT + 1)
                elif u == SB_ROOT:
                    between[2] = lambda: sum_features(sb_r, sb_sum_done, 1, (root_done, 3))\
                        .then_inc(x_sum_ready, 1)

                if u - 1 in REDUCE_END:
                    between[3] = lambda u=u: reduce_sample(REDUCE_END.index(u - 1), u - 1)
                if u - 1 in SUM_END:
                    between[4] = lambda u=u: sum_later_sample(SUM_END.index(u - 1), u - 1)

                if u < U_OUT:
                    unit(u, 1, in_operand, between=between)
                else:
                    slot0 = HEADS if u < U_OUT_SB else 0
                    n0 = KT if u < U_OUT_SB else KT + HEADS
                    unit(u, 2, lambda b: in_operand(slot0 + b % 8), between=between,
                         each=(lambda b: pe.wait_ge(x_lo_done, n0 + b % 8 + 1))
                         if u in (U_OUT, U_OUT_SB) else None)
                if u == 2:
                    sum_head(1)
                elif u == U_MLP:
                    pe.wait_ge(norm_done, HEADS)
                    wait_free(pair_free, (pair_read, 1))
                    for hd in range(HEADS):
                        mm = pe.transpose(pair_flat[0:SAMPLES, hd * P:(hd + 1) * P], q[:, hd, PROMPT:TOK],
                                          ident[:, :])
                    mm.then_inc(q_rows_ready, 1)
                elif U_MLP < u < U_KV and u % 2 == 1:
                    sum_head(HEADS + (u - U_MLP - 1) // 2)
                elif U_MLP < u <= U_KV:
                    mix((u - U_MLP - 2) // 2)
                elif U_KV < u < U_OUT and u % 2 == 1:
                    scores((u - U_KV - 1) // 2)
                elif u == U_OUT + 1:
                    sum_later(HEADS - 1)

            def ffn_operand(b):
                return in_operand((b + 8) % KT)

            for u in range(U_FFN, U_LOOP):
                unit(u, 1, ffn_operand,
                     each=(lambda b: pe.wait_ge(x_lo_done, 2 * KT + b + 1)) if u == U_FFN else None)
                if u == U_FFN:
                    sum_features(h_sum, h_sum_done, KT, (root_done, 4)).then_inc(x_sum_ready, 1)

            def down_unit(u, par, it=0):
                unit(u, 4, lambda b: (act_hi[:, par, b % 4, :], act_lo[:, par, b % 4, :]), it=it)

            with pe.Fori(0, (FFN_CHUNKS - 1) // 2) as it:
                for half in range(2):
                    u0 = U_LOOP + half * CHUNK_UNITS
                    for x in range(2 * FFN_GROUP):
                        unit(u0 + x, 1, ffn_operand, it=it)
                    pe.wait_ge(act_lo_done, it * (2 * FFN_GROUP) + FFN_GROUP * (1 + half))
                    for g in range(FFN_GROUP):
                        down_unit(u0 + 2 * FFN_GROUP + g, half, it)
            pe.wait_ge(act_lo_done, FFN_GROUP * FFN_CHUNKS)
            for g in range(FFN_GROUP):
                down_unit(U_LAST_DOWN + g, (FFN_CHUNKS - 1) % 2)

            pe.wait_ge(x_lo_done, 3 * KT + 2)
            for s in range(2):
                unit(U_PROJ + s, 8, lambda b: in_operand(b % 2))
            sum_features(h_sum, h_sum_done, 2 * KT, (root_done, 5)).then_inc(x_sum_ready, 1)
            for m in range(KT):
                unit(U_GATE + m, 1, lambda b: in_operand((b + 2) % KT),
                     each=(lambda b: pe.wait_ge(x_lo_done, 3 * KT + 2 + b + 1)) if m == 0 else None)


def kernel(x_prompt, x_sample, cache_k, cache_v, page_table, p_prompt, p_sample, g_mix, w_in, g_q, g_k,
           sb_bias, sgu_ln_g, sgu_ln_b, w_s, b_s, g_out_sb, g_out_cm, w_out, g_ffn, w_gate, w_up, w_down,
           g_ple, w_ple_gate, w_ple_proj):
    import numpy as np
    import concourse.bacc as bacc
    from concourse.bass_utils import run_bass_kernel_spmd as run

    a = lambda x: np.asarray(x)

    def feature_major(prompt, sample):
        x = np.concatenate([a(prompt).reshape(PROMPT, -1), a(sample).reshape(SAMPLES, -1)])
        return x.T.reshape(-1, P, TOK).transpose(1, 0, 2)

    def by_partition(g):
        return a(g).reshape(-1, P).T

    def by_tile(w):
        return w.reshape(w.shape[0] // P, P, w.shape[1] // P, P).transpose(2, 1, 0, 3)

    tile_order = list(range(HEADS))
    tile_order += [x for i in range(HEADS) for x in (4 * HEADS + i, 3 * HEADS + i)]
    tile_order += [x for i in range(HEADS) for x in (HEADS + i, 2 * HEADS + i)]
    w_in_u = by_tile(a(w_in)[0])[tile_order].reshape(-1, P, SLOTS * P)
    w_out_u = a(w_out)[0].reshape(2, 8, P, 8, 2, P).transpose(0, 3, 2, 4, 1, 5)[::-1]
    w_out_u = w_out_u.reshape(-1, P, SLOTS * P)
    gate_up = np.stack([by_tile(a(w_gate)[0]), by_tile(a(w_up)[0])], axis=1)
    gate_up = gate_up.reshape(FFN_CHUNKS, 2 * FFN_GROUP, P, SLOTS * P)
    down = a(w_down)[0].reshape(FFN_CHUNKS, FFN_GROUP, P, 4, 4, P).transpose(0, 3, 2, 4, 1, 5)
    down = down.reshape(FFN_CHUNKS, FFN_GROUP, P, SLOTS * P)
    ffn = [gate_up[0]]
    for c in range(1, FFN_CHUNKS):
        ffn += [gate_up[c], down[c - 1]]
    ffn.append(down[-1])
    proj_u = a(w_ple_proj)[0].reshape(2, P, 2, 8, P).transpose(2, 1, 3, 0, 4).reshape(2, P, SLOTS * P)
    gate_t = by_tile(a(w_ple_gate)[0])
    gate_u = np.concatenate([gate_t[:, :, 2:], gate_t[:, :, :2]], axis=2).reshape(-1, P, SLOTS * P)
    arrays = {
        "w_units": np.concatenate([w_in_u, w_out_u, *ffn, proj_u, gate_u]),
        "x_t": feature_major(x_prompt, x_sample),
        "p_t": feature_major(p_prompt, p_sample),
        "cache_k": a(cache_k).reshape(N_PHYS, P, HEADS * P),
        "cache_v": a(cache_v).reshape(N_PHYS, P, HEADS * P),
        "page_table": a(page_table).reshape(1, N_PAGES),
        "g_mix": by_partition(g_mix),
        "g_out": np.concatenate([by_partition(g_out_sb), by_partition(g_out_cm)], axis=1),
        "g_ffn": by_partition(g_ffn),
        "g_ple": by_partition(g_ple),
        "g_q": a(g_q).reshape(P, 1),
        "g_k": a(g_k).reshape(P, 1),
        "ln_g": by_partition(sgu_ln_g),
        "ln_b": by_partition(sgu_ln_b),
        "w_s_t": a(w_s)[0].transpose(2, 0, 1),
        "b_s": a(b_s).reshape(1, HEADS, P),
        "sb_bias": a(sb_bias).reshape(1, HEADS),
        "w_s00": a(w_s)[0, :, 0, 0].reshape(1, HEADS),
    }
    arrays = {k: np.ascontiguousarray(v) for k, v in arrays.items()}
    outs = {"y_t": (P, KT, TOK), "k_t": (HEADS, P, TOK), "v_t": (HEADS, P, TOK),
            "chunk_v_t": (P, HEADS, SAMPLES)}
    nc = bacc.Bacc("TRN2", target_bir_lowering=False, num_devices=1)
    aps = {k: nc.dram_tensor(k, v.shape, mybir.dt.from_np(v.dtype), kind="ExternalInput").ap()
           for k, v in arrays.items()}
    aps |= {k: nc.dram_tensor(k, s, F32, kind="ExternalOutput").ap() for k, s in outs.items()}
    build(nc, **aps)
    got = run(nc, [arrays], core_ids=[0]).results[0]

    y = got["y_t"].transpose(2, 1, 0).reshape(TOK, D_MODEL)
    k = got["k_t"].transpose(2, 0, 1)
    v = got["v_t"].transpose(2, 0, 1)
    chunk = got["chunk_v_t"].transpose(2, 1, 0)
    new = (SAMPLES, 1, HEADS, P)
    return tuple(np.ascontiguousarray(x) for x in (
        y[:PROMPT].reshape(1, PROMPT, D_MODEL), y[PROMPT:].reshape(SAMPLES, 1, D_MODEL),
        k[:PROMPT].reshape(1, 1, PROMPT, HEADS, P), v[:PROMPT].reshape(1, 1, PROMPT, HEADS, P),
        k[PROMPT:].reshape(1, *new), v[PROMPT:].reshape(1, *new), chunk.reshape(1, *new)))
```
